# Optimizing a Trainium2 kernel written in Bass

```python
import jax, jax.numpy as jnp
from jax import lax
import numpy as np

D_MODEL = 1024
BATCH = 1
SEQ = 1024
DEPTH = 1

PLE_DIM = 256
NORM_EPS = 1e-6
MIX_WIDTH = D_MODEL
GLA_WIDTH = MIX_WIDTH // 2
GLA_HEADS = 4
GLA_DV = GLA_WIDTH // GLA_HEADS
GLA_DK = GLA_DV // 2
GLA_GATE_RANK = 16
GLA_TAU = 16.0
GLA_CHUNK = 64
DSW_WIDTH = MIX_WIDTH - GLA_WIDTH
DSW_HEAD_DIM = 64
DSW_HEADS = DSW_WIDTH // DSW_HEAD_DIM
DSW_PATTERNS = ((128, 1), (512, 4), (2048, 16))
DSW_BLOCK = 128
ROT_DIM = DSW_HEAD_DIM // 4
ROPE_THETA = 500000.0
PEER_N_KEYS = 128
PEER_N_EXPERTS = PEER_N_KEYS * PEER_N_KEYS
PEER_HEADS = 8
PEER_TOPK = 16
PEER_QDIM = 256
PEER_HALF = PEER_QDIM // 2
PEER_TOKEN_BLOCK = 128

IN_SPLITS = (GLA_HEADS * GLA_DK, GLA_HEADS * GLA_DK, GLA_WIDTH, GLA_WIDTH, GLA_GATE_RANK,
             DSW_WIDTH, DSW_WIDTH, DSW_WIDTH)
IN_COLS = sum(IN_SPLITS)
IN_SPLIT_IDX = [int(c) for c in np.cumsum(IN_SPLITS)[:-1]]

kernel_name = "hymba_gla_dilated_peer_ple"

def rms_norm(x, g):
    xf = x.astype(jnp.float32)
    y = xf * lax.rsqrt(jnp.mean(xf * xf, axis=-1, keepdims=True) + NORM_EPS)
    return (y * g.astype(jnp.float32)).astype(x.dtype)

def partial_rope(t, positions):
    inv_freq = ROPE_THETA ** (-jnp.arange(0, ROT_DIM, 2, dtype=jnp.float32) / ROT_DIM)
    ang = positions.astype(jnp.float32)[..., None] * inv_freq
    ang = jnp.concatenate([ang, ang], axis=-1)[:, :, None, :]
    rot = t[..., :ROT_DIM].astype(jnp.float32)
    half = ROT_DIM // 2
    rot_half = jnp.concatenate([-rot[..., half:], rot[..., :half]], axis=-1)
    rot = rot * jnp.cos(ang) + rot_half * jnp.sin(ang)
    return jnp.concatenate([rot.astype(t.dtype), t[..., ROT_DIM:]], axis=-1)

def gla_chunked(q, k, v, log_a):
    bsz, slen, nh, dk = q.shape
    dv = v.shape[-1]
    n = slen // GLA_CHUNK

    def chunks(t):
        return t.astype(jnp.float32).reshape(bsz, n, GLA_CHUNK, nh, t.shape[-1]).transpose(0, 3, 1, 2, 4)

    qc = chunks(q) * (dk ** -0.5)
    kc = chunks(k)
    vc = chunks(v)
    b = jnp.cumsum(chunks(log_a), axis=3)
    b_last = b[:, :, :, -1:, :]
    q_dec = qc * jnp.exp(b)
    k_dec = kc * jnp.exp(-b)
    k_end = kc * jnp.exp(b_last - b)
    causal = jnp.tril(jnp.ones((GLA_CHUNK, GLA_CHUNK), dtype=bool))
    attn = jnp.where(causal, jnp.einsum('bhncd,bhnsd->bhncs', q_dec, k_dec), 0.0)
    o_intra = jnp.einsum('bhncs,bhnsv->bhncv', attn, vc)
    chunk_kv = jnp.einsum('bhncd,bhncv->bhndv', k_end, vc)
    decay = jnp.exp(b_last[:, :, :, 0, :])

    def step(state, inp):
        dec, kv = inp
        return dec[..., None] * state + kv, state

    init = jnp.zeros((bsz, nh, dk, dv), jnp.float32)
    _, s_prev = lax.scan(step, init, (jnp.moveaxis(decay, 2, 0), jnp.moveaxis(chunk_kv, 2, 0)))
    s_prev = jnp.moveaxis(s_prev, 0, 2)
    o = o_intra + jnp.einsum('bhncd,bhndv->bhncv', q_dec, s_prev)
    return o.transpose(0, 2, 3, 1, 4).reshape(bsz, slen, nh, dv)

def dilated_window_attention(q, k, v, window, dilation):
    bsz, slen, nh, hd = q.shape
    n_back = window // dilation
    span = dilation * DSW_BLOCK
    sp = -(-slen // span) * span
    pad = sp - slen
    m = sp // dilation
    nb = m // DSW_BLOCK

    def to_blocks(t):
        t = jnp.pad(t, ((0, 0), (0, pad), (0, 0), (0, 0)))
        t = t.reshape(bsz, m, dilation, nh, hd).transpose(0, 2, 1, 3, 4)
        return t.reshape(bsz, dilation, nb, DSW_BLOCK, nh, hd)

    qb, kb, vb = to_blocks(q), to_blocks(k), to_blocks(v)
    zpad = ((0, 0), (0, 0), (1, 0), (0, 0), (0, 0), (0, 0))
    kk = jnp.concatenate([jnp.pad(kb[:, :, :-1], zpad), kb], axis=3)
    vv = jnp.concatenate([jnp.pad(vb[:, :, :-1], zpad), vb], axis=3)
    scores = jnp.einsum('brnqhd,brnkhd->brnhqk', qb, kk).astype(jnp.float32) * (hd ** -0.5)
    qi = jnp.arange(DSW_BLOCK)[:, None]
    ki = jnp.arange(2 * DSW_BLOCK)[None, :]
    dist = qi + DSW_BLOCK - ki
    band = (dist >= 0) & (dist <= n_back)
    no_prev = (jnp.arange(nb) == 0)[:, None, None] & (ki < DSW_BLOCK)[None]
    mask = (band[None] & ~no_prev)[:, None]
    scores = jnp.where(mask, scores, -jnp.inf)
    lse = jax.nn.logsumexp(scores, axis=-1)
    probs = jnp.exp(scores - lse[..., None])
    o = jnp.einsum('brnhqk,brnkhd->brnqhd', probs.astype(v.dtype), vv)
    o = o.reshape(bsz, dilation, m, nh, hd).transpose(0, 2, 1, 3, 4).reshape(bsz, sp, nh, hd)[:, :slen]
    lse = lse.transpose(0, 1, 2, 4, 3).reshape(bsz, dilation, m, nh).transpose(0, 2, 1, 3)
    lse = lse.reshape(bsz, sp, nh)[:, :slen]
    return o, lse

def dilated_mixture(q, k, v):
    outs, lses = [], []
    for window, dilation in DSW_PATTERNS:
        o, lse = dilated_window_attention(q, k, v, window, dilation)
        outs.append(o.astype(jnp.float32))
        lses.append(lse)
    w = jax.nn.softmax(jnp.stack(lses, axis=0), axis=0)
    o = jnp.sum(w[..., None] * jnp.stack(outs, axis=0), axis=0)
    return o.astype(q.dtype)

def peer(h, w_q, sub_keys, u_table, v_table):
    bsz, slen, dm = h.shape
    t = bsz * slen
    hf = h.reshape(t, dm)
    qr = (hf @ w_q).reshape(t, PEER_HEADS, 2, PEER_HALF)
    sc = jnp.einsum('thcd,hcnd->thcn', qr, sub_keys).astype(jnp.float32)
    s_top, i_top = lax.top_k(sc, PEER_TOPK)
    cand = (s_top[:, :, 0, :, None] + s_top[:, :, 1, None, :]).reshape(t, PEER_HEADS, PEER_TOPK * PEER_TOPK)
    cand_idx = (i_top[:, :, 0, :, None] * PEER_N_KEYS + i_top[:, :, 1, None, :]).reshape(t, PEER_HEADS, PEER_TOPK * PEER_TOPK)
    best, pos = lax.top_k(cand, PEER_TOPK)
    expert_idx = jnp.take_along_axis(cand_idx, pos, axis=-1)
    gates = jax.nn.softmax(best, axis=-1)
    nblk = t // PEER_TOKEN_BLOCK

    def block(args):
        xb, ib, gb = args
        ub = jnp.take(u_table, ib, axis=0)
        a = jnp.einsum('td,thkd->thk', xb, ub).astype(jnp.float32)
        act = (jax.nn.gelu(a, approximate=False) * gb).astype(xb.dtype)
        vb = jnp.take(v_table, ib, axis=0)
        return jnp.einsum('thk,thkd->td', act, vb)

    out = lax.map(block, (hf.reshape(nblk, PEER_TOKEN_BLOCK, dm),
                          expert_idx.reshape(nblk, PEER_TOKEN_BLOCK, PEER_HEADS, PEER_TOPK),
                          gates.reshape(nblk, PEER_TOKEN_BLOCK, PEER_HEADS, PEER_TOPK)))
    return out.reshape(bsz, slen, dm)

def setup_inputs(seed: int = 0) -> dict:
    key = jax.random.key(seed)
    ks = jax.random.split(key, 20)
    f32 = jnp.float32
    nrm = lambda k, shape, s: jax.random.normal(k, shape, f32) * s
    gain = lambda k, shape: 1.0 + 0.02 * jax.random.normal(k, shape, f32)
    x = nrm(ks[0], (BATCH, SEQ, D_MODEL), 1.0)
    p = nrm(ks[1], (DEPTH, BATCH, SEQ, PLE_DIM), 1.0)
    positions = (jnp.arange(SEQ, dtype=jnp.int32)[None, :]
                 + jax.random.randint(ks[2], (BATCH, 1), 0, 1024, dtype=jnp.int32))
    return {
        "x": x,
        "p": p,
        "positions": positions,
        "g_mix": gain(ks[3], (DEPTH, D_MODEL)),
        "w_in": nrm(ks[4], (DEPTH, D_MODEL, IN_COLS), D_MODEL ** -0.5),
        "w_gla_gate_up": nrm(ks[5], (DEPTH, GLA_GATE_RANK, GLA_HEADS * GLA_DK), GLA_GATE_RANK ** -0.5),
        "b_gla_gate": nrm(ks[6], (DEPTH, GLA_HEADS * GLA_DK), 0.1),
        "g_gla_out": gain(ks[7], (DEPTH, GLA_HEADS, GLA_DV)),
        "w_out": nrm(ks[8], (DEPTH, MIX_WIDTH, D_MODEL), MIX_WIDTH ** -0.5),
        "g_peer": gain(ks[9], (DEPTH, D_MODEL)),
        "w_peer_q": nrm(ks[10], (DEPTH, D_MODEL, PEER_HEADS * PEER_QDIM), D_MODEL ** -0.5),
        "peer_sub_keys": nrm(ks[11], (DEPTH, PEER_HEADS, 2, PEER_N_KEYS, PEER_HALF), PEER_HALF ** -0.5),
        "peer_u": nrm(ks[12], (DEPTH, PEER_N_EXPERTS, D_MODEL), D_MODEL ** -0.5),
        "peer_v": nrm(ks[13], (DEPTH, PEER_N_EXPERTS, D_MODEL), 0.5),
        "g_ple": gain(ks[14], (DEPTH, D_MODEL)),
        "w_ple_gate": nrm(ks[15], (DEPTH, D_MODEL, D_MODEL), D_MODEL ** -0.5),
        "w_ple_proj": nrm(ks[16], (DEPTH, PLE_DIM, D_MODEL), PLE_DIM ** -0.5),
        "g_final": gain(ks[17], (D_MODEL,)),
    }

def reference(x, p, positions, g_mix, w_in, w_gla_gate_up, b_gla_gate, g_gla_out, w_out,
              g_peer, w_peer_q, peer_sub_keys, peer_u, peer_v, g_ple, w_ple_gate, w_ple_proj, g_final):
    bsz, slen, _ = x.shape
    for i in range(DEPTH):
        h = rms_norm(x, g_mix[i])
        proj = h @ w_in[i]
        qa, ka, va, ra, ga_low, qb, kb, vb = jnp.split(proj, IN_SPLIT_IDX, axis=-1)
        log_a = jax.nn.log_sigmoid((ga_low @ w_gla_gate_up[i] + b_gla_gate[i]).astype(jnp.float32)) / GLA_TAU
        oa = gla_chunked(qa.reshape(bsz, slen, GLA_HEADS, GLA_DK),
                         ka.reshape(bsz, slen, GLA_HEADS, GLA_DK),
                         va.reshape(bsz, slen, GLA_HEADS, GLA_DV),
                         log_a.reshape(bsz, slen, GLA_HEADS, GLA_DK)).astype(x.dtype)
        oa = rms_norm(oa, g_gla_out[i]).reshape(bsz, slen, GLA_WIDTH) * jax.nn.silu(ra)
        qb = partial_rope(qb.reshape(bsz, slen, DSW_HEADS, DSW_HEAD_DIM), positions)
        kb = partial_rope(kb.reshape(bsz, slen, DSW_HEADS, DSW_HEAD_DIM), positions)
        vb = vb.reshape(bsz, slen, DSW_HEADS, DSW_HEAD_DIM)
        ob = dilated_mixture(qb, kb, vb).reshape(bsz, slen, DSW_WIDTH)
        x = x + jnp.concatenate([oa, ob], axis=-1) @ w_out[i]
        x = x + peer(rms_norm(x, g_peer[i]), w_peer_q[i], peer_sub_keys[i], peer_u[i], peer_v[i])
        gate = jax.nn.sigmoid(rms_norm(x, g_ple[i]) @ w_ple_gate[i])
        x = x + (p[i] @ w_ple_proj[i]) * gate
    return rms_norm(x, g_final)


_drawn_inputs = setup_inputs


def setup_inputs(seed=0):
    import zlib

    import numpy as np

    out = dict(_drawn_inputs(seed))
    spreads = {}
    factors = {'g_gla_out': 2.72, 'g_ple': 144.334, 'g_final': 23.742}
    for name, (base, spread) in spreads.items():
        noise = np.random.default_rng([zlib.crc32(name.encode()), seed]).standard_normal(out[name].shape)
        drawn = base * np.exp(spread * noise) if base else spread * noise
        out[name] = __import__('jax').numpy.asarray(drawn.astype(out[name].dtype))
    for name, factor in factors.items():
        out[name] = (out[name] * factor).astype(out[name].dtype)
    return out
```

```python
from contextlib import ExitStack

import concourse.bass as bass
from concourse import mybir

F32 = mybir.dt.float32
F32R = mybir.dt.float32r
I32 = mybir.dt.int32
U32 = mybir.dt.uint32
ALU = mybir.AluOpType
ACT = mybir.ActivationFunctionType
AX_X = mybir.AxisListType.X

P = 128
SEQ = 1024
D = 1024
KD = D // P
NB = SEQ // P
HALF = 512
EPS = 1e-6
GH, GDK, GDV, CH = 4, 64, 128, 64
GW = GH * GDV
GK = GH * GDK
GP = GK // P
NCH = SEQ // CH
AH, AD = 8, 64
RANK = 16
KEYS = 128
PH, TOPK = 8, 16
SLOTS = PH * TOPK
SIDES = 2 * PH
PLE = 256
KP = PLE // P
NT_IN = 12
N_IN = 3 * HALF
CW = 256
TB = 64
NTB = SEQ // TB
LOWEST = -3e38
PASSES = ((0, 0), (0, 1), (1, 0))


class Steps:

    def __init__(self, eng, sem):
        self.eng, self.sem, self.n, self.base = eng, sem, 0, 0

    def __call__(self, ins):
        ins.then_inc(self.sem, 1)
        self.n += 1
        self.eng.wait_ge(self.sem, self.base + self.n)


def rounds(eng, count):
    def run(body):
        body(0)
        if count == 2:
            body(1)
        elif count > 2:
            with eng.Fori(1, count) as it:
                body(it)
    return run


def wait_past(eng, sem, value):
    if not (isinstance(value, int) and value <= 0):
        eng.wait_ge(sem, value)


def hold(nc, mark):
    nc.vector.memset(mark, 0.0)


class Core:

    def __init__(self, nc, top):
        self.nc, self.held = nc, []
        sb = self.sb(top)
        self.xres = sb("xres", [P, NB, D])
        self.ident = sb("ident", [P, P])
        self.projT = nc.dram_tensor("projT", [NT_IN + 1, P, SEQ], F32).ap()
        self.projN = nc.dram_tensor("projN", [SEQ, N_IN], F32).ap()
        self.gates = nc.dram_tensor("gates_dense", [NTB, P, KEYS, TB], F32).ap()

    def sem(self, name):
        self.held.append(self.nc.alloc_semaphore(name))
        return self.held[-1]

    def kept_sems(self, name, n):
        return [self.nc.alloc_semaphore(f"{name}{i}") for i in range(n)]

    def recycle(self):
        with self.nc.Block() as block:
            @block.gpsimd
            def _(pool):
                for h in self.held:
                    pool.sem_clear(h)
        for h in self.held:
            self.nc.release_semaphore(h)
        self.held = []

    def sems(self, name, n):
        return [self.sem(f"{name}{i}") for i in range(n)]

    def sb(self, scope):
        return lambda name, shape, dt=F32: scope.enter_context(self.nc.sbuf_tensor(name, shape, dt))

    def ps(self, scope):
        return lambda name, shape: scope.enter_context(self.nc.psum_tensor(name, shape, F32))

    def hT_pair(self, scope, tag):
        s = self.sb(scope)
        return [s(f"{tag}_hi", [P, KD, SEQ], F32R), s(f"{tag}_lo", [P, KD, SEQ], F32R)]


class Weights:

    def __init__(self, core, scope, tag, width, used, per=1):
        s = core.sb(scope)
        self.nc = core.nc
        self.raw = [s(f"{tag}_raw{u}", [P, KD, width]) for u in range(2)]
        self.part = [[s(f"{tag}_w{n}{u}", [P, KD, width], F32R) for n in ("hi", "lo")] for u in range(2)]
        self.landed = core.sems(f"{tag}_w_landed", 2)
        self.hi_done = core.sems(f"{tag}_w_hi", 2)
        self.lo_done = core.sems(f"{tag}_w_lo", 2)
        self.used, self.per = used, per

    def load(self, sp, u, n, src):
        wait_past(sp, self.lo_done[u], n)
        sp.dma_start(self.raw[u][:], src).then_inc(self.landed[u], 16)

    def hi(self, act, u, n):
        act.wait_ge(self.landed[u], 16 * n + 16)
        wait_past(act, self.used[u], self.per * n)
        self.nc.scalar.activation(self.part[u][0][:], self.raw[u][:], ACT.Copy).then_inc(self.hi_done[u], 1)

    def lo(self, dve, u, n):
        dve.wait_ge(self.hi_done[u], n + 1)
        self.nc.vector.tensor_tensor(self.part[u][1][:], self.raw[u][:], self.part[u][0][:].bitcast(F32),
                                     ALU.subtract).then_inc(self.lo_done[u], 1)


def product_T(nc, W, u, hT, banks):
    for half in range(2):
        for k in range(KD):
            for a, c in PASSES:
                last = nc.tensor.matmul(banks[:, half, :], W.part[u][a][:, k, :],
                                        hT[c][:, k, half * HALF:(half + 1) * HALF],
                                        start=(k == 0 and (a, c) == PASSES[0]),
                                        stop=(k == KD - 1 and (a, c) == PASSES[-1]))
    return last


def product_N(nc, part, hT, b, out, tiles=KD):
    for k in range(tiles):
        for a, c in PASSES:
            last = nc.tensor.matmul(out, hT[a][:, k, b * P:(b + 1) * P], part[c][:, k, :],
                                    start=(k == 0 and (a, c) == PASSES[0]),
                                    stop=(k == tiles - 1 and (a, c) == PASSES[-1]))
    return last


def rstd(nc, steps, ss, v, y, t, width, var_ready, root_ready):
    steps(nc.vector.tensor_scalar(v, ss, 1.0 / width, EPS, ALU.mult, ALU.add))
    nc.vector.reciprocal(t, v).then_inc(var_ready, 1)
    steps.eng.wait_ge(root_ready, 1)
    steps(nc.vector.tensor_tensor(t, y, y, ALU.mult))
    steps(nc.vector.tensor_tensor(t, t, v, ALU.mult))
    steps(nc.vector.tensor_scalar(t, t, -0.5, 1.5, ALU.mult, ALU.add))
    steps(nc.vector.tensor_tensor(y, y, t, ALU.mult))


def norm_stage(core, tag, g_row, hT=None, x=None, ident=None, out=None):
    nc = core.nc
    with ExitStack() as sc:
        s, p = core.sb(sc), core.ps(sc)
        g_b = s(f"{tag}_g", [P, D])
        squares = s(f"{tag}_sq", [P, 2, D])
        xn = s(f"{tag}_xn", [P, 2, D])
        ss, v, y, t = (s(f"{tag}_{n}", [P, NB]) for n in ("ss", "v", "y", "t"))
        tp = [p(f"{tag}_tp{u}", [P, KD, P]) for u in range(2)]
        g_in, ident_in, x_in = core.sem(f"{tag}_g_in"), core.sem(f"{tag}_id_in"), core.sems(f"{tag}_x_in", NB) if x is not None else None
        squared, var_ready, root_ready = (core.sem(f"{tag}_{n}") for n in ("squared", "var", "root"))
        chain, xn_ready, turned = (core.sem(f"{tag}_{n}") for n in ("chain", "xn_ready", "turned"))
        hi_done, lo_done = core.sem(f"{tag}_hi_done"), core.sem(f"{tag}_lo_done")
        stored = core.sems(f"{tag}_stored", 2)
        with nc.Block() as block:
            @block.sync
            def _(sp):
                if x is not None:
                    for b in range(NB):
                        sp.dma_start(core.xres[:, b, :], x[b * P:(b + 1) * P, :]).then_inc(x_in[b], 16)
                    sp.dma_start(core.ident[:], ident).then_inc(ident_in, 16)
                sp.dma_start(g_b[:], g_row.partition_broadcast(P)).then_inc(g_in, 16)
                if out is not None:
                    for b in range(NB):
                        sp.wait_ge(xn_ready, b + 1)
                        sp.dma_start(out[b * P:(b + 1) * P, :], xn[:, b % 2, :]).then_inc(stored[b % 2], 16)
                    for u in range(2):
                        sp.wait_ge(stored[u], 16 * (NB // 2))

            @block.scalar
            def _(act):
                for b in range(NB):
                    if x is not None:
                        act.wait_ge(x_in[b], 16)
                    if b >= 2:
                        act.wait_ge(squared, b - 1)
                    nc.scalar.activation(squares[:, b % 2, :], core.xres[:, b, :], ACT.Square,
                                         accum_out=ss[:, b:b + 1]).then_inc(squared, 1)
                act.wait_ge(var_ready, 1)
                nc.scalar.activation(y[:], t[:], ACT.Sqrt).then_inc(root_ready, 1)
                if hT is not None:
                    for b in range(NB):
                        act.wait_ge(turned, b + 1)
                        nc.scalar.activation(hT[0][:, :, b * P:(b + 1) * P], tp[b % 2][:], ACT.Copy)\
                            .then_inc(hi_done, 1)

            @block.vector
            def _(dve):
                steps = Steps(dve, chain)
                dve.wait_ge(squared, NB)
                rstd(nc, steps, ss[:], v[:], y[:], t[:], D, var_ready, root_ready)
                dve.wait_ge(g_in, 16)

                def scale(b):
                    if hT is not None and b >= 2:
                        dve.wait_ge(turned, b - 1)
                    if out is not None and b >= 2:
                        dve.wait_ge(stored[b % 2], 16 * (b // 2))
                    nc.vector.scalar_tensor_tensor(out=xn[:, b % 2, :], in0=core.xres[:, b, :],
                                                   scalar=y[:, b:b + 1], in1=g_b[:],
                                                   op0=ALU.mult, op1=ALU.mult).then_inc(xn_ready, 1)

                for b in range(NB + 1):
                    if b < NB:
                        scale(b)
                    if b and hT is not None:
                        dve.wait_ge(hi_done, b)
                        cols = slice((b - 1) * P, b * P)
                        nc.vector.tensor_tensor(hT[1][:, :, cols], tp[(b - 1) % 2][:],
                                                hT[0][:, :, cols].bitcast(F32), ALU.subtract)\
                            .then_inc(lo_done, 1)

            if hT is not None:
                @block.tensor
                def _(pe):
                    if x is not None:
                        pe.wait_ge(ident_in, 16)
                    for b in range(NB):
                        pe.wait_ge(xn_ready, b + 1)
                        if b >= 2:
                            pe.wait_ge(lo_done, b - 1)
                        for k in range(KD):
                            last = nc.tensor.transpose(tp[b % 2][:, k, :], xn[:, b % 2, k * P:(k + 1) * P],
                                                       core.ident[:])
                        last.then_inc(turned, 1)


def in_projection_T(core, hT, w_t):
    nc = core.nc
    with ExitStack() as sc:
        s, p = core.sb(sc), core.ps(sc)
        tile_done = core.sems("iT_tile_done", 2)
        W = Weights(core, sc, "iT", P, tile_done)
        stage = [s(f"iT_stage{u}", [P, SEQ]) for u in range(2)]
        ps = [p(f"iT_ps{u}", [P, 2, HALF]) for u in range(2)]
        copied, stored = core.sems("iT_copied", 2), core.kept_sems("iT_stored", 2)
        pairs = NT_IN // 2
        with nc.Block() as block:
            @block.sync
            def _(sp):
                @rounds(sp, pairs)
                def _(it):
                    for u in range(2):
                        W.load(sp, u, it, w_t[it * 2 + u])
                W.load(sp, 0, pairs, w_t[NT_IN])

            @block.scalar
            def _(act):
                def evacuate(u, n):
                    act.wait_ge(tile_done[u], n + 1)
                    wait_past(act, stored[u], 16 * n)
                    nc.scalar.activation(stage[u][:], ps[u][:], ACT.Copy).then_inc(copied[u], 1)

                for u in range(2):
                    W.hi(act, u, 0)
                @rounds(act, pairs - 1)
                def _(it):
                    for u in range(2):
                        evacuate(u, it)
                        W.hi(act, u, it + 1)
                evacuate(0, pairs - 1)
                W.hi(act, 0, pairs)
                evacuate(1, pairs - 1)
                evacuate(0, pairs)

            @block.vector
            def _(dve):
                @rounds(dve, pairs)
                def _(it):
                    for u in range(2):
                        W.lo(dve, u, it)
                W.lo(dve, 0, pairs)

            @block.gpsimd
            def _(pool):
                def store(u, n, row):
                    pool.wait_ge(copied[u], n + 1)
                    pool.dma_start(core.projT[row], stage[u][:]).then_inc(stored[u], 16)

                @rounds(pool, pairs)
                def _(it):
                    for u in range(2):
                        store(u, it, it * 2 + u)
                store(0, pairs, NT_IN)
                pool.wait_ge(stored[0], 16 * (pairs + 1))
                pool.wait_ge(stored[1], 16 * pairs)

            @block.tensor
            def _(pe):
                def tile(u, n):
                    pe.wait_ge(W.lo_done[u], n + 1)
                    wait_past(pe, copied[u], n)
                    product_T(nc, W, u, hT, ps[u]).then_inc(tile_done[u], 1)

                @rounds(pe, pairs)
                def _(it):
                    for u in range(2):
                        tile(u, it)
                tile(0, pairs)


def in_projection_N(core, hT, w_n):
    nc = core.nc
    with ExitStack() as sc:
        s, p = core.sb(sc), core.ps(sc)
        block_done = core.sems("iN_block_done", 2)
        W = Weights(core, sc, "iN", CW, block_done, NB)
        stage = [s(f"iN_stage{u}", [P, NB, CW]) for u in range(2)]
        ps = [[p(f"iN_ps{u}{r}", [P, HALF]) for r in range(4)] for u in range(2)]
        copied, stored = core.sems("iN_copied", 2), core.kept_sems("iN_stored", 2)
        pairs = N_IN // CW // 2
        w_v = w_n.rearrange("(k p) c -> p k c", p=P)
        o_v = core.projN.rearrange("(b p) c -> p b c", p=P)
        with nc.Block() as block:
            @block.sync
            def _(sp):
                @rounds(sp, pairs)
                def _(it):
                    for u in range(2):
                        W.load(sp, u, it, w_v[:, :, bass.ds((it * 2 + u) * CW, CW)])

            @block.scalar
            def _(act):
                def evacuate(u, n):
                    wait_past(act, stored[u], 16 * n)
                    for b in range(NB):
                        act.wait_ge(block_done[u], NB * n + b + 1)
                        nc.scalar.activation(stage[u][:, b, :], ps[u][b % 4][:, 0:CW], ACT.Copy)\
                            .then_inc(copied[u], 1)

                for u in range(2):
                    W.hi(act, u, 0)
                @rounds(act, pairs - 1)
                def _(it):
                    for u in range(2):
                        evacuate(u, it)
                        W.hi(act, u, it + 1)
                for u in range(2):
                    evacuate(u, pairs - 1)

            @block.vector
            def _(dve):
                @rounds(dve, pairs)
                def _(it):
                    for u in range(2):
                        W.lo(dve, u, it)

            @block.gpsimd
            def _(pool):
                @rounds(pool, pairs)
                def _(it):
                    for u in range(2):
                        pool.wait_ge(copied[u], NB * it + NB)
                        pool.dma_start(o_v[:, :, bass.ds((it * 2 + u) * CW, CW)], stage[u][:])\
                            .then_inc(stored[u], 16)
                for u in range(2):
                    pool.wait_ge(stored[u], 16 * pairs)

            @block.tensor
            def _(pe):
                @rounds(pe, pairs)
                def _(it):
                    for u in range(2):
                        pe.wait_ge(W.lo_done[u], it + 1)
                        for b in range(NB):
                            wait_past(pe, copied[u], NB * it + max(b - 3, 0))
                            product_N(nc, W.part[u], hT, b, ps[u][b % 4][:, 0:CW]).then_inc(block_done[u], 1)


def gla_stage(core, cat, w_up, b_up, g_gla, tri, rev):
    nc = core.nc
    with ExitStack() as sc:
        s, p = core.sb(sc), core.ps(sc)
        qT, kT = s("g_qT", [P, GP, SEQ]), s("g_kT", [P, GP, SEQ])
        code, up = s("g_code", [RANK + 1, SEQ]), s("g_up", [RANK + 1, GK])
        v, r = s("g_v", [P, NB, GW]), s("g_r", [P, NB, GW])
        tri_s, rev_s = s("g_tri", [P, P]), s("g_rev", [P, P])
        mask = s("g_mask", [P, NB, P])
        e, la = s("g_e", [P, NB, GK]), s("g_la", [P, NB, GK])
        grow, shrink = s("g_grow", [P, GP, SEQ]), s("g_shrink", [P, GP, SEQ])
        kend = s("g_kend", [P, NB, GK])
        attn = [s(f"g_attn{u}", [P, NB, P]) for u in range(2)]
        state = s("g_state", [P, NCH, GDV])
        g_b = s("g_gb", [P, GW])
        ss, va, y, t = (s(f"g_{n}", [P, NB * GH]) for n in ("ss", "va", "y", "t"))
        pA, pB = p("g_pA", [P, NB, GK]), p("g_pB", [P, GP * SEQ])
        logT = pB[:, :].rearrange("p (h t) -> p h t", h=GP)
        kv = pA[:, :, :].rearrange("p b c -> p (b c)").rearrange("p (o n v) -> p o n v", o=2, v=GDV)
        attn_p = pB[:, 0:SEQ].rearrange("p (b c) -> p b c", c=P)
        o_p = pB[:, SEQ:2 * SEQ].rearrange("p (b c) -> p b c", c=P)
        names = ("ones code_in up_in qk_in v_in r_in tri_in mask_in gb_in z_ready e_act e_ready la_ready cum_ready "
                 "rev_ready decay_ready rev_exp kt_ready kd_ready kend_ready kv_ready state_ready attn_ready "
                 "masked zeroed o_ready o_copied silu squared var root chain").split()
        m = {n: core.sem(f"g_{n}") for n in names}
        with nc.Block() as block:
            @block.sync
            def _(sp):
                sp.wait_ge(m["ones"], 1)
                sp.dma_start(code[0:RANK, :], core.projT[NT_IN][0:RANK, :]).then_inc(m["code_in"], 16)
                sp.dma_start(up[0:RANK, :], w_up).then_inc(m["up_in"], 16)
                sp.dma_start(up[RANK:RANK + 1, :], b_up.rearrange("(a c) -> a c", a=1)).then_inc(m["up_in"], 16)
                sp.dma_start(tri_s[:], tri).then_inc(m["tri_in"], 16)
                sp.dma_start(rev_s[:], rev).then_inc(m["tri_in"], 16)
                for i in range(GP):
                    sp.dma_start(qT[:, i, :], core.projT[i]).then_inc(m["qk_in"], 16)
                    sp.dma_start(kT[:, i, :], core.projT[GP + i]).then_inc(m["qk_in"], 16)
                rows = core.projN.rearrange("(b p) c -> p b c", p=P)
                for b in range(NB):
                    sp.dma_start(mask[:, b, :], tri).then_inc(m["mask_in"], 16)
                sp.dma_start(v[:], rows[:, :, 0:GW]).then_inc(m["v_in"], 16)
                sp.dma_start(r[:], rows[:, :, GW:2 * GW]).then_inc(m["r_in"], 16)
                sp.dma_start(g_b[:], g_gla.partition_broadcast(P)).then_inc(m["gb_in"], 16)

            @block.gpsimd
            def _(pool):
                nc.gpsimd.memset(code[:], 1.0).then_inc(m["ones"], 1)
                nc.gpsimd.memset(state[:, 0, :], 0.0).then_inc(m["zeroed"], 1)
                for u in range(2):
                    nc.gpsimd.memset(attn[u][:], 0.0).then_inc(m["zeroed"], 1)

            @block.scalar
            def _(act):
                steps = Steps(act, m["e_act"])
                act.wait_ge(m["z_ready"], 1)
                steps(nc.scalar.activation(e[:], pA[:], ACT.Abs))
                steps(nc.scalar.activation(e[:], e[:], ACT.Exp, scale=-1.0))
                nc.scalar.activation(la[:], e[:], ACT.Ln, bias=1.0).then_inc(m["e_ready"], 1)
                act.wait_ge(m["cum_ready"], 1)
                nc.scalar.activation(grow[:], logT, ACT.Exp).then_inc(m["decay_ready"], 1)
                nc.scalar.activation(shrink[:], logT, ACT.Exp, scale=-1.0).then_inc(m["decay_ready"], 1)
                act.wait_ge(m["rev_ready"], 1)
                nc.scalar.activation(kend[:], pA[:], ACT.Exp).then_inc(m["rev_exp"], 1)
                act.wait_ge(m["r_in"], 16)
                nc.scalar.activation(r[:], r[:], ACT.Silu).then_inc(m["silu"], 1)
                for h in range(GH):
                    act.wait_ge(m["o_ready"], h + 1)
                    nc.scalar.activation(cat[:, :, h * GDV:(h + 1) * GDV], o_p, ACT.Copy).then_inc(m["o_copied"], 1)
                act.wait_ge(m["o_copied"], GH)
                nc.scalar.activation(v[:], cat[:, :, 0:GW], ACT.Square).then_inc(m["squared"], 1)
                act.wait_ge(m["var"], 1)
                nc.scalar.activation(y[:], t[:], ACT.Sqrt).then_inc(m["root"], 1)

            @block.vector
            def _(dve):
                steps = Steps(dve, m["chain"])
                dve.wait_ge(m["e_ready"], 1)
                nc.vector.scalar_tensor_tensor(out=la[:], in0=pA[:], scalar=0.0, in1=la[:],
                                               op0=ALU.min, op1=ALU.subtract).then_inc(m["la_ready"], 1)
                dve.wait_ge(m["qk_in"], 32 * GP)
                dve.wait_ge(m["decay_ready"], 2)
                nc.vector.scalar_tensor_tensor(out=qT[:], in0=qT[:], scalar=float(GDK) ** -0.5, in1=grow[:],
                                               op0=ALU.mult, op1=ALU.mult).then_inc(m["kd_ready"], 1)
                nc.vector.tensor_tensor(shrink[:], kT[:], shrink[:], ALU.mult).then_inc(m["kd_ready"], 1)
                dve.wait_ge(m["kt_ready"], 1)
                dve.wait_ge(m["rev_exp"], 1)
                nc.vector.tensor_tensor(kend[:], pA[:], kend[:], ALU.mult).then_inc(m["kend_ready"], 1)
                dve.wait_ge(m["zeroed"], 3)
                dve.wait_ge(m["mask_in"], 16 * NB)
                for hp in range(GP):
                    if hp:
                        dve.wait_ge(m["o_ready"], 2 * hp)
                    dve.wait_ge(m["kv_ready"], hp + 1)
                    for n in range(NCH - 1):
                        last = nc.vector.scalar_tensor_tensor(
                            out=state[:, n + 1, :], in0=state[:, n, :],
                            scalar=grow[:, hp, n * CH + CH - 1:n * CH + CH],
                            in1=kv[:, n % 2, n // 2, :], op0=ALU.mult, op1=ALU.add)
                        if n < NCH - 2:
                            steps(last)
                    last.then_inc(m["state_ready"], 1)
                    for h in (2 * hp, 2 * hp + 1):
                        dve.wait_ge(m["attn_ready"], h + 1)
                        if h >= 2:
                            dve.wait_ge(m["o_ready"], h - 1)
                        nc.vector.copy_predicated(attn[h % 2][:], mask[:].bitcast(U32), attn_p)\
                            .then_inc(m["masked"], 1)
                dve.wait_ge(m["squared"], 1)
                steps(nc.vector.tensor_reduce(ss[:], v[:].rearrange("p b (h c) -> p (b h) c", h=GH), AX_X, ALU.add))
                rstd(nc, steps, ss[:], va[:], y[:], t[:], GDV, m["var"], m["root"])
                oa = cat[:, :, 0:GW]
                dve.wait_ge(m["silu"], 1)
                dve.wait_ge(m["gb_in"], 16)
                steps(nc.vector.tensor_tensor(r[:], r[:], g_b[:].unsqueeze(1).to_broadcast([P, NB, GW]), ALU.mult))
                for b in range(NB):
                    steps(nc.vector.tensor_tensor(
                        oa[:, b, :].rearrange("p (h c) -> p h c", h=GH),
                        oa[:, b, :].rearrange("p (h c) -> p h c", h=GH),
                        y[:, b * GH:(b + 1) * GH].unsqueeze(2).to_broadcast([P, GH, GDV]), ALU.mult))
                steps(nc.vector.tensor_tensor(oa, oa, r[:], ALU.mult))

            @block.tensor
            def _(pe):
                pe.wait_ge(m["code_in"], 16)
                pe.wait_ge(m["up_in"], 32)
                for b in range(NB):
                    last = nc.tensor.matmul(pA[:, b, :], code[:, b * P:(b + 1) * P], up[:], start=True, stop=True)
                last.then_inc(m["z_ready"], 1)
                pe.wait_ge(m["la_ready"], 1)
                pe.wait_ge(m["tri_in"], 32)
                for hp in range(GP):
                    for b in range(NB):
                        last = nc.tensor.matmul(logT[:, hp, b * P:(b + 1) * P], la[:, b, hp * P:(hp + 1) * P],
                                                tri_s[:], start=True, stop=True)
                last.then_inc(m["cum_ready"], 1)
                for b in range(NB):
                    last = nc.tensor.matmul(pA[:, b, :], rev_s[:], la[:, b, :], start=True, stop=True)
                last.then_inc(m["rev_ready"], 1)
                pe.wait_ge(m["rev_exp"], 1)
                pe.wait_ge(m["qk_in"], 32 * GP)
                for b in range(NB):
                    for hp in range(GP):
                        last = nc.tensor.transpose(pA[:, b, hp * P:(hp + 1) * P], kT[:, hp, b * P:(b + 1) * P],
                                                   core.ident[:])
                last.then_inc(m["kt_ready"], 1)
                pe.wait_ge(m["kd_ready"], 2)
                pe.wait_ge(m["kend_ready"], 1)
                pe.wait_ge(m["v_in"], 16)
                for hp in range(GP):
                    if hp:
                        pe.wait_ge(m["state_ready"], hp)
                    for j in range(2):
                        h = 2 * hp + j
                        for odd in range(2):
                            for n in range(odd, NCH, 2):
                                rows = slice(odd * CH, odd * CH + CH)
                                last = nc.tensor.matmul(kv[j * GDK:(j + 1) * GDK, odd, n // 2, :],
                                                        kend[rows, n // 2, h * GDK:(h + 1) * GDK],
                                                        v[rows, n // 2, h * GDV:(h + 1) * GDV],
                                                        start=True, stop=True, skip_group_check=True)
                    last.then_inc(m["kv_ready"], 1)
                    for j in range(2):
                        h = 2 * hp + j
                        rows = slice(j * GDK, (j + 1) * GDK)
                        if h:
                            pe.wait_ge(m["masked"], h)
                        for b in range(NB):
                            cols = slice(b * P, (b + 1) * P)
                            last = nc.tensor.matmul(attn_p[:, b, :], shrink[rows, hp, cols], qT[rows, hp, cols],
                                                    start=True, stop=True)
                        last.then_inc(m["attn_ready"], 1)
                        pe.wait_ge(m["state_ready"], hp + 1)
                        pe.wait_ge(m["masked"], h + 1)
                        if h:
                            pe.wait_ge(m["o_copied"], h)
                        for b in range(NB):
                            nc.tensor.matmul(o_p[:, b, :], attn[h % 2][:, b, :], v[:, b, h * GDV:(h + 1) * GDV],
                                             start=True, stop=False, skip_group_check=True)
                            for n in (2 * b, 2 * b + 1):
                                half = slice((n % 2) * CH, (n % 2) * CH + CH)
                                last = nc.tensor.matmul(o_p[half, b, :], qT[rows, hp, n * CH:(n + 1) * CH],
                                                        state[rows, n, :], start=False, stop=(n % 2 == 1),
                                                        skip_group_check=True)
                        last.then_inc(m["o_ready"], 1)


def attention_stage(core, cat, positions, rot, freq, logmult):
    nc = core.nc
    with ExitStack() as sc:
        s, p = core.sb(sc), core.ps(sc)
        cos, sin = s("a_cos", [P, SEQ]), s("a_sin", [P, SEQ])
        work, turns = s("a_work", [P, SEQ]), s("a_turns", [P, SEQ])
        pos_i = s("a_pos", [P, SEQ], I32)
        freq_s, rot_s, bias = s("a_freq", [P, 1]), s("a_rot", [P, P]), s("a_bias", [P, SEQ])
        raw, qk = s("a_raw", [P, 2, SEQ]), s("a_qk", [P, 2, SEQ])
        vb = s("a_v", [P, NB, AH * AD])
        sc_s = [s(f"a_scores{u}", [P, SEQ]) for u in range(2)]
        pr = [s(f"a_probs{u}", [P, SEQ]) for u in range(2)]
        prT = [s(f"a_probsT{u}", [P, NB, P]) for u in range(2)]
        top, low, mark = s("a_top", [P, 2]), s("a_low", [P, 2]), s("a_mark", [P, 1])
        units = 2 * NB
        den, inv = s("a_den", [P, units]), s("a_inv", [P, units])
        s_p = [p(f"a_ps{u}", [P, 2, HALF]) for u in range(2)]
        t_p = p("a_pt", [P, NB, P])
        o_p = [p(f"a_po{u}", [P, HALF]) for u in range(2)]
        m = {n: core.sem(f"a_{n}") for n in "pos_in freq_in bias_in rot_in v_in qk_in angle_ready sin_ready rope_ps rope_ready chain last_ready".split()}
        scored, topped, lowered, exped, turned, prT_ready, mixed, o_done = (
            core.sems(f"a_{n}", 2) for n in ("scored", "topped", "lowered", "exped", "turned", "prT", "mixed", "o_done"))
        UH = units // 2
        pairs = AH // 2

        def block_of(n):
            return n // NB, n % NB

        with nc.Block() as block:
            @block.sync
            def _(sp):
                sp.dma_start(pos_i[:], positions.rearrange("a t -> (a t)").partition_broadcast(P)).then_inc(m["pos_in"], 16)
                sp.dma_start(freq_s[:], freq).then_inc(m["freq_in"], 16)
                sp.dma_start(rot_s[:], rot).then_inc(m["rot_in"], 16)
                sp.dma_start(bias[:], logmult).then_inc(m["bias_in"], 16)
                sp.dma_start(vb[:], core.projN.rearrange("(b p) c -> p b c", p=P)[:, :, 2 * GW:N_IN])\
                    .then_inc(m["v_in"], 16)
                @rounds(sp, pairs)
                def _(it):
                    wait_past(sp, m["rope_ready"], 2 * it)
                    sp.dma_start(raw[:, 0, :], core.projT[it + 2 * GP]).then_inc(m["qk_in"], 16)
                    sp.dma_start(raw[:, 1, :], core.projT[it + 2 * GP + pairs]).then_inc(m["qk_in"], 16)

            @block.vector
            def _(dve):
                steps = Steps(dve, m["chain"])
                TT, TS = nc.vector.tensor_tensor, nc.vector.tensor_scalar
                dve.wait_ge(m["pos_in"], 16)
                dve.wait_ge(m["freq_in"], 16)
                steps(nc.vector.tensor_copy(work[:], pos_i[:]))
                steps(TS(work[:], work[:], freq_s[:, 0:1], None, ALU.mult))
                steps(TS(turns[:], work[:], 0.15915494309189535, 12582912.0, ALU.mult, ALU.add))
                steps(TS(turns[:], turns[:], 12582912.0, None, ALU.subtract))
                for part in (6.28125, 1.93500518798828125e-3, 3.0199159819567529e-7):
                    steps(nc.vector.scalar_tensor_tensor(out=work[:], in0=turns[:], scalar=-part, in1=work[:],
                                                         op0=ALU.mult, op1=ALU.add))
                TS(work[:], work[:], 3.1415925, -3.1415925, ALU.min, ALU.max).then_inc(m["angle_ready"], 1)
                dve.wait_ge(m["sin_ready"], 2)
                steps(TT(cos[:], cos[:], cos[:], ALU.mult))
                steps(TS(cos[:], cos[:], -2.0, 1.0, ALU.mult, ALU.add))
                dve.wait_ge(m["bias_in"], 16)
                start = steps.n
                @rounds(dve, pairs)
                def _(it):
                    steps.base, steps.n = it * 4 + start, 0
                    dve.wait_ge(m["qk_in"], 32 * it + 32)
                    dve.wait_ge(m["rope_ps"], it + 1)
                    for i in range(2):
                        steps(TT(qk[:, i, :], raw[:, i, :], cos[:], ALU.mult))
                        steps(TT(work[:], s_p[i][:].rearrange("p a b -> p (a b)"), sin[:], ALU.mult))
                        TT(qk[:, i, :], qk[:, i, :], work[:], ALU.add).then_inc(m["rope_ready"], 1)
                        dve.wait_ge(m["rope_ready"], 2 * it + i + 1)

                    def maximum(n):
                        _, i = block_of(n)
                        u, w = n % 2, (i + 1) * P
                        dve.wait_ge(scored[u], it * UH + n // 2 + 1)
                        wait_past(dve, exped[u], it * UH + n // 2)
                        hold(nc, mark[:])
                        nc.vector.tensor_tensor_reduce(
                            out=sc_s[u][:, 0:w], in0=s_p[u][:].rearrange("p a b -> p (a b)")[:, 0:w],
                            in1=bias[:, SEQ - w:SEQ], scale=1.0, scalar=LOWEST, op0=ALU.add, op1=ALU.max,
                            accum_out=top[:, u:u + 1]).then_inc(topped[u], 1)
                        dve.wait_ge(topped[u], it * UH + n // 2 + 1)
                        TS(low[:, u:u + 1], top[:, u:u + 1], -float(AD) ** -0.5, None, ALU.mult)\
                            .then_inc(lowered[u], 1)

                    def turn(n):
                        u, w = n % 2, block_of(n)[1] + 1
                        dve.wait_ge(turned[u], it * UH + n // 2 + 1)
                        wait_past(dve, mixed[u], it * UH + n // 2)
                        nc.vector.tensor_copy(prT[u][:, 0:w, :], t_p[:, 0:w, :]).then_inc(prT_ready[u], 1)

                    def output(n):
                        j, i = block_of(n)
                        u = n % 2
                        dve.wait_ge(mixed[u], it * UH + n // 2 + 1)
                        nc.vector.reciprocal(inv[:, n:n + 1], den[:, n:n + 1]).then_inc(m["last_ready"], 1)
                        dve.wait_ge(m["last_ready"], it * units + n + 1)
                        TS(cat[:, i, bass.ds(it * 2 * AD + (GW + j * AD), AD)], o_p[u][:, 0:AD],
                           inv[:, n:n + 1], None, ALU.mult).then_inc(o_done[u], 1)

                    maximum(0)
                    for n in range(units):
                        if n + 1 < units:
                            maximum(n + 1)
                        if n % 2:
                            turn(n)
                        if n:
                            output(n - 1)
                    output(units - 1)

            @block.scalar
            def _(act):
                act.wait_ge(m["angle_ready"], 1)
                nc.scalar.activation(sin[:], work[:], ACT.Sin).then_inc(m["sin_ready"], 1)
                nc.scalar.activation(cos[:], work[:], ACT.Sin, scale=0.5).then_inc(m["sin_ready"], 1)
                @rounds(act, pairs)
                def _(it):
                    def expo(n):
                        u, w = n % 2, (block_of(n)[1] + 1) * P
                        act.wait_ge(lowered[u], it * UH + n // 2 + 1)
                        wait_past(act, turned[u], it * UH + n // 2)
                        wait_past(act, o_done[u], it * UH)
                        nc.scalar.activation(pr[u][:, 0:w], sc_s[u][:, 0:w], ACT.Exp, bias=low[:, u:u + 1],
                                             scale=float(AD) ** -0.5, accum_out=den[:, n:n + 1])\
                            .then_inc(exped[u], 1)

                    def turn(n):
                        u, w = n % 2, block_of(n)[1] + 1
                        act.wait_ge(turned[u], it * UH + n // 2 + 1)
                        wait_past(act, mixed[u], it * UH + n // 2)
                        nc.scalar.activation(prT[u][:, 0:w, :], t_p[:, 0:w, :], ACT.Copy).then_inc(prT_ready[u], 1)

                    expo(0)
                    for n in range(units):
                        if n + 1 < units:
                            expo(n + 1)
                        if n % 2 == 0:
                            turn(n)

            @block.tensor
            def _(pe):
                pe.wait_ge(m["rot_in"], 16)
                pe.wait_ge(m["v_in"], 16)
                @rounds(pe, pairs)
                def _(it):
                    pe.wait_ge(m["qk_in"], 32 * it + 32)
                    for i in range(2):
                        wait_past(pe, topped[i], it * UH)
                        for half in range(2):
                            last = nc.tensor.matmul(s_p[i][:, half, :], rot_s[:],
                                                    raw[:, i, half * HALF:(half + 1) * HALF], start=True, stop=True)
                    last.then_inc(m["rope_ps"], 1)
                    pe.wait_ge(m["rope_ready"], 2 * it + 2)

                    def score(n):
                        j, i = block_of(n)
                        u, rows = n % 2, slice(j * AD, (j + 1) * AD)
                        wait_past(pe, topped[u], it * UH + n // 2)
                        w = (i + 1) * P
                        for half in range(0, w, HALF):
                            width = min(HALF, w - half)
                            last = nc.tensor.matmul(s_p[u][:, half // HALF, 0:width], qk[rows, 0, i * P:(i + 1) * P],
                                                    qk[rows, 1, half:half + width], start=True, stop=True)
                        last.then_inc(scored[u], 1)

                    def turn(n):
                        u, w = n % 2, block_of(n)[1] + 1
                        pe.wait_ge(exped[u], it * UH + n // 2 + 1)
                        wait_past(pe, prT_ready[1 - u], it * UH + (n + 1) // 2)
                        for b in range(w):
                            last = nc.tensor.transpose(t_p[:, b, :], pr[u][:, b * P:(b + 1) * P], core.ident[:])
                        last.then_inc(turned[u], 1)

                    def mix(n):
                        j, i = block_of(n)
                        u = n % 2
                        pe.wait_ge(prT_ready[u], it * UH + n // 2 + 1)
                        wait_past(pe, o_done[u], it * UH + n // 2)
                        for b in range(i + 1):
                            last = nc.tensor.matmul(o_p[u][:, 0:AD], prT[u][:, b, :],
                                                    vb[:, b, bass.ds(it * 2 * AD + j * AD, AD)],
                                                    start=(b == 0), stop=(b == i))
                        last.then_inc(mixed[u], 1)

                    score(0)
                    for n in range(units):
                        if n + 1 < units:
                            score(n + 1)
                        turn(n)
                        if n:
                            mix(n - 1)
                    mix(units - 1)


def out_projection(core, cat, w_out):
    nc = core.nc
    with ExitStack() as sc:
        p = core.ps(sc)
        catT = core.hT_pair(sc, "catT")
        block_done = core.sems("o_block_done", 2)
        W = Weights(core, sc, "o", CW, block_done, NB)
        turned, hi_done, lo_done, added = core.sem("o_turned"), core.sem("o_hi"), core.sem("o_lo"), core.sems("o_added", 2)
        pairs = D // CW // 2
        w_v = w_out.rearrange("(k p) c -> p k c", p=P)
        with ExitStack() as inner:
            tp = [core.ps(inner)(f"o_tp{u}", [P, KD, P]) for u in range(2)]
            with nc.Block() as block:
                @block.tensor
                def _(pe):
                    for b in range(NB):
                        if b >= 2:
                            pe.wait_ge(lo_done, b - 1)
                        for k in range(KD):
                            last = nc.tensor.transpose(tp[b % 2][:, k, :], cat[:, b, k * P:(k + 1) * P], core.ident[:])
                        last.then_inc(turned, 1)

                @block.scalar
                def _(act):
                    for b in range(NB):
                        act.wait_ge(turned, b + 1)
                        nc.scalar.activation(catT[0][:, :, b * P:(b + 1) * P], tp[b % 2][:], ACT.Copy)\
                            .then_inc(hi_done, 1)

                @block.vector
                def _(dve):
                    for b in range(NB):
                        dve.wait_ge(hi_done, b + 1)
                        cols = slice(b * P, (b + 1) * P)
                        nc.vector.tensor_tensor(catT[1][:, :, cols], tp[b % 2][:],
                                                catT[0][:, :, cols].bitcast(F32), ALU.subtract).then_inc(lo_done, 1)
        ps = [[p(f"o_ps{u}{r}", [P, HALF]) for r in range(4)] for u in range(2)]
        with nc.Block() as block:
            @block.sync
            def _(sp):
                @rounds(sp, pairs)
                def _(it):
                    for u in range(2):
                        W.load(sp, u, it, w_v[:, :, bass.ds((it * 2 + u) * CW, CW)])

            @block.scalar
            def _(act):
                @rounds(act, pairs)
                def _(it):
                    for u in range(2):
                        W.hi(act, u, it)

            @block.vector
            def _(dve):
                def add(u, n):
                    for b in range(NB):
                        dve.wait_ge(block_done[u], NB * n + b + 1)
                        cols = core.xres[:, b, bass.ds((n * 2 + u) * CW, CW)]
                        nc.vector.tensor_tensor(cols, ps[u][b % 4][:, 0:CW], cols, ALU.add).then_inc(added[u], 1)

                for u in range(2):
                    W.lo(dve, u, 0)
                @rounds(dve, pairs - 1)
                def _(it):
                    for u in range(2):
                        add(u, it)
                        W.lo(dve, u, it + 1)
                for u in range(2):
                    add(u, pairs - 1)

            @block.tensor
            def _(pe):
                @rounds(pe, pairs)
                def _(it):
                    for u in range(2):
                        pe.wait_ge(W.lo_done[u], it + 1)
                        for b in range(NB):
                            wait_past(pe, added[u], NB * it + max(b - 3, 0))
                            product_N(nc, W.part[u], catT, b, ps[u][b % 4][:, 0:CW]).then_inc(block_done[u], 1)


def query_stage(core, hT, w_q, keysT, top_v, top_i):
    nc = core.nc
    with ExitStack() as sc:
        s, p = core.sb(sc), core.ps(sc)
        tile_done = core.sems("q_tile_done", 2)
        W = Weights(core, sc, "q", P, tile_done)
        keys = s("q_keys", [P, SIDES, KEYS])
        qr = [s(f"q_qr{u}", [P, SEQ]) for u in range(2)]
        scores = [s(f"q_sc{u}", [P, NB, KEYS]) for u in range(2)]
        rest = s("q_rest", [P, NB, KEYS])
        mark = s("q_mark", [P, 1])
        best, best_i = s("q_best", [P, NB, TOPK]), s("q_best_i", [P, NB, TOPK], U32)
        ps = [p(f"q_ps{u}", [P, 2, HALF]) for u in range(2)]
        sc_p = [p(f"q_scp{u}", [P, NB, KEYS]) for u in range(2)]
        keys_in, chain = core.sem("q_keys_in"), core.sem("q_chain")
        copied, scored, sc_copied, picked = (core.sems(f"q_{n}", 2) for n in ("copied", "scored", "sc_copied", "picked"))
        pairs = SIDES // 2
        with nc.Block() as block:
            @block.sync
            def _(sp):
                sp.dma_start(keys[:], keysT).then_inc(keys_in, 16)
                @rounds(sp, pairs)
                def _(it):
                    for u in range(2):
                        W.load(sp, u, it, w_q[it * 2 + u])

            @block.scalar
            def _(act):
                def evacuate(u, n):
                    act.wait_ge(tile_done[u], n + 1)
                    wait_past(act, scored[u], n)
                    nc.scalar.activation(qr[u][:], ps[u][:], ACT.Copy).then_inc(copied[u], 1)

                def copy_scores(u, n):
                    act.wait_ge(scored[u], n + 1)
                    wait_past(act, picked[u], n)
                    nc.scalar.activation(scores[u][:], sc_p[u][:], ACT.Copy).then_inc(sc_copied[u], 1)

                for u in range(2):
                    W.hi(act, u, 0)
                @rounds(act, pairs - 1)
                def _(it):
                    for u in range(2):
                        evacuate(u, it)
                        W.hi(act, u, it + 1)
                        copy_scores(u, it)
                for u in range(2):
                    evacuate(u, pairs - 1)
                    copy_scores(u, pairs - 1)

            @block.vector
            def _(dve):
                steps = Steps(dve, chain)
                PER = 10

                def pick(u, n):
                    dve.wait_ge(sc_copied[u], n + 1)
                    V, src = nc.vector, scores[u]
                    hold(nc, mark[:])
                    for b in range(NB):
                        last = V.max(best[:, b, 0:8], src[:, b, :])
                    steps(last)
                    hold(nc, mark[:])
                    for b in range(NB):
                        last = V.max_index(best_i[:, b, 0:8], best[:, b, 0:8], src[:, b, :])
                    for b in range(NB):
                        last = V.match_replace(rest[:, b, :], best[:, b, 0:8], src[:, b, :], LOWEST)
                    steps(last)
                    hold(nc, mark[:])
                    for b in range(NB):
                        last = V.max(best[:, b, 8:16], rest[:, b, :])
                    steps(last)
                    hold(nc, mark[:])
                    for b in range(NB):
                        last = V.max_index(best_i[:, b, 8:16], best[:, b, 8:16], rest[:, b, :])
                    steps(last)
                    side = bass.ds(n * 2 + u, 1)
                    steps(V.tensor_scalar(top_v[:, :, side, :].rearrange("p b a k -> p (b a) k"), best[:], 1.0, None, ALU.mult))
                    V.tensor_scalar(top_i[:, :, side, :].rearrange("p b a k -> p (b a) k"), best_i[:], 1.0, None,
                                    ALU.mult).then_inc(picked[u], 1)
                    dve.wait_ge(picked[u], n + 1)

                for u in range(2):
                    W.lo(dve, u, 0)
                @rounds(dve, pairs - 1)
                def _(it):
                    steps.base, steps.n = it * PER, 0
                    for u in range(2):
                        W.lo(dve, u, it + 1)
                        pick(u, it)
                    assert steps.n == PER
                steps.base = (pairs - 1) * PER
                steps.n = 0
                for u in range(2):
                    pick(u, pairs - 1)

            @block.tensor
            def _(pe):
                def tile(u, n):
                    pe.wait_ge(W.lo_done[u], n + 1)
                    wait_past(pe, copied[u], n)
                    product_T(nc, W, u, hT, ps[u]).then_inc(tile_done[u], 1)

                def score(u, n):
                    pe.wait_ge(copied[u], n + 1)
                    wait_past(pe, sc_copied[u], n)
                    for b in range(NB):
                        last = nc.tensor.matmul(sc_p[u][:, b, :], qr[u][:, b * P:(b + 1) * P],
                                                keys[:, bass.ds(n * 2 + u, 1), :].rearrange("p a k -> p (a k)"),
                                                start=True, stop=True)
                    last.then_inc(scored[u], 1)

                pe.wait_ge(keys_in, 16)
                tile(0, 0)
                @rounds(pe, pairs - 1)
                def _(it):
                    tile(1, it)
                    score(0, it)
                    tile(0, it + 1)
                    score(1, it)
                tile(1, pairs - 1)
                score(0, pairs - 1)
                score(1, pairs - 1)


def gate_stage(core, top_v, top_i):
    nc = core.nc
    with ExitStack() as sc:
        s, p = core.sb(sc), core.ps(sc)
        CN = TOPK * TOPK
        cand, rest = s("t_cand", [P, PH, CN]), s("t_rest", [P, PH, CN])
        best, pos = s("t_best", [P, PH, TOPK]), s("t_pos", [P, PH, TOPK], U32)
        part_u = s("t_part_u", [P, PH, TOPK], U32)
        part = s("t_part", [P, PH, TOPK])
        packed = s("t_packed", [P, 3, SLOTS])
        packedT = s("t_packedT", [P, 3, P])
        total, mark = s("t_total", [P, PH]), s("t_mark", [P, 1])
        iota = s("t_iota", [P, KEYS])
        iota_i = s("t_iota_i", [P, KEYS], I32)
        RQ, TQ = 2, 4
        first, second = s("t_first", [P, RQ, TQ, KEYS]), s("t_second", [P, RQ, TQ, KEYS])
        dense = [s(f"t_dense{u}", [P, KEYS, TB]) for u in range(2)]
        tr_p = p("t_trp", [P, HALF])
        g_p = [p(f"t_gp{r}", [P, TQ, KEYS]) for r in range(RQ)]
        m = {n: core.sem(f"t_{n}") for n in "iota_i iota chain best_ready exped packed turned unpacked half0 half1".split()}
        hot, produced, copied = core.sems("t_hot", RQ), core.sems("t_produced", RQ), core.sems("t_copied", RQ)
        stored = core.sems("t_stored", 2)
        groups = P // TQ
        G4 = groups // RQ
        HG = groups // 2
        with nc.Block() as block:
            @block.gpsimd
            def _(pool):
                nc.gpsimd.iota(iota_i[:], pattern=[[1, KEYS]], base=0, channel_multiplier=0).then_inc(m["iota_i"], 1)
                pool.wait_ge(m["iota_i"], 1)
                nc.gpsimd.tensor_copy(iota[:], iota_i[:]).then_inc(m["iota"], 1)

            @block.vector
            def _(dve):
                V = nc.vector
                steps = Steps(dve, m["chain"])
                dve.wait_ge(m["iota"], 1)
                PER = 18
                @rounds(dve, NB)
                def _(b):
                    steps.base, steps.n = b * PER, 0
                    tv = [top_v[:, bass.ds(b, 1), c::2, :].rearrange("p a h k -> p (a h) k") for c in range(2)]
                    ti = [top_i[:, bass.ds(b, 1), c::2, :].rearrange("p a h k -> p (a h) k") for c in range(2)]
                    wide = [P, PH, TOPK, TOPK]
                    steps(V.tensor_tensor(cand[:].rearrange("p h (i j) -> p h i j", i=TOPK),
                                          tv[0].unsqueeze(3).to_broadcast(wide), tv[1].unsqueeze(2).to_broadcast(wide),
                                          ALU.add))
                    hold(nc, mark[:])
                    for h in range(PH):
                        last = V.max(best[:, h, 0:8], cand[:, h, :])
                    steps(last)
                    hold(nc, mark[:])
                    for h in range(PH):
                        last = V.max_index(pos[:, h, 0:8], best[:, h, 0:8], cand[:, h, :])
                    for h in range(PH):
                        last = V.match_replace(rest[:, h, :], best[:, h, 0:8], cand[:, h, :], LOWEST)
                    steps(last)
                    hold(nc, mark[:])
                    for h in range(PH):
                        last = V.max(best[:, h, 8:16], rest[:, h, :])
                    steps(last)
                    hold(nc, mark[:])
                    for h in range(PH):
                        last = V.max_index(pos[:, h, 8:16], best[:, h, 8:16], rest[:, h, :])
                    steps(last)
                    wait_past(dve, m["turned"], 3 * b)
                    gate = packed[:, 0, :].rearrange("p (h k) -> p h k", h=PH)
                    V.tensor_tensor(gate, best[:], best[:, :, 0:1].to_broadcast([P, PH, TOPK]), ALU.subtract)\
                        .then_inc(m["best_ready"], 1)
                    hot4 = rest[:].rearrange("p h (i j) -> p h i j", i=TOPK)
                    for c in range(2):
                        if c == 0:
                            steps(V.tensor_scalar(part_u[:], pos[:], 4, None, ALU.logical_shift_right))
                        else:
                            steps(V.tensor_scalar(part_u[:], pos[:], TOPK - 1, None, ALU.bitwise_and))
                        steps(V.tensor_copy(part[:], part_u[:]))
                        steps(V.tensor_tensor(hot4, part[:].unsqueeze(3).to_broadcast(wide),
                                              iota[:, 0:TOPK].unsqueeze(1).unsqueeze(1).to_broadcast(wide),
                                              ALU.is_equal))
                        steps(V.tensor_tensor(hot4, hot4, ti[c].unsqueeze(2).to_broadcast(wide), ALU.mult))
                        steps(V.tensor_reduce(packed[:, 1 + c, :], rest[:].rearrange("p h (i j) -> p (h i) j", i=TOPK),
                                              AX_X, ALU.add))
                    dve.wait_ge(m["exped"], b + 1)
                    steps(V.tensor_reduce(total[:], gate, AX_X, ALU.add))
                    steps(V.reciprocal(total[:], total[:]))
                    V.tensor_tensor(gate, gate, total[:].unsqueeze(2).to_broadcast([P, PH, TOPK]), ALU.mult)\
                        .then_inc(m["packed"], 1)
                    dve.wait_ge(m["turned"], 3 * b + 3)
                    steps(V.tensor_copy(packedT[:], tr_p[:, 0:3 * P].rearrange("p (a t) -> p a t", a=3)))
                    for q in range(groups):
                        r = q % RQ
                        wait_past(dve, produced[r], b * G4 + q // RQ)
                        for i in range(TQ):
                            tok = q * TQ + i
                            V.tensor_scalar(first[:, r, i, :], iota[:], packedT[:, 1, tok:tok + 1], None, ALU.is_equal)
                            last = V.tensor_scalar(second[:, r, i, :], iota[:], packedT[:, 2, tok:tok + 1],
                                                   packedT[:, 0, tok:tok + 1], ALU.is_equal, ALU.mult)
                        last.then_inc(hot[r], 1)
                    dve.wait_ge(hot[RQ - 1], b * G4 + G4)
                    assert steps.n == PER, steps.n

            @block.scalar
            def _(act):
                @rounds(act, NB)
                def _(b):
                    act.wait_ge(m["best_ready"], b + 1)
                    nc.scalar.activation(packed[:, 0, :], packed[:, 0, :], ACT.Exp).then_inc(m["exped"], 1)
                    for q in range(groups):
                        r, u = q % RQ, q // HG
                        if q % HG == 0:
                            wait_past(act, stored[u], 16 * b)
                        act.wait_ge(produced[r], b * G4 + q // RQ + 1)
                        at = (q % HG) * TQ
                        ins = nc.scalar.activation(dense[u][:, :, at:at + TQ],
                                                   g_p[r][:].rearrange("p t j -> p j t"), ACT.Copy)
                        ins.then_inc(copied[r], 1)

            @block.sync
            def _(sp):
                @rounds(sp, NB)
                def _(b):
                    for u in range(2):
                        for r in range(RQ):
                            sp.wait_ge(copied[r], b * G4 + (u + 1) * HG // RQ)
                        sp.dma_start(core.gates[b * 2 + u], dense[u][:]).then_inc(stored[u], 16)
                for u in range(2):
                    sp.wait_ge(stored[u], 16 * NB)

            @block.tensor
            def _(pe):
                @rounds(pe, NB)
                def _(b):
                    pe.wait_ge(m["packed"], b + 1)
                    for i in range(3):
                        nc.tensor.transpose(tr_p[:, i * P:(i + 1) * P], packed[:, i, :], core.ident[:])\
                            .then_inc(m["turned"], 1)
                    for q in range(groups):
                        r = q % RQ
                        pe.wait_ge(hot[r], b * G4 + q // RQ + 1)
                        wait_past(pe, copied[r], b * G4 + q // RQ)
                        for i in range(TQ):
                            last = nc.tensor.matmul(g_p[r][:, i, :], first[:, r, i, :], second[:, r, i, :],
                                                    start=True, stop=True)
                        last.then_inc(produced[r], 1)


def expert_stage(core, hT, uT, v_tab):
    nc = core.nc
    GT = 2
    BT = 2 * GT
    groups = KEYS // GT
    bodies = groups // 2
    with ExitStack() as sc:
        s, p = core.sb(sc), core.ps(sc)
        u_raw = [s(f"e_uraw{i}", [P, KD, P]) for i in range(2)]
        u_part = [[s(f"e_u{n}{i}", [P, KD, P], F32R) for n in ("hi", "lo")] for i in range(2)]
        v_raw = s("e_vraw", [P, D])
        v_part = [[s(f"e_v{n}{i}", [P, D], F32R) for n in ("hi", "lo")] for i in range(BT)]
        w_part = [[s(f"e_w{n}{i}", [P, SEQ], F32R) for n in ("hi", "lo")] for i in range(BT)]
        gates = s("e_gates", [P, NTB, GT, TB])
        act_s = [s(f"e_act{i}", [P, SEQ]) for i in range(2)]
        a_p = [p(f"e_ap{i}", [P, 2, HALF]) for i in range(2)]
        o_p = [p(f"e_op{i}", [P, 2, HALF]) for i in range(2)]
        g_in = core.sem("e_g_in")
        v_in = core.sem("e_v_in")
        u_in = core.sems("e_u_in", 2)
        u_hi, u_lo, v_hi, v_lo, h_done, gelu_done, w_done, w_hi, w_lo = (
            core.sems(f"e_{n}", BT) for n in ("u_hi", "u_lo", "v_hi", "v_lo", "h_done", "gelu", "w", "w_hi", "w_lo"))
        out_done, added = core.sems("e_out_done", 2), core.sems("e_added", 2)
        gates_v = core.gates.rearrange("t i j c -> i t j c")
        v_v = v_tab.rearrange("(i j) d -> j i d", j=KEYS)

        def reached(eng, sems_, it, k, back=0):
            n = k - back
            value = it + (n // BT + 1)
            wait_past(eng, sems_[n % BT], value)

        with nc.Block() as block:
            @block.sync
            def _(sp):
                def load_u(it, k):
                    reached(sp, u_lo, it, k, 2)
                    sp.dma_start(u_raw[k % 2][:], uT[it * BT + k]).then_inc(u_in[k % 2], 16)

                def load_v(it, k):
                    reached(sp, v_lo, it, k, 1)
                    sp.dma_start(v_raw[:], v_v[it * BT + k]).then_inc(v_in, 16)

                def load_gates(it, k):
                    reached(sp, w_done, it, k, 1)
                    sp.dma_start(gates[:], gates_v[:, :, bass.ds(it * BT + k, GT), :]).then_inc(g_in, 16)

                def tile(it, k):
                    load_u(it, k)
                    if k % GT == 0:
                        load_gates(it, k)
                    load_v(it, k)

                for k in range(BT):
                    tile(0, k)
                with sp.Fori(1, bodies) as it:
                    for k in range(BT):
                        tile(it, k)

            @block.scalar
            def _(act):
                def split_u(it, k):
                    act.wait_ge(u_in[k % 2], 16 * (it * 2 + k // 2 + 1))
                    reached(act, h_done, it, k, 2)
                    nc.scalar.activation(u_part[k % 2][0][:], u_raw[k % 2][:], ACT.Copy).then_inc(u_hi[k % BT], 1)

                def gelu(it, k):
                    reached(act, h_done, it, k)
                    reached(act, w_lo, it, k, 2)
                    nc.scalar.activation(act_s[k % 2][:], a_p[k % 2][:], ACT.Gelu).then_inc(gelu_done[k % BT], 1)

                def group_read(it, k):
                    group = k // GT - 2
                    wait_past(act, out_done[group % 2], NB * (it + (group // 2 + 1)))

                def split_w(it, k):
                    reached(act, w_done, it, k)
                    group_read(it, k)
                    nc.scalar.activation(w_part[k % BT][0][:], act_s[k % 2][:], ACT.Copy).then_inc(w_hi[k % BT], 1)

                def split_v(it, k):
                    act.wait_ge(v_in, 16 * (it * BT + k + 1))
                    group_read(it, k)
                    nc.scalar.activation(v_part[k % BT][0][:], v_raw[:], ACT.Copy).then_inc(v_hi[k % BT], 1)

                def weigh(it, k):
                    for t in range(k, k + GT):
                        split_v(it, t)
                        gelu(it, t)
                        split_w(it, t)

                def split_us(it, k):
                    for t in range(k, k + GT):
                        split_u(it, t)

                split_us(0, 0)
                weigh(0, 0)
                split_us(0, 2)
                weigh(0, 2)
                split_us(0, 4)
                weigh(0, 4)
                split_us(0, 6)
                with act.Fori(1, bodies - 1) as it:
                    weigh(it, 2)
                    split_us(it, 4)
                    weigh(it, 4)
                    split_us(it, 6)
                weigh(bodies - 1, 2)

            @block.gpsimd
            def _(pool):
                def split_v(it, k):
                    reached(pool, v_hi, it, k)
                    nc.gpsimd.tensor_tensor(v_part[k][1][:], v_raw[:], v_part[k][0][:].bitcast(F32), ALU.subtract)\
                        .then_inc(v_lo[k], 1)

                for k in range(BT):
                    split_v(0, k)
                with pool.Fori(1, bodies) as it:
                    for k in range(BT):
                        split_v(it, k)

            @block.vector
            def _(dve):
                def split_us(it, k):
                    for t in range(k, k + GT):
                        reached(dve, u_hi, it, t)
                        nc.vector.tensor_tensor(u_part[t % 2][1][:], u_raw[t % 2][:],
                                                u_part[t % 2][0][:].bitcast(F32), ALU.subtract)\
                            .then_inc(u_lo[t % BT], 1)

                def weigh(it, k):
                    for t in range(k, k + GT):
                        if t == k:
                            dve.wait_ge(g_in, 16 * (it * 2 + k // GT + 1))
                        reached(dve, gelu_done, it, t)
                        w = act_s[t % 2][:].rearrange("p (t c) -> p t c", c=TB)
                        nc.vector.tensor_tensor(w, w, gates[:, :, t % GT, :], ALU.mult).then_inc(w_done[t % BT], 1)
                        reached(dve, w_hi, it, t)
                        nc.vector.tensor_tensor(w_part[t % BT][1][:], act_s[t % 2][:],
                                                w_part[t % BT][0][:].bitcast(F32), ALU.subtract)\
                            .then_inc(w_lo[t % BT], 1)

                def add(it, g):
                    for b in range(NB):
                        dve.wait_ge(out_done[g], NB * it + b + 1)
                        nc.vector.tensor_tensor(core.xres[:, b, :], o_p[b % 2][:].rearrange("p a c -> p (a c)"),
                                                core.xres[:, b, :], ALU.add).then_inc(added[g], 1)

                split_us(0, 0)
                weigh(0, 0)
                split_us(0, 2)
                @rounds(dve, bodies - 1)
                def _(it):
                    weigh(it, 2)
                    split_us(it, 4)
                    add(it, 0)
                    weigh(it, 4)
                    split_us(it, 6)
                    add(it, 1)
                weigh(bodies - 1, 2)
                add(bodies - 1, 0)
                add(bodies - 1, 1)

            @block.tensor
            def _(pe):
                def with_u(it, k):
                    for t in range(k, k + GT):
                        reached(pe, u_lo, it, t)
                        reached(pe, gelu_done, it, t, 2)
                        for half in range(2):
                            for kd in range(KD):
                                for a, c in PASSES:
                                    last = nc.tensor.matmul(a_p[t % 2][:, half, :], u_part[t % 2][a][:, kd, :],
                                                            hT[c][:, kd, half * HALF:(half + 1) * HALF],
                                                            start=(kd == 0 and (a, c) == PASSES[0]),
                                                            stop=(kd == KD - 1 and (a, c) == PASSES[-1]))
                        last.then_inc(h_done[t % BT], 1)

                def with_v(it, g):
                    tiles = range(g * GT, g * GT + GT)
                    for t in tiles:
                        reached(pe, w_lo, it, t)
                        reached(pe, v_lo, it, t)
                    for b in range(NB):
                        if b >= 2:
                            pe.wait_ge(added[g], NB * it + b - 1)
                        elif g:
                            pe.wait_ge(added[0], NB * it + NB - 1 + b)
                        elif not (isinstance(it, int) and it == 0):
                            pe.wait_ge(added[1], NB * (it - 1) + NB - 1 + b)
                        for t in tiles:
                            for a in range(2):
                                for c in range(2 - a):
                                    for half in range(2):
                                        last = nc.tensor.matmul(
                                            o_p[b % 2][:, half, :], w_part[t][a][:, b * P:(b + 1) * P],
                                            v_part[t][c][:, half * HALF:(half + 1) * HALF],
                                            start=(t == tiles[0] and a == 0 and c == 0),
                                            stop=(t == tiles[-1] and a == 1))
                        last.then_inc(out_done[g], 1)

                with_u(0, 0)
                with_u(0, 2)
                with_v(0, 0)
                with_u(0, 4)
                with_v(0, 1)
                with pe.Fori(1, bodies - 1) as it:
                    with_u(it, 2)
                    with_v(it, 0)
                    with_u(it, 4)
                    with_v(it, 1)
                with_u(bodies - 1, 2)
                with_v(bodies - 1, 0)
                with_v(bodies - 1, 1)


def embedding_stage(core, hT, w_gate, pT, w_proj):
    nc = core.nc
    with ExitStack() as sc:
        s, p = core.sb(sc), core.ps(sc)
        gate_done = core.sems("l_gate_done", 2)
        W = Weights(core, sc, "l", CW, gate_done, NB)
        p_raw, w_raw = s("l_praw", [P, KP, SEQ]), s("l_wraw", [P, KP, D])
        p_part = [s(f"l_p{n}", [P, KP, SEQ], F32R) for n in ("hi", "lo")]
        w_part = [s(f"l_wp{n}", [P, KP, D], F32R) for n in ("hi", "lo")]
        gate = [s(f"l_gate{i}", [P, CW]) for i in range(2)]
        gate_p = [p(f"l_gp{r}", [P, HALF]) for r in range(4)]
        proj_p = [p(f"l_pp{r}", [P, HALF]) for r in range(4)]
        small_in, small_hi, small_lo, chain = (core.sem(f"l_{n}") for n in ("small_in", "small_hi", "small_lo", "chain"))
        proj_done, opened, added = (core.sems(f"l_{n}", 2) for n in ("proj_done", "opened", "added"))
        pairs = D // CW // 2
        w_v = w_gate.rearrange("(k p) c -> p k c", p=P)
        with nc.Block() as block:
            @block.sync
            def _(sp):
                sp.dma_start(p_raw[:], pT).then_inc(small_in, 16)
                sp.dma_start(w_raw[:], w_proj).then_inc(small_in, 16)
                for it in range(pairs):
                    for u in range(2):
                        W.load(sp, u, it, w_v[:, :, (it * 2 + u) * CW:(it * 2 + u + 1) * CW])

            @block.scalar
            def _(act):
                act.wait_ge(small_in, 32)
                nc.scalar.activation(p_part[0][:], p_raw[:], ACT.Copy).then_inc(small_hi, 1)
                nc.scalar.activation(w_part[0][:], w_raw[:], ACT.Copy).then_inc(small_hi, 1)

                def open_gates(u, n):
                    for b in range(NB):
                        act.wait_ge(gate_done[u], NB * n + b + 1)
                        if b >= 2:
                            act.wait_ge(added[u], NB * n + b - 1)
                        elif u:
                            act.wait_ge(added[0], NB * n + NB - 1 + b)
                        elif n:
                            act.wait_ge(added[1], NB * (n - 1) + NB - 1 + b)
                        nc.scalar.activation(gate[b % 2][:], gate_p[b % 4][:, 0:CW], ACT.Sigmoid)\
                            .then_inc(opened[u], 1)

                for u in range(2):
                    W.hi(act, u, 0)
                for it in range(pairs):
                    for u in range(2):
                        open_gates(u, it)
                        if it + 1 < pairs:
                            W.hi(act, u, it + 1)

            @block.vector
            def _(dve):
                dve.wait_ge(small_hi, 2)
                for part, raw in ((p_part, p_raw), (w_part, w_raw)):
                    nc.vector.tensor_tensor(part[1][:], raw[:], part[0][:].bitcast(F32), ALU.subtract)\
                        .then_inc(small_lo, 1)
                steps = Steps(dve, chain)

                def add(u, n):
                    for b in range(NB):
                        dve.wait_ge(opened[u], NB * n + b + 1)
                        dve.wait_ge(proj_done[u], NB * n + b + 1)
                        steps(nc.vector.tensor_tensor(gate[b % 2][:], proj_p[b % 4][:, 0:CW], gate[b % 2][:], ALU.mult))
                        cols = core.xres[:, b, (n * 2 + u) * CW:(n * 2 + u + 1) * CW]
                        nc.vector.tensor_tensor(cols, cols, gate[b % 2][:], ALU.add).then_inc(added[u], 1)

                for u in range(2):
                    W.lo(dve, u, 0)
                for it in range(pairs):
                    for u in range(2):
                        add(u, it)
                        if it + 1 < pairs:
                            W.lo(dve, u, it + 1)

            @block.tensor
            def _(pe):
                pe.wait_ge(small_lo, 2)
                for it in range(pairs):
                    for u in range(2):
                        pe.wait_ge(W.lo_done[u], it + 1)
                        for b in range(NB):
                            if b >= 4:
                                pe.wait_ge(added[u], NB * it + b - 3)
                            elif u:
                                pe.wait_ge(added[0], NB * it + NB - 3 + b)
                            elif it:
                                pe.wait_ge(added[1], NB * (it - 1) + NB - 3 + b)
                            product_N(nc, W.part[u], hT, b, gate_p[b % 4][:, 0:CW]).then_inc(gate_done[u], 1)
                            at = (it * 2 + u) * CW
                            part = [w[:, :, at:at + CW] for w in w_part]
                            product_N(nc, part, p_part, b, proj_p[b % 4][:, 0:CW], KP).then_inc(proj_done[u], 1)


def layer(nc, x, pT, positions, w_t, w_n, w_up, b_up, g_mix, g_peer, g_ple, g_final, g_gla, w_out,
          w_q, keysT, uT, v_tab, w_gate, w_proj, ident, tri, rev, rot, freq, logmult, out):
    with ExitStack() as top:
        core = Core(nc, top)
        with ExitStack() as sc:
            hT = core.hT_pair(sc, "h1T")
            norm_stage(core, "n1", g_mix, hT=hT, x=x, ident=ident)
            in_projection_T(core, hT, w_t)
            in_projection_N(core, hT, w_n)
        with ExitStack() as sc:
            cat = core.sb(sc)("cat", [P, NB, D])
            gla_stage(core, cat, w_up, b_up, g_gla, tri, rev)
            attention_stage(core, cat, positions, rot, freq, logmult)
            out_projection(core, cat, w_out)
        core.recycle()
        with ExitStack() as sc:
            hT = core.hT_pair(sc, "h2T")
            norm_stage(core, "n2", g_peer, hT=hT)
            with ExitStack() as inner:
                sb = core.sb(inner)
                top_v, top_i = sb("top_v", [P, NB, SIDES, TOPK]), sb("top_i", [P, NB, SIDES, TOPK])
                query_stage(core, hT, w_q, keysT, top_v, top_i)
                gate_stage(core, top_v, top_i)
            core.recycle()
            expert_stage(core, hT, uT, v_tab)
            norm_stage(core, "n3", g_ple, hT=hT)
            embedding_stage(core, hT, w_gate, pT, w_proj)
        norm_stage(core, "n4", g_final, out=out)


def constants():
    import numpy as np

    s, c = np.arange(P)[:, None], np.arange(P)[None, :]
    same = s // CH == c // CH
    tri = np.where(same & (s <= c), 1 / 16, 0).astype(np.float32)
    rev = np.where(same & (s > c), 1 / 16, 0).astype(np.float32)
    rot, freq = np.zeros((P, P), np.float32), np.zeros((P, 1), np.float32)
    rotated = AD // 4
    inv = np.float32(500000.0) ** (-np.arange(0, rotated, 2, dtype=np.float32) / np.float32(rotated))
    for head in range(0, P, AD):
        for i in range(rotated // 2):
            rot[head + rotated // 2 + i, head + i] = -1.0
            rot[head + i, head + rotated // 2 + i] = 1.0
            freq[head + i] = freq[head + rotated // 2 + i] = inv[i]
    back = s + (SEQ - P) - np.arange(SEQ)[None, :]
    count = sum(((back >= 0) & (back <= w) & (back % d == 0)).astype(np.float64)
                for w, d in ((128, 1), (512, 4), (2048, 16)))
    logmult = np.where(count > 0, AD ** 0.5 * np.log(np.maximum(count, 1)), -1e30).astype(np.float32)
    return {"c_ident": np.eye(P, dtype=np.float32), "c_tri": tri, "c_rev": rev, "c_rot": rot, "c_freq": freq,
            "c_logmult": logmult}


def laid_out(inputs):
    import numpy as np

    a = {k: np.asarray(v) for k, v in inputs.items()}

    def tiles(w):
        return np.ascontiguousarray(w.reshape(KD, P, -1, P).transpose(2, 1, 0, 3))

    w = a["w_in"][0]
    cut = np.cumsum([GK, GK, GW, GW, RANK, HALF, HALF, HALF])
    q, k, v, r, ga, qb, kb, vb = (w[:, i:j] for i, j in zip([0, *cut], cut))
    code = w[:, cut[3]:cut[3] + P]
    return {
        "x": a["x"][0],
        "pT": np.ascontiguousarray(a["p"][0, 0].reshape(SEQ, KP, P).transpose(2, 1, 0)),
        "positions": a["positions"],
        "w_t": tiles(np.concatenate([q, k, qb, kb, code], axis=1)),
        "w_n": np.ascontiguousarray(np.concatenate([v, r, vb], axis=1)),
        "w_up": a["w_gla_gate_up"][0],
        "b_up": a["b_gla_gate"][0],
        "g_mix": a["g_mix"][0], "g_peer": a["g_peer"][0], "g_ple": a["g_ple"][0], "g_final": a["g_final"],
        "g_gla": a["g_gla_out"][0].reshape(GW),
        "w_out": a["w_out"][0],
        "w_q": tiles(a["w_peer_q"][0]),
        "keysT": np.ascontiguousarray(a["peer_sub_keys"][0].reshape(SIDES, KEYS, P).transpose(2, 0, 1)),
        "uT": np.ascontiguousarray(a["peer_u"][0].reshape(P, KEYS, KD, P).transpose(1, 3, 2, 0)),
        "v_tab": a["peer_v"][0],
        "w_gate": a["w_ple_gate"][0],
        "w_proj": np.ascontiguousarray(a["w_ple_proj"][0].reshape(KP, P, D).transpose(1, 0, 2)),
    }


def kernel(**inputs):
    import numpy as np
    import concourse.bacc as bacc
    from concourse.bass_utils import run_bass_kernel_spmd

    nc = bacc.Bacc("TRN2", target_bir_lowering=False, num_devices=1)
    arrays = {f"in_{k}": np.ascontiguousarray(v) for k, v in {**laid_out(inputs), **constants()}.items()}
    args = [nc.dram_tensor(k, v.shape, mybir.dt.from_np(v.dtype), kind="ExternalInput").ap()
            for k, v in arrays.items()]
    out = nc.dram_tensor("out", (SEQ, D), F32, kind="ExternalOutput").ap()
    layer(nc, *args, out)
    r = run_bass_kernel_spmd(nc, [arrays], core_ids=[0])
    return r.results[0]["out"].reshape(1, SEQ, D)
```

```python
from contextlib import ExitStack

import concourse.bass as bass
from concourse import mybir

F32 = mybir.dt.float32
F32R = mybir.dt.float32r
I32 = mybir.dt.int32
U32 = mybir.dt.uint32
ALU = mybir.AluOpType
ACT = mybir.ActivationFunctionType
AX_X = mybir.AxisListType.X

P = 128
SEQ = 1024
D = 1024
KD = D // P
NB = SEQ // P
HALF = 512
EPS = 1e-6
GH, GDK, GDV, CH = 4, 64, 128, 64
GW = GH * GDV
GK = GH * GDK
GP = GK // P
NCH = SEQ // CH
AH, AD = 8, 64
RANK = 16
KEYS = 128
PH, TOPK = 8, 16
SLOTS = PH * TOPK
SIDES = 2 * PH
PLE = 256
KP = PLE // P
NT_IN = 12
N_IN = 3 * HALF
CW = 256
TB = 64
NTB = SEQ // TB
LOWEST = -3e38
GROUP, BODY = 2, 4
PASSES = ((0, 0), (0, 1), (1, 0))


class Steps:

    def __init__(self, eng, sem):
        self.eng, self.sem, self.n, self.base = eng, sem, 0, 0

    def __call__(self, ins):
        ins.then_inc(self.sem, 1)
        self.n += 1
        self.eng.wait_ge(self.sem, self.base + self.n)


def rounds(eng, count):
    def run(body):
        body(0)
        if count == 2:
            body(1)
        elif count > 2:
            with eng.Fori(1, count) as it:
                body(it)
    return run


def wait_past(eng, sem, value):
    if not (isinstance(value, int) and value <= 0):
        eng.wait_ge(sem, value)


def hold(nc, mark):
    nc.vector.memset(mark, 0.0)


class Core:

    def __init__(self, nc, top):
        self.nc, self.held = nc, []
        sb = self.sb(top)
        self.xres = sb("xres", [P, NB, D])
        self.ident = sb("ident", [P, P])
        self.projT = nc.dram_tensor("projT", [NT_IN + 1, P, SEQ], F32).ap()
        self.projN = nc.dram_tensor("projN", [SEQ, N_IN], F32).ap()
        self.gates = nc.dram_tensor("gates_dense", [NTB, P, KEYS, TB], F32).ap()
        self.acts = nc.dram_tensor("early_acts", [KEYS * GROUP // BODY, P, SEQ], F32).ap()
        self.resting = nc.dram_tensor("resting", [P, NB, D], F32).ap()

    def sem(self, name):
        self.held.append(self.nc.alloc_semaphore(name))
        return self.held[-1]

    def kept_sems(self, name, n):
        return [self.nc.alloc_semaphore(f"{name}{i}") for i in range(n)]

    def recycle(self):
        with self.nc.Block() as block:
            @block.gpsimd
            def _(pool):
                for h in self.held:
                    pool.sem_clear(h)
        for h in self.held:
            self.nc.release_semaphore(h)
        self.held = []

    def sems(self, name, n):
        return [self.sem(f"{name}{i}") for i in range(n)]

    def sb(self, scope):
        return lambda name, shape, dt=F32: scope.enter_context(self.nc.sbuf_tensor(name, shape, dt))

    def ps(self, scope):
        return lambda name, shape: scope.enter_context(self.nc.psum_tensor(name, shape, F32))

    def hT_pair(self, scope, tag):
        s = self.sb(scope)
        return [s(f"{tag}_hi", [P, KD, SEQ], F32R), s(f"{tag}_lo", [P, KD, SEQ], F32R)]


class Weights:

    def __init__(self, core, scope, tag, width, used, per=1):
        s = core.sb(scope)
        self.nc = core.nc
        self.raw = [s(f"{tag}_raw{u}", [P, KD, width]) for u in range(2)]
        self.part = [[s(f"{tag}_w{n}{u}", [P, KD, width], F32R) for n in ("hi", "lo")] for u in range(2)]
        self.landed = core.sems(f"{tag}_w_landed", 2)
        self.hi_done = core.sems(f"{tag}_w_hi", 2)
        self.lo_done = core.sems(f"{tag}_w_lo", 2)
        self.used, self.per = used, per

    def load(self, sp, u, n, src):
        wait_past(sp, self.lo_done[u], n)
        sp.dma_start(self.raw[u][:], src).then_inc(self.landed[u], 16)

    def hi(self, act, u, n):
        act.wait_ge(self.landed[u], 16 * n + 16)
        wait_past(act, self.used[u], self.per * n)
        self.nc.scalar.activation(self.part[u][0][:], self.raw[u][:], ACT.Copy).then_inc(self.hi_done[u], 1)

    def lo(self, dve, u, n):
        dve.wait_ge(self.hi_done[u], n + 1)
        self.nc.vector.tensor_tensor(self.part[u][1][:], self.raw[u][:], self.part[u][0][:].bitcast(F32),
                                     ALU.subtract).then_inc(self.lo_done[u], 1)


def product_T(nc, W, u, hT, banks):
    for half in range(2):
        for k in range(KD):
            for a, c in PASSES:
                last = nc.tensor.matmul(banks[:, half, :], W.part[u][a][:, k, :],
                                        hT[c][:, k, half * HALF:(half + 1) * HALF],
                                        start=(k == 0 and (a, c) == PASSES[0]),
                                        stop=(k == KD - 1 and (a, c) == PASSES[-1]))
    return last


def product_N(nc, part, hT, b, out, tiles=KD):
    for k in range(tiles):
        for a, c in PASSES:
            last = nc.tensor.matmul(out, hT[a][:, k, b * P:(b + 1) * P], part[c][:, k, :],
                                    start=(k == 0 and (a, c) == PASSES[0]),
                                    stop=(k == tiles - 1 and (a, c) == PASSES[-1]))
    return last


def rstd(nc, steps, ss, v, y, t, width, var_ready, root_ready):
    steps(nc.vector.tensor_scalar(v, ss, 1.0 / width, EPS, ALU.mult, ALU.add))
    nc.vector.reciprocal(t, v).then_inc(var_ready, 1)
    steps.eng.wait_ge(root_ready, 1)
    steps(nc.vector.tensor_tensor(t, y, y, ALU.mult))
    steps(nc.vector.tensor_tensor(t, t, v, ALU.mult))
    steps(nc.vector.tensor_scalar(t, t, -0.5, 1.5, ALU.mult, ALU.add))
    steps(nc.vector.tensor_tensor(y, y, t, ALU.mult))


def norm_stage(core, tag, g_row, hT=None, x=None, ident=None, out=None):
    nc = core.nc
    with ExitStack() as sc:
        s, p = core.sb(sc), core.ps(sc)
        g_b = s(f"{tag}_g", [P, D])
        squares = s(f"{tag}_sq", [P, 2, D])
        xn = s(f"{tag}_xn", [P, 2, D])
        ss, v, y, t = (s(f"{tag}_{n}", [P, NB]) for n in ("ss", "v", "y", "t"))
        tp = [p(f"{tag}_tp{u}", [P, KD, P]) for u in range(2)]
        g_in, ident_in, x_in = core.sem(f"{tag}_g_in"), core.sem(f"{tag}_id_in"), core.sems(f"{tag}_x_in", NB) if x is not None else None
        squared, var_ready, root_ready = (core.sem(f"{tag}_{n}") for n in ("squared", "var", "root"))
        chain, xn_ready, turned = (core.sem(f"{tag}_{n}") for n in ("chain", "xn_ready", "turned"))
        hi_done, lo_done = core.sem(f"{tag}_hi_done"), core.sem(f"{tag}_lo_done")
        stored = core.sems(f"{tag}_stored", 2)
        with nc.Block() as block:
            @block.sync
            def _(sp):
                if x is not None:
                    for b in range(NB):
                        sp.dma_start(core.xres[:, b, :], x[b * P:(b + 1) * P, :]).then_inc(x_in[b], 16)
                    sp.dma_start(core.ident[:], ident).then_inc(ident_in, 16)
                sp.dma_start(g_b[:], g_row.partition_broadcast(P)).then_inc(g_in, 16)
                if out is not None:
                    for b in range(NB):
                        sp.wait_ge(xn_ready, b + 1)
                        sp.dma_start(out[b * P:(b + 1) * P, :], xn[:, b % 2, :]).then_inc(stored[b % 2], 16)
                    for u in range(2):
                        sp.wait_ge(stored[u], 16 * (NB // 2))

            @block.scalar
            def _(act):
                for b in range(NB):
                    if x is not None:
                        act.wait_ge(x_in[b], 16)
                    if b >= 2:
                        act.wait_ge(squared, b - 1)
                    nc.scalar.activation(squares[:, b % 2, :], core.xres[:, b, :], ACT.Square,
                                         accum_out=ss[:, b:b + 1]).then_inc(squared, 1)
                act.wait_ge(var_ready, 1)
                nc.scalar.activation(y[:], t[:], ACT.Sqrt).then_inc(root_ready, 1)
                if hT is not None:
                    for b in range(NB):
                        act.wait_ge(turned, b + 1)
                        nc.scalar.activation(hT[0][:, :, b * P:(b + 1) * P], tp[b % 2][:], ACT.Copy)\
                            .then_inc(hi_done, 1)

            @block.vector
            def _(dve):
                steps = Steps(dve, chain)
                dve.wait_ge(squared, NB)
                rstd(nc, steps, ss[:], v[:], y[:], t[:], D, var_ready, root_ready)
                dve.wait_ge(g_in, 16)

                def scale(b):
                    if hT is not None and b >= 2:
                        dve.wait_ge(turned, b - 1)
                    if out is not None and b >= 2:
                        dve.wait_ge(stored[b % 2], 16 * (b // 2))
                    nc.vector.scalar_tensor_tensor(out=xn[:, b % 2, :], in0=core.xres[:, b, :],
                                                   scalar=y[:, b:b + 1], in1=g_b[:],
                                                   op0=ALU.mult, op1=ALU.mult).then_inc(xn_ready, 1)

                for b in range(NB + 1):
                    if b < NB:
                        scale(b)
                    if b and hT is not None:
                        dve.wait_ge(hi_done, b)
                        cols = slice((b - 1) * P, b * P)
                        nc.vector.tensor_tensor(hT[1][:, :, cols], tp[(b - 1) % 2][:],
                                                hT[0][:, :, cols].bitcast(F32), ALU.subtract)\
                            .then_inc(lo_done, 1)

            if hT is not None:
                @block.tensor
                def _(pe):
                    if x is not None:
                        pe.wait_ge(ident_in, 16)
                    for b in range(NB):
                        pe.wait_ge(xn_ready, b + 1)
                        if b >= 2:
                            pe.wait_ge(lo_done, b - 1)
                        for k in range(KD):
                            last = nc.tensor.transpose(tp[b % 2][:, k, :], xn[:, b % 2, k * P:(k + 1) * P],
                                                       core.ident[:])
                        last.then_inc(turned, 1)


def in_projection_T(core, hT, w_t):
    nc = core.nc
    with ExitStack() as sc:
        s, p = core.sb(sc), core.ps(sc)
        tile_done = core.sems("iT_tile_done", 2)
        W = Weights(core, sc, "iT", P, tile_done)
        stage = [s(f"iT_stage{u}", [P, SEQ]) for u in range(2)]
        ps = [p(f"iT_ps{u}", [P, 2, HALF]) for u in range(2)]
        copied, stored = core.sems("iT_copied", 2), core.kept_sems("iT_stored", 2)
        pairs = NT_IN // 2
        with nc.Block() as block:
            @block.sync
            def _(sp):
                @rounds(sp, pairs)
                def _(it):
                    for u in range(2):
                        W.load(sp, u, it, w_t[it * 2 + u])
                W.load(sp, 0, pairs, w_t[NT_IN])

            @block.scalar
            def _(act):
                def evacuate(u, n):
                    act.wait_ge(tile_done[u], n + 1)
                    wait_past(act, stored[u], 16 * n)
                    nc.scalar.activation(stage[u][:], ps[u][:], ACT.Copy).then_inc(copied[u], 1)

                for u in range(2):
                    W.hi(act, u, 0)
                @rounds(act, pairs - 1)
                def _(it):
                    for u in range(2):
                        evacuate(u, it)
                        W.hi(act, u, it + 1)
                evacuate(0, pairs - 1)
                W.hi(act, 0, pairs)
                evacuate(1, pairs - 1)
                evacuate(0, pairs)

            @block.vector
            def _(dve):
                @rounds(dve, pairs)
                def _(it):
                    for u in range(2):
                        W.lo(dve, u, it)
                W.lo(dve, 0, pairs)

            @block.gpsimd
            def _(pool):
                def store(u, n, row):
                    pool.wait_ge(copied[u], n + 1)
                    pool.dma_start(core.projT[row], stage[u][:]).then_inc(stored[u], 16)

                @rounds(pool, pairs)
                def _(it):
                    for u in range(2):
                        store(u, it, it * 2 + u)
                store(0, pairs, NT_IN)
                pool.wait_ge(stored[0], 16 * (pairs + 1))
                pool.wait_ge(stored[1], 16 * pairs)

            @block.tensor
            def _(pe):
                def tile(u, n):
                    pe.wait_ge(W.lo_done[u], n + 1)
                    wait_past(pe, copied[u], n)
                    product_T(nc, W, u, hT, ps[u]).then_inc(tile_done[u], 1)

                @rounds(pe, pairs)
                def _(it):
                    for u in range(2):
                        tile(u, it)
                tile(0, pairs)


def in_projection_N(core, hT, w_n):
    nc = core.nc
    with ExitStack() as sc:
        s, p = core.sb(sc), core.ps(sc)
        block_done = core.sems("iN_block_done", 2)
        W = Weights(core, sc, "iN", CW, block_done, NB)
        stage = [s(f"iN_stage{u}", [P, NB, CW]) for u in range(2)]
        ps = [[p(f"iN_ps{u}{r}", [P, HALF]) for r in range(4)] for u in range(2)]
        copied, stored = core.sems("iN_copied", 2), core.kept_sems("iN_stored", 2)
        pairs = N_IN // CW // 2
        w_v = w_n.rearrange("(k p) c -> p k c", p=P)
        o_v = core.projN.rearrange("(b p) c -> p b c", p=P)
        with nc.Block() as block:
            @block.sync
            def _(sp):
                @rounds(sp, pairs)
                def _(it):
                    for u in range(2):
                        W.load(sp, u, it, w_v[:, :, bass.ds((it * 2 + u) * CW, CW)])

            @block.scalar
            def _(act):
                def evacuate(u, n):
                    wait_past(act, stored[u], 16 * n)
                    for b in range(NB):
                        act.wait_ge(block_done[u], NB * n + b + 1)
                        nc.scalar.activation(stage[u][:, b, :], ps[u][b % 4][:, 0:CW], ACT.Copy)\
                            .then_inc(copied[u], 1)

                for u in range(2):
                    W.hi(act, u, 0)
                @rounds(act, pairs - 1)
                def _(it):
                    for u in range(2):
                        evacuate(u, it)
                        W.hi(act, u, it + 1)
                for u in range(2):
                    evacuate(u, pairs - 1)

            @block.vector
            def _(dve):
                @rounds(dve, pairs)
                def _(it):
                    for u in range(2):
                        W.lo(dve, u, it)

            @block.gpsimd
            def _(pool):
                @rounds(pool, pairs)
                def _(it):
                    for u in range(2):
                        pool.wait_ge(copied[u], NB * it + NB)
                        pool.dma_start(o_v[:, :, bass.ds((it * 2 + u) * CW, CW)], stage[u][:])\
                            .then_inc(stored[u], 16)
                for u in range(2):
                    pool.wait_ge(stored[u], 16 * pairs)

            @block.tensor
            def _(pe):
                @rounds(pe, pairs)
                def _(it):
                    for u in range(2):
                        pe.wait_ge(W.lo_done[u], it + 1)
                        for b in range(NB):
                            wait_past(pe, copied[u], NB * it + max(b - 3, 0))
                            product_N(nc, W.part[u], hT, b, ps[u][b % 4][:, 0:CW]).then_inc(block_done[u], 1)


def gla_stage(core, cat, w_up, b_up, g_gla, tri, rev):
    nc = core.nc
    with ExitStack() as sc:
        s, p = core.sb(sc), core.ps(sc)
        qT, kT = s("g_qT", [P, GP, SEQ]), s("g_kT", [P, GP, SEQ])
        code, up = s("g_code", [RANK + 1, SEQ]), s("g_up", [RANK + 1, GK])
        v, r = s("g_v", [P, NB, GW]), s("g_r", [P, NB, GW])
        tri_s, rev_s = s("g_tri", [P, P]), s("g_rev", [P, P])
        mask = s("g_mask", [P, NB, P])
        e, la = s("g_e", [P, NB, GK]), s("g_la", [P, NB, GK])
        grow, shrink = s("g_grow", [P, GP, SEQ]), s("g_shrink", [P, GP, SEQ])
        kend = s("g_kend", [P, NB, GK])
        attn = [s(f"g_attn{u}", [P, NB, P]) for u in range(2)]
        state = s("g_state", [P, NCH, GDV])
        g_b = s("g_gb", [P, GW])
        ss, va, y, t = (s(f"g_{n}", [P, NB * GH]) for n in ("ss", "va", "y", "t"))
        pA, pB = p("g_pA", [P, NB, GK]), p("g_pB", [P, GP * SEQ])
        logT = pB[:, :].rearrange("p (h t) -> p h t", h=GP)
        kv = pA[:, :, :].rearrange("p b c -> p (b c)").rearrange("p (o n v) -> p o n v", o=2, v=GDV)
        attn_p = pB[:, 0:SEQ].rearrange("p (b c) -> p b c", c=P)
        o_p = pB[:, SEQ:2 * SEQ].rearrange("p (b c) -> p b c", c=P)
        names = ("ones code_in up_in qk_in v_in r_in tri_in mask_in gb_in z_ready e_act e_ready la_ready cum_ready "
                 "rev_ready decay_ready rev_exp kt_ready kd_ready kend_ready kv_ready state_ready attn_ready "
                 "masked zeroed o_ready o_copied silu squared var root chain").split()
        m = {n: core.sem(f"g_{n}") for n in names}
        with nc.Block() as block:
            @block.sync
            def _(sp):
                sp.wait_ge(m["ones"], 1)
                sp.dma_start(code[0:RANK, :], core.projT[NT_IN][0:RANK, :]).then_inc(m["code_in"], 16)
                sp.dma_start(up[0:RANK, :], w_up).then_inc(m["up_in"], 16)
                sp.dma_start(up[RANK:RANK + 1, :], b_up.rearrange("(a c) -> a c", a=1)).then_inc(m["up_in"], 16)
                sp.dma_start(tri_s[:], tri).then_inc(m["tri_in"], 16)
                sp.dma_start(rev_s[:], rev).then_inc(m["tri_in"], 16)
                for i in range(GP):
                    sp.dma_start(qT[:, i, :], core.projT[i]).then_inc(m["qk_in"], 16)
                    sp.dma_start(kT[:, i, :], core.projT[GP + i]).then_inc(m["qk_in"], 16)
                rows = core.projN.rearrange("(b p) c -> p b c", p=P)
                for b in range(NB):
                    sp.dma_start(mask[:, b, :], tri).then_inc(m["mask_in"], 16)
                sp.dma_start(v[:], rows[:, :, 0:GW]).then_inc(m["v_in"], 16)
                sp.dma_start(r[:], rows[:, :, GW:2 * GW]).then_inc(m["r_in"], 16)
                sp.dma_start(g_b[:], g_gla.partition_broadcast(P)).then_inc(m["gb_in"], 16)

            @block.gpsimd
            def _(pool):
                nc.gpsimd.memset(code[:], 1.0).then_inc(m["ones"], 1)
                nc.gpsimd.memset(state[:, 0, :], 0.0).then_inc(m["zeroed"], 1)
                for u in range(2):
                    nc.gpsimd.memset(attn[u][:], 0.0).then_inc(m["zeroed"], 1)

            @block.scalar
            def _(act):
                steps = Steps(act, m["e_act"])
                act.wait_ge(m["z_ready"], 1)
                steps(nc.scalar.activation(e[:], pA[:], ACT.Abs))
                steps(nc.scalar.activation(e[:], e[:], ACT.Exp, scale=-1.0))
                nc.scalar.activation(la[:], e[:], ACT.Ln, bias=1.0).then_inc(m["e_ready"], 1)
                act.wait_ge(m["cum_ready"], 1)
                nc.scalar.activation(grow[:], logT, ACT.Exp).then_inc(m["decay_ready"], 1)
                nc.scalar.activation(shrink[:], logT, ACT.Exp, scale=-1.0).then_inc(m["decay_ready"], 1)
                act.wait_ge(m["rev_ready"], 1)
                nc.scalar.activation(kend[:], pA[:], ACT.Exp).then_inc(m["rev_exp"], 1)
                act.wait_ge(m["r_in"], 16)
                nc.scalar.activation(r[:], r[:], ACT.Silu).then_inc(m["silu"], 1)
                for h in range(GH):
                    act.wait_ge(m["o_ready"], h + 1)
                    nc.scalar.activation(cat[:, :, h * GDV:(h + 1) * GDV], o_p, ACT.Copy).then_inc(m["o_copied"], 1)
                act.wait_ge(m["o_copied"], GH)
                nc.scalar.activation(v[:], cat[:, :, 0:GW], ACT.Square).then_inc(m["squared"], 1)
                act.wait_ge(m["var"], 1)
                nc.scalar.activation(y[:], t[:], ACT.Sqrt).then_inc(m["root"], 1)

            @block.vector
            def _(dve):
                steps = Steps(dve, m["chain"])
                dve.wait_ge(m["e_ready"], 1)
                nc.vector.scalar_tensor_tensor(out=la[:], in0=pA[:], scalar=0.0, in1=la[:],
                                               op0=ALU.min, op1=ALU.subtract).then_inc(m["la_ready"], 1)
                dve.wait_ge(m["qk_in"], 32 * GP)
                dve.wait_ge(m["decay_ready"], 2)
                nc.vector.scalar_tensor_tensor(out=qT[:], in0=qT[:], scalar=float(GDK) ** -0.5, in1=grow[:],
                                               op0=ALU.mult, op1=ALU.mult).then_inc(m["kd_ready"], 1)
                nc.vector.tensor_tensor(shrink[:], kT[:], shrink[:], ALU.mult).then_inc(m["kd_ready"], 1)
                dve.wait_ge(m["kt_ready"], 1)
                dve.wait_ge(m["rev_exp"], 1)
                nc.vector.tensor_tensor(kend[:], pA[:], kend[:], ALU.mult).then_inc(m["kend_ready"], 1)
                dve.wait_ge(m["zeroed"], 3)
                dve.wait_ge(m["mask_in"], 16 * NB)
                for hp in range(GP):
                    if hp:
                        dve.wait_ge(m["o_ready"], 2 * hp)
                    dve.wait_ge(m["kv_ready"], hp + 1)
                    for n in range(NCH - 1):
                        last = nc.vector.scalar_tensor_tensor(
                            out=state[:, n + 1, :], in0=state[:, n, :],
                            scalar=grow[:, hp, n * CH + CH - 1:n * CH + CH],
                            in1=kv[:, n % 2, n // 2, :], op0=ALU.mult, op1=ALU.add)
                        if n < NCH - 2:
                            steps(last)
                    last.then_inc(m["state_ready"], 1)
                    for h in (2 * hp, 2 * hp + 1):
                        dve.wait_ge(m["attn_ready"], h + 1)
                        if h >= 2:
                            dve.wait_ge(m["o_ready"], h - 1)
                        nc.vector.copy_predicated(attn[h % 2][:], mask[:].bitcast(U32), attn_p)\
                            .then_inc(m["masked"], 1)
                dve.wait_ge(m["squared"], 1)
                steps(nc.vector.tensor_reduce(ss[:], v[:].rearrange("p b (h c) -> p (b h) c", h=GH), AX_X, ALU.add))
                rstd(nc, steps, ss[:], va[:], y[:], t[:], GDV, m["var"], m["root"])
                oa = cat[:, :, 0:GW]
                dve.wait_ge(m["silu"], 1)
                dve.wait_ge(m["gb_in"], 16)
                steps(nc.vector.tensor_tensor(r[:], r[:], g_b[:].unsqueeze(1).to_broadcast([P, NB, GW]), ALU.mult))
                for b in range(NB):
                    steps(nc.vector.tensor_tensor(
                        oa[:, b, :].rearrange("p (h c) -> p h c", h=GH),
                        oa[:, b, :].rearrange("p (h c) -> p h c", h=GH),
                        y[:, b * GH:(b + 1) * GH].unsqueeze(2).to_broadcast([P, GH, GDV]), ALU.mult))
                steps(nc.vector.tensor_tensor(oa, oa, r[:], ALU.mult))

            @block.tensor
            def _(pe):
                pe.wait_ge(m["code_in"], 16)
                pe.wait_ge(m["up_in"], 32)
                for b in range(NB):
                    last = nc.tensor.matmul(pA[:, b, :], code[:, b * P:(b + 1) * P], up[:], start=True, stop=True)
                last.then_inc(m["z_ready"], 1)
                pe.wait_ge(m["la_ready"], 1)
                pe.wait_ge(m["tri_in"], 32)
                for hp in range(GP):
                    for b in range(NB):
                        last = nc.tensor.matmul(logT[:, hp, b * P:(b + 1) * P], la[:, b, hp * P:(hp + 1) * P],
                                                tri_s[:], start=True, stop=True)
                last.then_inc(m["cum_ready"], 1)
                for b in range(NB):
                    last = nc.tensor.matmul(pA[:, b, :], rev_s[:], la[:, b, :], start=True, stop=True)
                last.then_inc(m["rev_ready"], 1)
                pe.wait_ge(m["rev_exp"], 1)
                pe.wait_ge(m["qk_in"], 32 * GP)
                for b in range(NB):
                    for hp in range(GP):
                        last = nc.tensor.transpose(pA[:, b, hp * P:(hp + 1) * P], kT[:, hp, b * P:(b + 1) * P],
                                                   core.ident[:])
                last.then_inc(m["kt_ready"], 1)
                pe.wait_ge(m["kd_ready"], 2)
                pe.wait_ge(m["kend_ready"], 1)
                pe.wait_ge(m["v_in"], 16)
                for hp in range(GP):
                    if hp:
                        pe.wait_ge(m["state_ready"], hp)
                    for j in range(2):
                        h = 2 * hp + j
                        for odd in range(2):
                            for n in range(odd, NCH, 2):
                                rows = slice(odd * CH, odd * CH + CH)
                                last = nc.tensor.matmul(kv[j * GDK:(j + 1) * GDK, odd, n // 2, :],
                                                        kend[rows, n // 2, h * GDK:(h + 1) * GDK],
                                                        v[rows, n // 2, h * GDV:(h + 1) * GDV],
                                                        start=True, stop=True, skip_group_check=True)
                    last.then_inc(m["kv_ready"], 1)
                    for j in range(2):
                        h = 2 * hp + j
                        rows = slice(j * GDK, (j + 1) * GDK)
                        if h:
                            pe.wait_ge(m["masked"], h)
                        for b in range(NB):
                            cols = slice(b * P, (b + 1) * P)
                            last = nc.tensor.matmul(attn_p[:, b, :], shrink[rows, hp, cols], qT[rows, hp, cols],
                                                    start=True, stop=True)
                        last.then_inc(m["attn_ready"], 1)
                        pe.wait_ge(m["state_ready"], hp + 1)
                        pe.wait_ge(m["masked"], h + 1)
                        if h:
                            pe.wait_ge(m["o_copied"], h)
                        for b in range(NB):
                            nc.tensor.matmul(o_p[:, b, :], attn[h % 2][:, b, :], v[:, b, h * GDV:(h + 1) * GDV],
                                             start=True, stop=False, skip_group_check=True)
                            for n in (2 * b, 2 * b + 1):
                                half = slice((n % 2) * CH, (n % 2) * CH + CH)
                                last = nc.tensor.matmul(o_p[half, b, :], qT[rows, hp, n * CH:(n + 1) * CH],
                                                        state[rows, n, :], start=False, stop=(n % 2 == 1),
                                                        skip_group_check=True)
                        last.then_inc(m["o_ready"], 1)


def attention_stage(core, cat, positions, rot, freq, logmult):
    nc = core.nc
    with ExitStack() as sc:
        s, p = core.sb(sc), core.ps(sc)
        cos, sin = s("a_cos", [P, SEQ]), s("a_sin", [P, SEQ])
        work, turns = s("a_work", [P, SEQ]), s("a_turns", [P, SEQ])
        pos_i = s("a_pos", [P, SEQ], I32)
        freq_s, rot_s, bias = s("a_freq", [P, 1]), s("a_rot", [P, P]), s("a_bias", [P, SEQ])
        raw, qk = s("a_raw", [P, 2, SEQ]), s("a_qk", [P, 2, SEQ])
        vb = s("a_v", [P, NB, AH * AD])
        sc_s = [s(f"a_scores{u}", [P, SEQ]) for u in range(2)]
        pr = [s(f"a_probs{u}", [P, SEQ]) for u in range(2)]
        prT = [s(f"a_probsT{u}", [P, NB, P]) for u in range(2)]
        top, low, mark = s("a_top", [P, 2]), s("a_low", [P, 2]), s("a_mark", [P, 1])
        units = 2 * NB
        den, inv = s("a_den", [P, units]), s("a_inv", [P, units])
        s_p = [p(f"a_ps{u}", [P, 2, HALF]) for u in range(2)]
        t_p = p("a_pt", [P, NB, P])
        o_p = [p(f"a_po{u}", [P, HALF]) for u in range(2)]
        m = {n: core.sem(f"a_{n}") for n in "pos_in freq_in bias_in rot_in v_in qk_in angle_ready sin_ready rope_ps rope_ready chain last_ready".split()}
        scored, topped, lowered, exped, turned, prT_ready, mixed, o_done = (
            core.sems(f"a_{n}", 2) for n in ("scored", "topped", "lowered", "exped", "turned", "prT", "mixed", "o_done"))
        UH = units // 2
        pairs = AH // 2

        def block_of(n):
            return n // NB, n % NB

        with nc.Block() as block:
            @block.sync
            def _(sp):
                sp.dma_start(pos_i[:], positions.rearrange("a t -> (a t)").partition_broadcast(P)).then_inc(m["pos_in"], 16)
                sp.dma_start(freq_s[:], freq).then_inc(m["freq_in"], 16)
                sp.dma_start(rot_s[:], rot).then_inc(m["rot_in"], 16)
                sp.dma_start(bias[:], logmult).then_inc(m["bias_in"], 16)
                sp.dma_start(vb[:], core.projN.rearrange("(b p) c -> p b c", p=P)[:, :, 2 * GW:N_IN])\
                    .then_inc(m["v_in"], 16)
                @rounds(sp, pairs)
                def _(it):
                    wait_past(sp, m["rope_ready"], 2 * it)
                    sp.dma_start(raw[:, 0, :], core.projT[it + 2 * GP]).then_inc(m["qk_in"], 16)
                    sp.dma_start(raw[:, 1, :], core.projT[it + 2 * GP + pairs]).then_inc(m["qk_in"], 16)

            @block.vector
            def _(dve):
                steps = Steps(dve, m["chain"])
                TT, TS = nc.vector.tensor_tensor, nc.vector.tensor_scalar
                dve.wait_ge(m["pos_in"], 16)
                dve.wait_ge(m["freq_in"], 16)
                steps(nc.vector.tensor_copy(work[:], pos_i[:]))
                steps(TS(work[:], work[:], freq_s[:, 0:1], None, ALU.mult))
                steps(TS(turns[:], work[:], 0.15915494309189535, 12582912.0, ALU.mult, ALU.add))
                steps(TS(turns[:], turns[:], 12582912.0, None, ALU.subtract))
                for part in (6.28125, 1.93500518798828125e-3, 3.0199159819567529e-7):
                    steps(nc.vector.scalar_tensor_tensor(out=work[:], in0=turns[:], scalar=-part, in1=work[:],
                                                         op0=ALU.mult, op1=ALU.add))
                TS(work[:], work[:], 3.1415925, -3.1415925, ALU.min, ALU.max).then_inc(m["angle_ready"], 1)
                dve.wait_ge(m["sin_ready"], 2)
                steps(TT(cos[:], cos[:], cos[:], ALU.mult))
                steps(TS(cos[:], cos[:], -2.0, 1.0, ALU.mult, ALU.add))
                dve.wait_ge(m["bias_in"], 16)
                start = steps.n
                @rounds(dve, pairs)
                def _(it):
                    steps.base, steps.n = it * 4 + start, 0
                    dve.wait_ge(m["qk_in"], 32 * it + 32)
                    dve.wait_ge(m["rope_ps"], it + 1)
                    for i in range(2):
                        steps(TT(qk[:, i, :], raw[:, i, :], cos[:], ALU.mult))
                        steps(TT(work[:], s_p[i][:].rearrange("p a b -> p (a b)"), sin[:], ALU.mult))
                        TT(qk[:, i, :], qk[:, i, :], work[:], ALU.add).then_inc(m["rope_ready"], 1)
                        dve.wait_ge(m["rope_ready"], 2 * it + i + 1)

                    def maximum(n):
                        _, i = block_of(n)
                        u, w = n % 2, (i + 1) * P
                        dve.wait_ge(scored[u], it * UH + n // 2 + 1)
                        wait_past(dve, exped[u], it * UH + n // 2)
                        hold(nc, mark[:])
                        nc.vector.tensor_tensor_reduce(
                            out=sc_s[u][:, 0:w], in0=s_p[u][:].rearrange("p a b -> p (a b)")[:, 0:w],
                            in1=bias[:, SEQ - w:SEQ], scale=1.0, scalar=LOWEST, op0=ALU.add, op1=ALU.max,
                            accum_out=top[:, u:u + 1]).then_inc(topped[u], 1)
                        dve.wait_ge(topped[u], it * UH + n // 2 + 1)
                        TS(low[:, u:u + 1], top[:, u:u + 1], -float(AD) ** -0.5, None, ALU.mult)\
                            .then_inc(lowered[u], 1)

                    def turn(n):
                        u, w = n % 2, block_of(n)[1] + 1
                        dve.wait_ge(turned[u], it * UH + n // 2 + 1)
                        wait_past(dve, mixed[u], it * UH + n // 2)
                        nc.vector.tensor_copy(prT[u][:, 0:w, :], t_p[:, 0:w, :]).then_inc(prT_ready[u], 1)

                    def output(n):
                        j, i = block_of(n)
                        u = n % 2
                        dve.wait_ge(mixed[u], it * UH + n // 2 + 1)
                        nc.vector.reciprocal(inv[:, n:n + 1], den[:, n:n + 1]).then_inc(m["last_ready"], 1)
                        dve.wait_ge(m["last_ready"], it * units + n + 1)
                        TS(cat[:, i, bass.ds(it * 2 * AD + (GW + j * AD), AD)], o_p[u][:, 0:AD],
                           inv[:, n:n + 1], None, ALU.mult).then_inc(o_done[u], 1)

                    maximum(0)
                    for n in range(units):
                        if n + 1 < units:
                            maximum(n + 1)
                        if n % 2:
                            turn(n)
                        if n:
                            output(n - 1)
                    output(units - 1)

            @block.scalar
            def _(act):
                act.wait_ge(m["angle_ready"], 1)
                nc.scalar.activation(sin[:], work[:], ACT.Sin).then_inc(m["sin_ready"], 1)
                nc.scalar.activation(cos[:], work[:], ACT.Sin, scale=0.5).then_inc(m["sin_ready"], 1)
                @rounds(act, pairs)
                def _(it):
                    def expo(n):
                        u, w = n % 2, (block_of(n)[1] + 1) * P
                        act.wait_ge(lowered[u], it * UH + n // 2 + 1)
                        wait_past(act, turned[u], it * UH + n // 2)
                        wait_past(act, o_done[u], it * UH)
                        nc.scalar.activation(pr[u][:, 0:w], sc_s[u][:, 0:w], ACT.Exp, bias=low[:, u:u + 1],
                                             scale=float(AD) ** -0.5, accum_out=den[:, n:n + 1])\
                            .then_inc(exped[u], 1)

                    def turn(n):
                        u, w = n % 2, block_of(n)[1] + 1
                        act.wait_ge(turned[u], it * UH + n // 2 + 1)
                        wait_past(act, mixed[u], it * UH + n // 2)
                        nc.scalar.activation(prT[u][:, 0:w, :], t_p[:, 0:w, :], ACT.Copy).then_inc(prT_ready[u], 1)

                    expo(0)
                    for n in range(units):
                        if n + 1 < units:
                            expo(n + 1)
                        if n % 2 == 0:
                            turn(n)

            @block.tensor
            def _(pe):
                pe.wait_ge(m["rot_in"], 16)
                pe.wait_ge(m["v_in"], 16)
                @rounds(pe, pairs)
                def _(it):
                    pe.wait_ge(m["qk_in"], 32 * it + 32)
                    for i in range(2):
                        wait_past(pe, topped[i], it * UH)
                        for half in range(2):
                            last = nc.tensor.matmul(s_p[i][:, half, :], rot_s[:],
                                                    raw[:, i, half * HALF:(half + 1) * HALF], start=True, stop=True)
                    last.then_inc(m["rope_ps"], 1)
                    pe.wait_ge(m["rope_ready"], 2 * it + 2)

                    def score(n):
                        j, i = block_of(n)
                        u, rows = n % 2, slice(j * AD, (j + 1) * AD)
                        wait_past(pe, topped[u], it * UH + n // 2)
                        w = (i + 1) * P
                        for half in range(0, w, HALF):
                            width = min(HALF, w - half)
                            last = nc.tensor.matmul(s_p[u][:, half // HALF, 0:width], qk[rows, 0, i * P:(i + 1) * P],
                                                    qk[rows, 1, half:half + width], start=True, stop=True)
                        last.then_inc(scored[u], 1)

                    def turn(n):
                        u, w = n % 2, block_of(n)[1] + 1
                        pe.wait_ge(exped[u], it * UH + n // 2 + 1)
                        wait_past(pe, prT_ready[1 - u], it * UH + (n + 1) // 2)
                        for b in range(w):
                            last = nc.tensor.transpose(t_p[:, b, :], pr[u][:, b * P:(b + 1) * P], core.ident[:])
                        last.then_inc(turned[u], 1)

                    def mix(n):
                        j, i = block_of(n)
                        u = n % 2
                        pe.wait_ge(prT_ready[u], it * UH + n // 2 + 1)
                        wait_past(pe, o_done[u], it * UH + n // 2)
                        for b in range(i + 1):
                            last = nc.tensor.matmul(o_p[u][:, 0:AD], prT[u][:, b, :],
                                                    vb[:, b, bass.ds(it * 2 * AD + j * AD, AD)],
                                                    start=(b == 0), stop=(b == i))
                        last.then_inc(mixed[u], 1)

                    score(0)
                    for n in range(units):
                        if n + 1 < units:
                            score(n + 1)
                        turn(n)
                        if n:
                            mix(n - 1)
                    mix(units - 1)


def out_projection(core, cat, w_out):
    nc = core.nc
    with ExitStack() as sc:
        p = core.ps(sc)
        catT = core.hT_pair(sc, "catT")
        block_done = core.sems("o_block_done", 2)
        W = Weights(core, sc, "o", CW, block_done, NB)
        turned, hi_done, lo_done, added = core.sem("o_turned"), core.sem("o_hi"), core.sem("o_lo"), core.sems("o_added", 2)
        pairs = D // CW // 2
        w_v = w_out.rearrange("(k p) c -> p k c", p=P)
        with ExitStack() as inner:
            tp = [core.ps(inner)(f"o_tp{u}", [P, KD, P]) for u in range(2)]
            with nc.Block() as block:
                @block.tensor
                def _(pe):
                    for b in range(NB):
                        if b >= 2:
                            pe.wait_ge(lo_done, b - 1)
                        for k in range(KD):
                            last = nc.tensor.transpose(tp[b % 2][:, k, :], cat[:, b, k * P:(k + 1) * P], core.ident[:])
                        last.then_inc(turned, 1)

                @block.scalar
                def _(act):
                    for b in range(NB):
                        act.wait_ge(turned, b + 1)
                        nc.scalar.activation(catT[0][:, :, b * P:(b + 1) * P], tp[b % 2][:], ACT.Copy)\
                            .then_inc(hi_done, 1)

                @block.vector
                def _(dve):
                    for b in range(NB):
                        dve.wait_ge(hi_done, b + 1)
                        cols = slice(b * P, (b + 1) * P)
                        nc.vector.tensor_tensor(catT[1][:, :, cols], tp[b % 2][:],
                                                catT[0][:, :, cols].bitcast(F32), ALU.subtract).then_inc(lo_done, 1)
        ps = [[p(f"o_ps{u}{r}", [P, HALF]) for r in range(4)] for u in range(2)]
        with nc.Block() as block:
            @block.sync
            def _(sp):
                @rounds(sp, pairs)
                def _(it):
                    for u in range(2):
                        W.load(sp, u, it, w_v[:, :, bass.ds((it * 2 + u) * CW, CW)])

            @block.scalar
            def _(act):
                @rounds(act, pairs)
                def _(it):
                    for u in range(2):
                        W.hi(act, u, it)

            @block.vector
            def _(dve):
                def add(u, n):
                    for b in range(NB):
                        dve.wait_ge(block_done[u], NB * n + b + 1)
                        cols = core.xres[:, b, bass.ds((n * 2 + u) * CW, CW)]
                        nc.vector.tensor_tensor(cols, ps[u][b % 4][:, 0:CW], cols, ALU.add).then_inc(added[u], 1)

                for u in range(2):
                    W.lo(dve, u, 0)
                @rounds(dve, pairs - 1)
                def _(it):
                    for u in range(2):
                        add(u, it)
                        W.lo(dve, u, it + 1)
                for u in range(2):
                    add(u, pairs - 1)

            @block.tensor
            def _(pe):
                @rounds(pe, pairs)
                def _(it):
                    for u in range(2):
                        pe.wait_ge(W.lo_done[u], it + 1)
                        for b in range(NB):
                            wait_past(pe, added[u], NB * it + max(b - 3, 0))
                            product_N(nc, W.part[u], catT, b, ps[u][b % 4][:, 0:CW]).then_inc(block_done[u], 1)


def query_stage(core, hT, w_q, keysT, top_v, top_i):
    nc = core.nc
    with ExitStack() as sc:
        s, p = core.sb(sc), core.ps(sc)
        tile_done = core.sems("q_tile_done", 2)
        W = Weights(core, sc, "q", P, tile_done)
        keys = s("q_keys", [P, SIDES, KEYS])
        qr = [s(f"q_qr{u}", [P, SEQ]) for u in range(2)]
        scores = [s(f"q_sc{u}", [P, NB, KEYS]) for u in range(2)]
        rest = s("q_rest", [P, NB, KEYS])
        mark = s("q_mark", [P, 1])
        best, best_i = s("q_best", [P, NB, TOPK]), s("q_best_i", [P, NB, TOPK], U32)
        ps = [p(f"q_ps{u}", [P, 2, HALF]) for u in range(2)]
        sc_p = [p(f"q_scp{u}", [P, NB, KEYS]) for u in range(2)]
        keys_in, chain = core.sem("q_keys_in"), core.sem("q_chain")
        copied, scored, sc_copied, picked = (core.sems(f"q_{n}", 2) for n in ("copied", "scored", "sc_copied", "picked"))
        pairs = SIDES // 2
        with nc.Block() as block:
            @block.sync
            def _(sp):
                sp.dma_start(keys[:], keysT).then_inc(keys_in, 16)
                @rounds(sp, pairs)
                def _(it):
                    for u in range(2):
                        W.load(sp, u, it, w_q[it * 2 + u])

            @block.scalar
            def _(act):
                def evacuate(u, n):
                    act.wait_ge(tile_done[u], n + 1)
                    wait_past(act, scored[u], n)
                    nc.scalar.activation(qr[u][:], ps[u][:], ACT.Copy).then_inc(copied[u], 1)

                def copy_scores(u, n):
                    act.wait_ge(scored[u], n + 1)
                    wait_past(act, picked[u], n)
                    nc.scalar.activation(scores[u][:], sc_p[u][:], ACT.Copy).then_inc(sc_copied[u], 1)

                for u in range(2):
                    W.hi(act, u, 0)
                @rounds(act, pairs - 1)
                def _(it):
                    for u in range(2):
                        evacuate(u, it)
                        W.hi(act, u, it + 1)
                        copy_scores(u, it)
                for u in range(2):
                    evacuate(u, pairs - 1)
                    copy_scores(u, pairs - 1)

            @block.vector
            def _(dve):
                steps = Steps(dve, chain)
                PER = 10

                def pick(u, n):
                    dve.wait_ge(sc_copied[u], n + 1)
                    V, src = nc.vector, scores[u]
                    hold(nc, mark[:])
                    for b in range(NB):
                        last = V.max(best[:, b, 0:8], src[:, b, :])
                    steps(last)
                    hold(nc, mark[:])
                    for b in range(NB):
                        last = V.max_index(best_i[:, b, 0:8], best[:, b, 0:8], src[:, b, :])
                    for b in range(NB):
                        last = V.match_replace(rest[:, b, :], best[:, b, 0:8], src[:, b, :], LOWEST)
                    steps(last)
                    hold(nc, mark[:])
                    for b in range(NB):
                        last = V.max(best[:, b, 8:16], rest[:, b, :])
                    steps(last)
                    hold(nc, mark[:])
                    for b in range(NB):
                        last = V.max_index(best_i[:, b, 8:16], best[:, b, 8:16], rest[:, b, :])
                    steps(last)
                    side = bass.ds(n * 2 + u, 1)
                    steps(V.tensor_scalar(top_v[:, :, side, :].rearrange("p b a k -> p (b a) k"), best[:], 1.0, None, ALU.mult))
                    V.tensor_scalar(top_i[:, :, side, :].rearrange("p b a k -> p (b a) k"), best_i[:], 1.0, None,
                                    ALU.mult).then_inc(picked[u], 1)
                    dve.wait_ge(picked[u], n + 1)

                for u in range(2):
                    W.lo(dve, u, 0)
                @rounds(dve, pairs - 1)
                def _(it):
                    steps.base, steps.n = it * PER, 0
                    for u in range(2):
                        W.lo(dve, u, it + 1)
                        pick(u, it)
                    assert steps.n == PER
                steps.base = (pairs - 1) * PER
                steps.n = 0
                for u in range(2):
                    pick(u, pairs - 1)

            @block.tensor
            def _(pe):
                def tile(u, n):
                    pe.wait_ge(W.lo_done[u], n + 1)
                    wait_past(pe, copied[u], n)
                    product_T(nc, W, u, hT, ps[u]).then_inc(tile_done[u], 1)

                def score(u, n):
                    pe.wait_ge(copied[u], n + 1)
                    wait_past(pe, sc_copied[u], n)
                    for b in range(NB):
                        last = nc.tensor.matmul(sc_p[u][:, b, :], qr[u][:, b * P:(b + 1) * P],
                                                keys[:, bass.ds(n * 2 + u, 1), :].rearrange("p a k -> p (a k)"),
                                                start=True, stop=True)
                    last.then_inc(scored[u], 1)

                pe.wait_ge(keys_in, 16)
                tile(0, 0)
                @rounds(pe, pairs - 1)
                def _(it):
                    tile(1, it)
                    score(0, it)
                    tile(0, it + 1)
                    score(1, it)
                tile(1, pairs - 1)
                score(0, pairs - 1)
                score(1, pairs - 1)


def gate_stage(core, hT, top_v, top_i, uT):
    nc = core.nc
    with ExitStack() as sc:
        s, p = core.sb(sc), core.ps(sc)
        CN = TOPK * TOPK
        cand, rest = s("t_cand", [P, PH, CN]), s("t_rest", [P, PH, CN])
        best, pos = s("t_best", [P, PH, TOPK]), s("t_pos", [P, PH, TOPK], U32)
        part_u = s("t_part_u", [P, PH, TOPK], U32)
        part = s("t_part", [P, PH, TOPK])
        packed = s("t_packed", [P, 3, SLOTS])
        packedT = s("t_packedT", [P, 3, P])
        total, mark = s("t_total", [P, PH]), s("t_mark", [P, 1])
        iota = s("t_iota", [P, KEYS])
        iota_i = s("t_iota_i", [P, KEYS], I32)
        RQ, TQ = 2, 4
        first, second = s("t_first", [P, RQ, TQ, KEYS]), s("t_second", [P, RQ, TQ, KEYS])
        dense = [core.xres[:].rearrange("p b (j t) -> p (b j) t", t=TB), s("t_dense", [P, KEYS, TB])[:]]
        u_raw = [s(f"t_uraw{i}", [P, KD, P]) for i in range(2)]
        u_part = [[s(f"t_u{n}{i}", [P, KD, P], F32R) for n in ("hi", "lo")] for i in range(2)]
        act_s = [s(f"t_act{i}", [P, SEQ]) for i in range(2)]
        tr_p = p("t_trp", [P, HALF])
        g_p = [p(f"t_gp{r}", [P, TQ, KEYS]) for r in range(RQ)]
        a_p = [p(f"t_ap{i}", [P, 2, HALF]) for i in range(2)]
        m = {n: core.sem(f"t_{n}")
             for n in "iota_i iota chain best_ready exped packed turned unpacked x_resting".split()}
        hot, produced, copied = (core.sems(f"t_{n}", RQ) for n in ("hot", "produced", "copied"))
        stored = core.sems("t_stored", 2)
        u_in, u_hi, u_lo, h_done, gelu_done = (
            core.sems(f"t_{n}", 2) for n in ("u_in", "u_hi", "u_lo", "h_done", "gelu"))
        act_stored = core.kept_sems("t_act_stored", 2)
        ET = KEYS * GROUP // BODY // NB
        ES = ET // 2
        groups = P // TQ
        G4 = groups // RQ
        HG = groups // 2
        TS = 2 * KD
        AHEAD, LAG = 3 * TS, 6

        def steps_before(q):
            begin = AHEAD + LAG
            return begin + (ET * TS - begin) * q // groups

        def tiles_before(q):
            return range(steps_before(q - 1) // TS if q else 0, steps_before(q) // TS)

        with nc.Block() as block:
            @block.gpsimd
            def _(pool):
                def split_u(b, t):
                    pool.wait_ge(u_hi[t % 2], b * ES + t // 2 + 1)
                    nc.gpsimd.tensor_tensor(u_part[t % 2][1][:], u_raw[t % 2][:],
                                            u_part[t % 2][0][:].bitcast(F32), ALU.subtract).then_inc(u_lo[t % 2], 1)

                def store(b, t):
                    pool.wait_ge(gelu_done[t % 2], b * ES + t // 2 + 1)
                    pool.dma_start(core.acts[b * ET + t], act_s[t % 2][:]).then_inc(act_stored[t % 2], 16)

                def token_block(b, final=False):
                    def after(t):
                        if t + 2 < ET:
                            split_u(b, t + 2)
                        elif not final:
                            split_u(b + 1, t + 2 - ET)
                        store(b, t)

                    for t in range(ET):
                        after(t)

                nc.gpsimd.iota(iota_i[:], pattern=[[1, KEYS]], base=0, channel_multiplier=0).then_inc(m["iota_i"], 1)
                pool.wait_ge(m["iota_i"], 1)
                nc.gpsimd.tensor_copy(iota[:], iota_i[:]).then_inc(m["iota"], 1)
                split_u(0, 0)
                split_u(0, 1)
                rounds(pool, NB - 1)(token_block)
                token_block(NB - 1, final=True)
                for u in range(2):
                    pool.wait_ge(act_stored[u], 16 * ES * NB)

            @block.vector
            def _(dve):
                V = nc.vector
                steps = Steps(dve, m["chain"])
                dve.wait_ge(m["iota"], 1)
                PER = 17

                @rounds(dve, NB)
                def _(b):
                    steps.base, steps.n = b * PER, 0
                    tv = [top_v[:, bass.ds(b, 1), c::2, :].rearrange("p a h k -> p (a h) k") for c in range(2)]
                    ti = [top_i[:, bass.ds(b, 1), c::2, :].rearrange("p a h k -> p (a h) k") for c in range(2)]
                    wide = [P, PH, TOPK, TOPK]
                    steps(V.tensor_tensor(cand[:].rearrange("p h (i j) -> p h i j", i=TOPK),
                                          tv[0].unsqueeze(3).to_broadcast(wide), tv[1].unsqueeze(2).to_broadcast(wide),
                                          ALU.add))
                    hold(nc, mark[:])
                    for h in range(PH):
                        last = V.max(best[:, h, 0:8], cand[:, h, :])
                    steps(last)
                    hold(nc, mark[:])
                    for h in range(PH):
                        last = V.max_index(pos[:, h, 0:8], best[:, h, 0:8], cand[:, h, :])
                    for h in range(PH):
                        last = V.match_replace(rest[:, h, :], best[:, h, 0:8], cand[:, h, :], LOWEST)
                    steps(last)
                    hold(nc, mark[:])
                    for h in range(PH):
                        last = V.max(best[:, h, 8:16], rest[:, h, :])
                    steps(last)
                    hold(nc, mark[:])
                    for h in range(PH):
                        last = V.max_index(pos[:, h, 8:16], best[:, h, 8:16], rest[:, h, :])
                    steps(last)
                    wait_past(dve, m["turned"], 3 * b)
                    gate = packed[:, 0, :].rearrange("p (h k) -> p h k", h=PH)
                    V.tensor_tensor(gate, best[:], best[:, :, 0:1].to_broadcast([P, PH, TOPK]), ALU.subtract)\
                        .then_inc(m["best_ready"], 1)
                    hot4 = rest[:].rearrange("p h (i j) -> p h i j", i=TOPK)
                    for c in range(2):
                        if c == 0:
                            steps(V.tensor_scalar(part_u[:], pos[:], 4, None, ALU.logical_shift_right))
                        else:
                            steps(V.tensor_scalar(part_u[:], pos[:], TOPK - 1, None, ALU.bitwise_and))
                        steps(V.tensor_copy(part[:], part_u[:]))
                        steps(V.tensor_tensor(hot4, part[:].unsqueeze(3).to_broadcast(wide),
                                              iota[:, 0:TOPK].unsqueeze(1).unsqueeze(1).to_broadcast(wide),
                                              ALU.is_equal))
                        steps(V.tensor_tensor(hot4, hot4, ti[c].unsqueeze(2).to_broadcast(wide), ALU.mult))
                        steps(V.tensor_reduce(packed[:, 1 + c, :], rest[:].rearrange("p h (i j) -> p (h i) j", i=TOPK),
                                              AX_X, ALU.add))
                    dve.wait_ge(m["exped"], b + 1)
                    steps(V.tensor_reduce(total[:], gate, AX_X, ALU.add))
                    steps(V.reciprocal(total[:], total[:]))
                    V.tensor_tensor(gate, gate, total[:].unsqueeze(2).to_broadcast([P, PH, TOPK]), ALU.mult)\
                        .then_inc(m["packed"], 1)
                    dve.wait_ge(m["turned"], 3 * b + 3)
                    V.tensor_copy(packedT[:], tr_p[:, 0:3 * P].rearrange("p (a t) -> p a t", a=3))\
                        .then_inc(m["unpacked"], 1)
                    dve.wait_ge(m["unpacked"], b + 1)
                    for q in range(groups):
                        r = q % RQ
                        wait_past(dve, produced[r], b * G4 + q // RQ)
                        keys = packedT[:, 1, q * TQ:(q + 1) * TQ].unsqueeze(2)
                        V.tensor_tensor(first[:, r, :, :], iota[:].unsqueeze(1).to_broadcast([P, TQ, KEYS]),
                                        keys.to_broadcast([P, TQ, KEYS]), ALU.is_equal)
                        for i in range(TQ):
                            tok = q * TQ + i
                            last = V.tensor_scalar(second[:, r, i, :], iota[:], packedT[:, 2, tok:tok + 1],
                                                   packedT[:, 0, tok:tok + 1], ALU.is_equal, ALU.mult)
                        last.then_inc(hot[r], 1)
                    assert steps.n == PER, steps.n

            @block.scalar
            def _(act):
                def split_u(b, t):
                    act.wait_ge(u_in[t % 2], 16 * (b * ES + t // 2 + 1))
                    wait_past(act, h_done[t % 2], b * ES + t // 2)
                    nc.scalar.activation(u_part[t % 2][0][:], u_raw[t % 2][:], ACT.Copy).then_inc(u_hi[t % 2], 1)

                def gelu(b, t):
                    act.wait_ge(h_done[t % 2], b * ES + t // 2 + 1)
                    wait_past(act, act_stored[t % 2], 16 * (b * ES + t // 2))
                    nc.scalar.activation(act_s[t % 2][:], a_p[t % 2][:], ACT.Gelu).then_inc(gelu_done[t % 2], 1)

                def copy(b, q):
                    r, u = q % RQ, q // HG
                    if q % HG == 0:
                        wait_past(act, stored[u], 16 * b)
                    act.wait_ge(produced[r], b * G4 + q // RQ + 1)
                    at = (q % HG) * TQ
                    nc.scalar.activation(dense[u][:, :, at:at + TQ], g_p[r][:].rearrange("p t j -> p j t"),
                                         ACT.Copy).then_inc(copied[r], 1)

                def token_block(b, final=False):
                    def after(t):
                        gelu(b, t)
                        if t + 2 < ET:
                            split_u(b, t + 2)
                        elif not final:
                            split_u(b + 1, t + 2 - ET)
                        if t == 1:
                            act.wait_ge(m["best_ready"], b + 1)
                            nc.scalar.activation(packed[:, 0, :], packed[:, 0, :], ACT.Exp).then_inc(m["exped"], 1)

                    for q in range(groups):
                        for t in tiles_before(q):
                            after(t)
                        copy(b, q)
                    for t in range(steps_before(groups - 1) // TS, ET):
                        after(t)

                split_u(0, 0)
                split_u(0, 1)
                act.wait_ge(m["x_resting"], 16)
                rounds(act, NB - 1)(token_block)
                token_block(NB - 1, final=True)

            @block.sync
            def _(sp):
                def load_u(b, t):
                    wait_past(sp, u_lo[t % 2], b * ES + t // 2)
                    sp.dma_start(u_raw[t % 2][:], uT[b * (ET * BODY // GROUP) + t // GROUP * BODY + t % GROUP])\
                        .then_inc(u_in[t % 2], 16)

                def store(b, u):
                    for r in range(RQ):
                        sp.wait_ge(copied[r], b * G4 + (u + 1) * HG // RQ)
                    sp.dma_start(core.gates[b * 2 + u], dense[u]).then_inc(stored[u], 16)

                def token_block(b):
                    for t in range(ET):
                        load_u(b, t)
                        if t == 1 and not (isinstance(b, int) and b == 0):
                            store(b - 1, 1)
                    store(b, 0)

                for t in range(2):
                    load_u(0, t)
                sp.dma_start(core.resting, core.xres[:]).then_inc(m["x_resting"], 16)
                for t in range(2, ET):
                    load_u(0, t)
                store(0, 0)
                with sp.Fori(1, NB) as b:
                    token_block(b)
                store(NB - 1, 1)
                for u in range(2):
                    sp.wait_ge(stored[u], 16 * NB)

            @block.tensor
            def _(pe):
                def with_u(b, begin, end):
                    for step in range(begin, end):
                        t, at = step // TS, step % TS
                        half, kd = at // KD, at % KD
                        if at == 0:
                            pe.wait_ge(u_lo[t % 2], b * ES + t // 2 + 1)
                            wait_past(pe, gelu_done[t % 2], b * ES + t // 2)
                        for a, c in PASSES:
                            last = nc.tensor.matmul(a_p[t % 2][:, half, :], u_part[t % 2][a][:, kd, :],
                                                    hT[c][:, kd, half * HALF:(half + 1) * HALF],
                                                    start=(kd == 0 and (a, c) == PASSES[0]),
                                                    stop=(kd == KD - 1 and (a, c) == PASSES[-1]))
                        if at == TS - 1:
                            last.then_inc(h_done[t % 2], 1)

                @rounds(pe, NB)
                def _(b):
                    with_u(b, 0, AHEAD)
                    pe.wait_ge(m["packed"], b + 1)
                    for i in range(3):
                        nc.tensor.transpose(tr_p[:, i * P:(i + 1) * P], packed[:, i, :], core.ident[:])\
                            .then_inc(m["turned"], 1)
                    with_u(b, AHEAD, AHEAD + LAG)
                    for q in range(groups):
                        r = q % RQ
                        if q:
                            with_u(b, steps_before(q - 1), steps_before(q))
                        pe.wait_ge(hot[r], b * G4 + q // RQ + 1)
                        wait_past(pe, copied[r], b * G4 + q // RQ)
                        for i in range(TQ):
                            last = nc.tensor.matmul(g_p[r][:, i, :], first[:, r, i, :], second[:, r, i, :],
                                                    start=True, stop=True)
                        last.then_inc(produced[r], 1)
                    with_u(b, steps_before(groups - 1), ET * TS)


def expert_stage(core, hT, uT, v_tab):
    nc = core.nc
    bodies = KEYS // BODY
    late = range(GROUP, BODY)
    with ExitStack() as sc:
        s, p = core.sb(sc), core.ps(sc)
        u_raw, v_raw = s("e_uraw", [P, KD, P]), [s(f"e_vraw{i}", [P, D]) for i in range(GROUP)]
        u_part = {k: [s(f"e_u{n}{k}", [P, KD, P], F32R) for n in ("hi", "lo")] for k in late}
        v_part = [[s(f"e_v{n}{k}", [P, D], F32R) for n in ("hi", "lo")] for k in range(BODY)]
        w_part = [[s(f"e_w{n}{k}", [P, SEQ], F32R) for n in ("hi", "lo")] for k in range(BODY)]
        gates = s("e_gates", [P, NTB, GROUP, TB])
        act_s = [s(f"e_act{i}", [P, SEQ]) for i in range(GROUP)]
        a_p = {k: p(f"e_ap{k}", [P, 2, HALF]) for k in late}
        o_p = [p(f"e_op{i}", [P, 2, HALF]) for i in range(2)]
        x_back = core.sem("e_x_back")
        g_in, out_done, added = (core.sems(f"e_{n}", 2) for n in ("g_in", "out_done", "added"))
        u_in, act_in, u_hi, u_lo, v_in, v_hi, v_lo, h_done, gelu_done, weighed, w_hi, w_lo = (
            core.sems(f"e_{n}", BODY) for n in ("u_in", "act_in", "u_hi", "u_lo", "v_in", "v_hi", "v_lo", "h_done",
                                                "gelu", "weighed", "w_hi", "w_lo"))
        gates_v = core.gates.rearrange("t i j c -> i t j c")
        v_v = v_tab.rearrange("(i j) d -> j i d", j=KEYS)
        with nc.Block() as block:
            @block.sync
            def _(sp):
                def load_u(it, k):
                    if k == GROUP:
                        wait_past(sp, u_lo[BODY - 1], it)
                    else:
                        sp.wait_ge(u_lo[k - 1], it + 1)
                    sp.dma_start(u_raw[:], uT[it * BODY + k]).then_inc(u_in[k], 16)

                def load_v(it, k):
                    if k < GROUP:
                        wait_past(sp, v_lo[k + GROUP], it)
                    else:
                        sp.wait_ge(v_lo[k - GROUP], it + 1)
                    sp.dma_start(v_raw[k % GROUP][:], v_v[it * BODY + k]).then_inc(v_in[k], 16)

                def load_act(it, k):
                    wait_past(sp, w_lo[k + GROUP], it)
                    sp.dma_start(act_s[k][:], core.acts[it * GROUP + k]).then_inc(act_in[k], 16)

                def load_gates(it, g):
                    for k in range(GROUP):
                        if g:
                            sp.wait_ge(weighed[k], it + 1)
                        else:
                            wait_past(sp, weighed[k + GROUP], it)
                    sp.dma_start(gates[:], gates_v[:, :, bass.ds(it * BODY + g * GROUP, GROUP), :])\
                        .then_inc(g_in[g], 16)

                @rounds(sp, bodies)
                def _(it):
                    for k in late:
                        load_u(it, k)
                    for k in range(GROUP):
                        load_act(it, k)
                    load_gates(it, 0)
                    for k in range(BODY):
                        load_v(it, k)
                    load_gates(it, 1)
                    if isinstance(it, int) and it == 0:
                        sp.dma_start(core.xres[:], core.resting).then_inc(x_back, 16)

            @block.scalar
            def _(act):
                def split_u(it, k):
                    act.wait_ge(u_in[k], 16 * (it + 1))
                    wait_past(act, h_done[k], it)
                    nc.scalar.activation(u_part[k][0][:], u_raw[:], ACT.Copy).then_inc(u_hi[k], 1)

                def split_v(it, k):
                    act.wait_ge(v_in[k], 16 * (it + 1))
                    wait_past(act, out_done[k // GROUP], NB * it)
                    nc.scalar.activation(v_part[k][0][:], v_raw[k % GROUP][:], ACT.Copy).then_inc(v_hi[k], 1)

                def gelu(it, k):
                    act.wait_ge(h_done[k], it + 1)
                    act.wait_ge(w_lo[k - GROUP], it + 1)
                    nc.scalar.activation(act_s[k % GROUP][:], a_p[k][:], ACT.Gelu).then_inc(gelu_done[k], 1)

                def split_w(it, k):
                    act.wait_ge(weighed[k], it + 1)
                    wait_past(act, out_done[k // GROUP], NB * it)
                    nc.scalar.activation(w_part[k][0][:], act_s[k % GROUP][:], ACT.Copy).then_inc(w_hi[k], 1)

                @rounds(act, bodies)
                def _(it):
                    for k in late:
                        split_u(it, k)
                    for k in range(GROUP):
                        split_v(it, k)
                    for k in range(GROUP):
                        split_w(it, k)
                    for k in late:
                        split_v(it, k)
                    for k in late:
                        gelu(it, k)
                        split_w(it, k)

            @block.gpsimd
            def _(pool):
                def lo(raw, part, hi_done, lo_done, it, k):
                    pool.wait_ge(hi_done[k], it + 1)
                    nc.gpsimd.tensor_tensor(part[k][1][:], raw[:], part[k][0][:].bitcast(F32),
                                            ALU.subtract).then_inc(lo_done[k], 1)

                @rounds(pool, bodies)
                def _(it):
                    for k in late:
                        lo(u_raw, u_part, u_hi, u_lo, it, k)
                    for k in range(BODY):
                        lo(v_raw[k % GROUP], v_part, v_hi, v_lo, it, k)

            @block.vector
            def _(dve):
                def weigh(it, k):
                    dve.wait_ge(g_in[k // GROUP], 16 * (it + 1))
                    if k < GROUP:
                        dve.wait_ge(act_in[k], 16 * (it + 1))
                    else:
                        dve.wait_ge(gelu_done[k], it + 1)
                    w = act_s[k % GROUP][:].rearrange("p (t c) -> p t c", c=TB)
                    nc.vector.tensor_tensor(w, w, gates[:, :, k % GROUP, :], ALU.mult)\
                        .then_inc(weighed[k], 1)

                def lo(it, k):
                    dve.wait_ge(w_hi[k], it + 1)
                    nc.vector.tensor_tensor(w_part[k][1][:], act_s[k % GROUP][:], w_part[k][0][:].bitcast(F32),
                                            ALU.subtract).then_inc(w_lo[k], 1)

                def add(it, g, b):
                    dve.wait_ge(out_done[g], NB * it + b + 1)
                    nc.vector.tensor_tensor(core.xres[:, b, :], o_p[b % 2][:].rearrange("p a c -> p (a c)"),
                                            core.xres[:, b, :], ALU.add).then_inc(added[g], 1)

                @rounds(dve, bodies)
                def _(it):
                    for k in range(GROUP):
                        weigh(it, k)
                    for k in range(GROUP):
                        lo(it, k)
                    weigh(it, GROUP)
                    lo(it, GROUP)
                    weigh(it, GROUP + 1)
                    if isinstance(it, int) and it == 0:
                        dve.wait_ge(x_back, 16)
                    add(it, 0, 0)
                    lo(it, GROUP + 1)
                    for b in range(1, NB):
                        add(it, 0, b)
                    for b in range(NB):
                        add(it, 1, b)

            @block.tensor
            def _(pe):
                def with_u(it, k):
                    pe.wait_ge(u_lo[k], it + 1)
                    wait_past(pe, gelu_done[k], it)
                    for half in range(2):
                        for kd in range(KD):
                            for a, c in PASSES:
                                last = nc.tensor.matmul(a_p[k][:, half, :], u_part[k][a][:, kd, :],
                                                        hT[c][:, kd, half * HALF:(half + 1) * HALF],
                                                        start=(kd == 0 and (a, c) == PASSES[0]),
                                                        stop=(kd == KD - 1 and (a, c) == PASSES[-1]))
                    last.then_inc(h_done[k], 1)

                def with_v(it, g):
                    tiles = range(g * GROUP, (g + 1) * GROUP)
                    for k in tiles:
                        pe.wait_ge(w_lo[k], it + 1)
                        pe.wait_ge(v_lo[k], it + 1)
                    for b in range(NB):
                        if b >= 2:
                            pe.wait_ge(added[g], NB * it + b - 1)
                        elif g:
                            pe.wait_ge(added[0], NB * it + NB - 1 + b)
                        elif not (isinstance(it, int) and it == 0):
                            pe.wait_ge(added[1], NB * (it - 1) + NB - 1 + b)
                        for k in tiles:
                            for a in range(2):
                                for c in range(2 - a):
                                    for half in range(2):
                                        last = nc.tensor.matmul(
                                            o_p[b % 2][:, half, :], w_part[k][a][:, b * P:(b + 1) * P],
                                            v_part[k][c][:, half * HALF:(half + 1) * HALF],
                                            start=(k == tiles[0] and a == 0 and c == 0),
                                            stop=(k == tiles[-1] and a == 1))
                        last.then_inc(out_done[g], 1)

                @rounds(pe, bodies)
                def _(it):
                    for k in late:
                        with_u(it, k)
                    with_v(it, 0)
                    with_v(it, 1)


def embedding_stage(core, hT, w_gate, pT, w_proj):
    nc = core.nc
    with ExitStack() as sc:
        s, p = core.sb(sc), core.ps(sc)
        gate_done = core.sems("l_gate_done", 2)
        W = Weights(core, sc, "l", CW, gate_done, NB)
        p_raw, w_raw = s("l_praw", [P, KP, SEQ]), s("l_wraw", [P, KP, D])
        p_part = [s(f"l_p{n}", [P, KP, SEQ], F32R) for n in ("hi", "lo")]
        w_part = [s(f"l_wp{n}", [P, KP, D], F32R) for n in ("hi", "lo")]
        gate = [s(f"l_gate{i}", [P, CW]) for i in range(2)]
        gate_p = [p(f"l_gp{r}", [P, HALF]) for r in range(4)]
        proj_p = [p(f"l_pp{r}", [P, HALF]) for r in range(4)]
        small_in, small_hi, small_lo, chain = (core.sem(f"l_{n}") for n in ("small_in", "small_hi", "small_lo", "chain"))
        proj_done, opened, added = (core.sems(f"l_{n}", 2) for n in ("proj_done", "opened", "added"))
        pairs = D // CW // 2
        w_v = w_gate.rearrange("(k p) c -> p k c", p=P)
        with nc.Block() as block:
            @block.sync
            def _(sp):
                sp.dma_start(p_raw[:], pT).then_inc(small_in, 16)
                sp.dma_start(w_raw[:], w_proj).then_inc(small_in, 16)
                for it in range(pairs):
                    for u in range(2):
                        W.load(sp, u, it, w_v[:, :, (it * 2 + u) * CW:(it * 2 + u + 1) * CW])

            @block.scalar
            def _(act):
                act.wait_ge(small_in, 32)
                nc.scalar.activation(p_part[0][:], p_raw[:], ACT.Copy).then_inc(small_hi, 1)
                nc.scalar.activation(w_part[0][:], w_raw[:], ACT.Copy).then_inc(small_hi, 1)

                def open_gates(u, n):
                    for b in range(NB):
                        act.wait_ge(gate_done[u], NB * n + b + 1)
                        if b >= 2:
                            act.wait_ge(added[u], NB * n + b - 1)
                        elif u:
                            act.wait_ge(added[0], NB * n + NB - 1 + b)
                        elif n:
                            act.wait_ge(added[1], NB * (n - 1) + NB - 1 + b)
                        nc.scalar.activation(gate[b % 2][:], gate_p[b % 4][:, 0:CW], ACT.Sigmoid)\
                            .then_inc(opened[u], 1)

                for u in range(2):
                    W.hi(act, u, 0)
                for it in range(pairs):
                    for u in range(2):
                        open_gates(u, it)
                        if it + 1 < pairs:
                            W.hi(act, u, it + 1)

            @block.vector
            def _(dve):
                dve.wait_ge(small_hi, 2)
                for part, raw in ((p_part, p_raw), (w_part, w_raw)):
                    nc.vector.tensor_tensor(part[1][:], raw[:], part[0][:].bitcast(F32), ALU.subtract)\
                        .then_inc(small_lo, 1)
                steps = Steps(dve, chain)

                def add(u, n):
                    for b in range(NB):
                        dve.wait_ge(opened[u], NB * n + b + 1)
                        dve.wait_ge(proj_done[u], NB * n + b + 1)
                        steps(nc.vector.tensor_tensor(gate[b % 2][:], proj_p[b % 4][:, 0:CW], gate[b % 2][:], ALU.mult))
                        cols = core.xres[:, b, (n * 2 + u) * CW:(n * 2 + u + 1) * CW]
                        nc.vector.tensor_tensor(cols, cols, gate[b % 2][:], ALU.add).then_inc(added[u], 1)

                for u in range(2):
                    W.lo(dve, u, 0)
                for it in range(pairs):
                    for u in range(2):
                        add(u, it)
                        if it + 1 < pairs:
                            W.lo(dve, u, it + 1)

            @block.tensor
            def _(pe):
                pe.wait_ge(small_lo, 2)
                for it in range(pairs):
                    for u in range(2):
                        pe.wait_ge(W.lo_done[u], it + 1)
                        for b in range(NB):
                            if b >= 4:
                                pe.wait_ge(added[u], NB * it + b - 3)
                            elif u:
                                pe.wait_ge(added[0], NB * it + NB - 3 + b)
                            elif it:
                                pe.wait_ge(added[1], NB * (it - 1) + NB - 3 + b)
                            product_N(nc, W.part[u], hT, b, gate_p[b % 4][:, 0:CW]).then_inc(gate_done[u], 1)
                            at = (it * 2 + u) * CW
                            part = [w[:, :, at:at + CW] for w in w_part]
                            product_N(nc, part, p_part, b, proj_p[b % 4][:, 0:CW], KP).then_inc(proj_done[u], 1)


def layer(nc, x, pT, positions, w_t, w_n, w_up, b_up, g_mix, g_peer, g_ple, g_final, g_gla, w_out,
          w_q, keysT, uT, v_tab, w_gate, w_proj, ident, tri, rev, rot, freq, logmult, out):
    with ExitStack() as top:
        core = Core(nc, top)
        with ExitStack() as sc:
            hT = core.hT_pair(sc, "h1T")
            norm_stage(core, "n1", g_mix, hT=hT, x=x, ident=ident)
            in_projection_T(core, hT, w_t)
            in_projection_N(core, hT, w_n)
        with ExitStack() as sc:
            cat = core.sb(sc)("cat", [P, NB, D])
            gla_stage(core, cat, w_up, b_up, g_gla, tri, rev)
            attention_stage(core, cat, positions, rot, freq, logmult)
            out_projection(core, cat, w_out)
        core.recycle()
        with ExitStack() as sc:
            hT = core.hT_pair(sc, "h2T")
            norm_stage(core, "n2", g_peer, hT=hT)
            with ExitStack() as inner:
                sb = core.sb(inner)
                top_v, top_i = sb("top_v", [P, NB, SIDES, TOPK]), sb("top_i", [P, NB, SIDES, TOPK])
                query_stage(core, hT, w_q, keysT, top_v, top_i)
                gate_stage(core, hT, top_v, top_i, uT)
            core.recycle()
            expert_stage(core, hT, uT, v_tab)
            norm_stage(core, "n3", g_ple, hT=hT)
            embedding_stage(core, hT, w_gate, pT, w_proj)
        norm_stage(core, "n4", g_final, out=out)


def constants():
    import numpy as np

    s, c = np.arange(P)[:, None], np.arange(P)[None, :]
    same = s // CH == c // CH
    tri = np.where(same & (s <= c), 1 / 16, 0).astype(np.float32)
    rev = np.where(same & (s > c), 1 / 16, 0).astype(np.float32)
    rot, freq = np.zeros((P, P), np.float32), np.zeros((P, 1), np.float32)
    rotated = AD // 4
    inv = np.float32(500000.0) ** (-np.arange(0, rotated, 2, dtype=np.float32) / np.float32(rotated))
    for head in range(0, P, AD):
        for i in range(rotated // 2):
            rot[head + rotated // 2 + i, head + i] = -1.0
            rot[head + i, head + rotated // 2 + i] = 1.0
            freq[head + i] = freq[head + rotated // 2 + i] = inv[i]
    back = s + (SEQ - P) - np.arange(SEQ)[None, :]
    count = sum(((back >= 0) & (back <= w) & (back % d == 0)).astype(np.float64)
                for w, d in ((128, 1), (512, 4), (2048, 16)))
    logmult = np.where(count > 0, AD ** 0.5 * np.log(np.maximum(count, 1)), -1e30).astype(np.float32)
    return {"c_ident": np.eye(P, dtype=np.float32), "c_tri": tri, "c_rev": rev, "c_rot": rot, "c_freq": freq,
            "c_logmult": logmult}


def laid_out(inputs):
    import numpy as np

    a = {k: np.asarray(v) for k, v in inputs.items()}

    def tiles(w):
        return np.ascontiguousarray(w.reshape(KD, P, -1, P).transpose(2, 1, 0, 3))

    w = a["w_in"][0]
    cut = np.cumsum([GK, GK, GW, GW, RANK, HALF, HALF, HALF])
    q, k, v, r, ga, qb, kb, vb = (w[:, i:j] for i, j in zip([0, *cut], cut))
    code = w[:, cut[3]:cut[3] + P]
    return {
        "x": a["x"][0],
        "pT": np.ascontiguousarray(a["p"][0, 0].reshape(SEQ, KP, P).transpose(2, 1, 0)),
        "positions": a["positions"],
        "w_t": tiles(np.concatenate([q, k, qb, kb, code], axis=1)),
        "w_n": np.ascontiguousarray(np.concatenate([v, r, vb], axis=1)),
        "w_up": a["w_gla_gate_up"][0],
        "b_up": a["b_gla_gate"][0],
        "g_mix": a["g_mix"][0], "g_peer": a["g_peer"][0], "g_ple": a["g_ple"][0], "g_final": a["g_final"],
        "g_gla": a["g_gla_out"][0].reshape(GW),
        "w_out": a["w_out"][0],
        "w_q": tiles(a["w_peer_q"][0]),
        "keysT": np.ascontiguousarray(a["peer_sub_keys"][0].reshape(SIDES, KEYS, P).transpose(2, 0, 1)),
        "uT": np.ascontiguousarray(a["peer_u"][0].reshape(P, KEYS, KD, P).transpose(1, 3, 2, 0)),
        "v_tab": a["peer_v"][0],
        "w_gate": a["w_ple_gate"][0],
        "w_proj": np.ascontiguousarray(a["w_ple_proj"][0].reshape(KP, P, D).transpose(1, 0, 2)),
    }


def kernel(**inputs):
    import numpy as np
    import concourse.bacc as bacc
    from concourse.bass_utils import run_bass_kernel_spmd

    nc = bacc.Bacc("TRN2", target_bir_lowering=False, num_devices=1)
    arrays = {f"in_{k}": np.ascontiguousarray(v) for k, v in {**laid_out(inputs), **constants()}.items()}
    args = [nc.dram_tensor(k, v.shape, mybir.dt.from_np(v.dtype), kind="ExternalInput").ap()
            for k, v in arrays.items()]
    out = nc.dram_tensor("out", (SEQ, D), F32, kind="ExternalOutput").ap()
    layer(nc, *args, out)
    r = run_bass_kernel_spmd(nc, [arrays], core_ids=[0])
    return r.results[0]["out"].reshape(1, SEQ, D)
```

```python
from contextlib import ExitStack

import concourse.bass as bass
from concourse import mybir

F32 = mybir.dt.float32
F32R = mybir.dt.float32r
I32 = mybir.dt.int32
U32 = mybir.dt.uint32
ALU = mybir.AluOpType
ACT = mybir.ActivationFunctionType
AX_X = mybir.AxisListType.X

P = 128
SEQ = 1024
D = 1024
KD = D // P
NB = SEQ // P
HALF = 512
EPS = 1e-6
GH, GDK, GDV, CH = 4, 64, 128, 64
GW = GH * GDV
GK = GH * GDK
GP = GK // P
NCH = SEQ // CH
AH, AD = 8, 64
RANK = 16
KEYS = 128
PH, TOPK = 8, 16
SLOTS = PH * TOPK
SIDES = 2 * PH
PLE = 256
KP = PLE // P
NT_IN = 12
N_IN = 3 * HALF
CW = 256
TB = 64
NTB = SEQ // TB
LOWEST = -3e38
GROUP, BODY = 2, 4
PASSES = ((0, 0), (0, 1), (1, 0))


class Steps:

    def __init__(self, eng, sem):
        self.eng, self.sem, self.n, self.base = eng, sem, 0, 0

    def __call__(self, ins):
        ins.then_inc(self.sem, 1)
        self.n += 1
        self.eng.wait_ge(self.sem, self.base + self.n)


def rounds(eng, count):
    def run(body):
        body(0)
        if count == 2:
            body(1)
        elif count > 2:
            with eng.Fori(1, count) as it:
                body(it)
    return run


def wait_past(eng, sem, value):
    if not (isinstance(value, int) and value <= 0):
        eng.wait_ge(sem, value)


def hold(nc, mark):
    nc.vector.memset(mark, 0.0)


class Core:

    def __init__(self, nc, top):
        self.nc, self.held = nc, []
        sb = self.sb(top)
        self.xres = sb("xres", [P, NB, D])
        self.ident = sb("ident", [P, P])
        self.ss = sb("ss", [P, NB])
        self.projT = nc.dram_tensor("projT", [NT_IN + 1, P, SEQ], F32).ap()
        self.projN = nc.dram_tensor("projN", [SEQ, N_IN], F32).ap()
        self.gates = nc.dram_tensor("gates_dense", [NTB, P, KEYS, TB], F32).ap()
        self.acts = nc.dram_tensor("early_acts", [KEYS * GROUP // BODY, P, SEQ], F32).ap()
        self.resting = nc.dram_tensor("resting", [P, NB, D], F32).ap()

    def sem(self, name):
        self.held.append(self.nc.alloc_semaphore(name))
        return self.held[-1]

    def kept_sems(self, name, n):
        return [self.nc.alloc_semaphore(f"{name}{i}") for i in range(n)]

    def recycle(self):
        with self.nc.Block() as block:
            @block.gpsimd
            def _(pool):
                for h in self.held[0::5]:
                    pool.sem_clear(h)

            @block.scalar
            def _(act):
                for h in self.held[1::5]:
                    act.sem_clear(h)

            @block.vector
            def _(dve):
                for h in self.held[2::5]:
                    dve.sem_clear(h)

            @block.tensor
            def _(pe):
                for h in self.held[3::5]:
                    pe.sem_clear(h)

            @block.sync
            def _(sp):
                for h in self.held[4::5]:
                    sp.sem_clear(h)

        for h in self.held:
            self.nc.release_semaphore(h)
        self.held = []

    def sems(self, name, n):
        return [self.sem(f"{name}{i}") for i in range(n)]

    def sb(self, scope):
        return lambda name, shape, dt=F32: scope.enter_context(self.nc.sbuf_tensor(name, shape, dt))

    def ps(self, scope):
        return lambda name, shape: scope.enter_context(self.nc.psum_tensor(name, shape, F32))

    def hT_pair(self, scope, tag):
        s = self.sb(scope)
        return [s(f"{tag}_hi", [P, KD, SEQ], F32R), s(f"{tag}_lo", [P, KD, SEQ], F32R)]


class Weights:

    def __init__(self, core, scope, tag, width, src, per=1):
        s = core.sb(scope)
        self.nc = core.nc
        self.raw = [s(f"{tag}_raw{u}", [P, KD, width]) for u in range(2)]
        self.part = [[s(f"{tag}_w{n}{u}", [P, KD, width], F32R) for n in ("hi", "lo")] for u in range(2)]
        self.landed = core.sems(f"{tag}_w_landed", 2)
        self.hi_done = core.sems(f"{tag}_w_hi", 2)
        self.lo_done = core.sems(f"{tag}_w_lo", 2)
        self.used, self.per = core.sems(f"{tag}_w_used", 2), per
        self.src = src

    def load(self, sp, u, n):
        wait_past(sp, self.lo_done[u], n)
        sp.dma_start(self.raw[u][:], self.src(n * 2 + u)).then_inc(self.landed[u], 16)

    def hi(self, act, u, n):
        act.wait_ge(self.landed[u], 16 * n + 16)
        wait_past(act, self.used[u], self.per * n)
        self.nc.scalar.activation(self.part[u][0][:], self.raw[u][:], ACT.Copy).then_inc(self.hi_done[u], 1)

    def lo(self, eng, u, n):
        eng.wait_ge(self.hi_done[u], n + 1)
        eng.tensor_tensor(self.part[u][1][:], self.raw[u][:], self.part[u][0][:].bitcast(F32),
                                     ALU.subtract).then_inc(self.lo_done[u], 1)


def product_T(nc, W, u, hT, banks):
    for half in range(2):
        for k in range(KD):
            for a, c in PASSES:
                last = nc.tensor.matmul(banks[:, half, :], W.part[u][a][:, k, :],
                                        hT[c][:, k, half * HALF:(half + 1) * HALF],
                                        start=(k == 0 and (a, c) == PASSES[0]),
                                        stop=(k == KD - 1 and (a, c) == PASSES[-1]))
    return last


def product_N(nc, part, hT, b, out, tiles=KD):
    for k in range(tiles):
        for a, c in PASSES:
            last = nc.tensor.matmul(out, hT[a][:, k, b * P:(b + 1) * P], part[c][:, k, :],
                                    start=(k == 0 and (a, c) == PASSES[0]),
                                    stop=(k == tiles - 1 and (a, c) == PASSES[-1]))
    return last


def rstd(nc, steps, ss, v, y, t, width, var_ready, root_ready, turn=1):
    steps(nc.vector.tensor_scalar(v, ss, 1.0 / width, EPS, ALU.mult, ALU.add))
    nc.vector.reciprocal(t, v).then_inc(var_ready, 1)
    steps.eng.wait_ge(root_ready, turn)
    steps(nc.vector.tensor_tensor(t, y, y, ALU.mult))
    steps(nc.vector.tensor_tensor(t, t, v, ALU.mult))
    steps(nc.vector.tensor_scalar(t, t, -0.5, 1.5, ALU.mult, ALU.add))
    steps(nc.vector.tensor_tensor(y, y, t, ALU.mult))


class Squares:

    def __init__(self, core, tag, places):
        self.core, self.places, self.squared = core, places, core.sem(f"{tag}_squared")

    def __call__(self, act, b):
        n = len(self.places)
        if b >= n:
            act.wait_ge(self.squared, b - n + 1)
        self.core.nc.scalar.activation(self.places[b % n], self.core.xres[:, b, :], ACT.Square,
                                       accum_out=self.core.ss[:, b:b + 1]).then_inc(self.squared, 1)


def norm_stage(core, tag, g_row, hT, W, x=None, ident=None):
    nc = core.nc
    with ExitStack() as sc:
        s, p = core.sb(sc), core.ps(sc)
        g_b = s(f"{tag}_g", [P, D])
        xn = s(f"{tag}_xn", [P, 2, D])
        ss = core.ss
        v, y, t = (s(f"{tag}_{n}", [P, NB]) for n in ("v", "y", "t"))
        if x is not None:
            squares = s(f"{tag}_sq", [P, 2, D])
            square = Squares(core, tag, [squares[:, u, :] for u in range(2)])
        tp = [p(f"{tag}_tp{u}", [P, KD, P]) for u in range(2)]
        g_in, ident_in = core.sem(f"{tag}_g_in"), core.sem(f"{tag}_id_in")
        x_in = core.sems(f"{tag}_x_in", NB) if x is not None else None
        var_ready, root_ready = (core.sem(f"{tag}_{n}") for n in ("var", "root"))
        chain, xn_ready, turned = (core.sem(f"{tag}_{n}") for n in ("chain", "xn_ready", "turned"))
        hi_done, lo_done = core.sem(f"{tag}_hi_done"), core.sem(f"{tag}_lo_done")
        parts = ((0, NB // 2), (NB // 2, NB)) if x is not None else ((0, NB),)
        with nc.Block() as block:
            @block.gpsimd
            def _(pool):
                for u in range(2):
                    W.lo(pool, u, 0)

            @block.sync
            def _(sp):
                if x is not None:
                    for b in range(NB):
                        sp.dma_start(core.xres[:, b, :], x[b * P:(b + 1) * P, :]).then_inc(x_in[b], 16)
                    sp.dma_start(core.ident[:], ident).then_inc(ident_in, 16)
                sp.dma_start(g_b[:], g_row.partition_broadcast(P)).then_inc(g_in, 16)
                for u in range(2):
                    W.load(sp, u, 0)

            @block.scalar
            def _(act):
                def squares_of(b):
                    act.wait_ge(x_in[b], 16)
                    square(act, b)

                def root(part):
                    cols = slice(*parts[part])
                    act.wait_ge(var_ready, part + 1)
                    nc.scalar.activation(y[:, cols], t[:, cols], ACT.Sqrt).then_inc(root_ready, 1)

                def hi(b):
                    act.wait_ge(turned, b + 1)
                    nc.scalar.activation(hT[0][:, :, b * P:(b + 1) * P], tp[b % 2][:], ACT.Copy)\
                        .then_inc(hi_done, 1)

                if x is not None:
                    for b in range(NB // 2):
                        squares_of(b)
                root(0)
                for b in range(NB // 2):
                    if x is not None:
                        squares_of(NB // 2 + b)
                    hi(b)
                if x is not None:
                    root(1)
                for u in range(2):
                    W.hi(act, u, 0)
                for b in range(NB // 2, NB):
                    hi(b)

            @block.vector
            def _(dve):
                steps = Steps(dve, chain)

                def factors(part):
                    cols = slice(*parts[part])
                    if x is not None:
                        dve.wait_ge(square.squared, parts[part][1])
                    rstd(nc, steps, ss[:, cols], v[:, cols], y[:, cols], t[:, cols], D, var_ready, root_ready,
                         part + 1)

                def scale(b):
                    if b >= 2:
                        dve.wait_ge(turned, b - 1)
                    nc.vector.scalar_tensor_tensor(out=xn[:, b % 2, :], in0=core.xres[:, b, :],
                                                   scalar=y[:, b:b + 1], in1=g_b[:],
                                                   op0=ALU.mult, op1=ALU.mult).then_inc(xn_ready, 1)

                for b in range(NB + 1):
                    for part, (begin, _) in enumerate(parts):
                        if b == begin:
                            factors(part)
                    if b == 0:
                        dve.wait_ge(g_in, 16)
                    if b < NB:
                        scale(b)
                    if b:
                        dve.wait_ge(hi_done, b)
                        cols = slice((b - 1) * P, b * P)
                        nc.vector.tensor_tensor(hT[1][:, :, cols], tp[(b - 1) % 2][:],
                                                hT[0][:, :, cols].bitcast(F32), ALU.subtract)\
                            .then_inc(lo_done, 1)

            @block.tensor
            def _(pe):
                if x is not None:
                    pe.wait_ge(ident_in, 16)
                for b in range(NB):
                    pe.wait_ge(xn_ready, b + 1)
                    if b >= 2:
                        pe.wait_ge(lo_done, b - 1)
                    for k in range(KD):
                        last = nc.tensor.transpose(tp[b % 2][:, k, :], xn[:, b % 2, k * P:(k + 1) * P],
                                                   core.ident[:])
                    last.then_inc(turned, 1)


def in_projection_T(core, hT, W, W_next):
    nc = core.nc
    with ExitStack() as sc:
        s, p = core.sb(sc), core.ps(sc)
        tile_done = W.used
        stage = [s(f"iT_stage{u}", [P, SEQ]) for u in range(2)]
        ps = [p(f"iT_ps{u}", [P, 2, HALF]) for u in range(2)]
        copied, stored = core.sems("iT_copied", 2), core.kept_sems("iT_stored", 2)
        pairs = NT_IN // 2
        with nc.Block() as block:
            @block.sync
            def _(sp):
                with sp.Fori(1, pairs) as it:
                    for u in range(2):
                        W.load(sp, u, it)
                W.load(sp, 0, pairs)
                for u in range(2):
                    W_next.load(sp, u, 0)

            @block.scalar
            def _(act):
                def evacuate(u, n):
                    act.wait_ge(tile_done[u], n + 1)
                    wait_past(act, stored[u], 16 * n)
                    nc.scalar.activation(stage[u][:], ps[u][:], ACT.Copy).then_inc(copied[u], 1)

                @rounds(act, pairs - 1)
                def _(it):
                    for u in range(2):
                        evacuate(u, it)
                        W.hi(act, u, it + 1)
                for u in range(2):
                    W_next.hi(act, u, 0)
                evacuate(0, pairs - 1)
                W.hi(act, 0, pairs)
                evacuate(1, pairs - 1)
                evacuate(0, pairs)

            @block.vector
            def _(dve):
                with dve.Fori(1, pairs) as it:
                    for u in range(2):
                        W.lo(dve, u, it)
                W.lo(dve, 0, pairs)

            @block.gpsimd
            def _(pool):
                def store(u, n, row):
                    pool.wait_ge(copied[u], n + 1)
                    pool.dma_start(core.projT[row], stage[u][:]).then_inc(stored[u], 16)

                @rounds(pool, pairs)
                def _(it):
                    for u in range(2):
                        store(u, it, it * 2 + u)
                for u in range(2):
                    W_next.lo(pool, u, 0)
                store(0, pairs, NT_IN)
                pool.wait_ge(stored[0], 16 * (pairs + 1))
                pool.wait_ge(stored[1], 16 * pairs)

            @block.tensor
            def _(pe):
                def tile(u, n):
                    pe.wait_ge(W.lo_done[u], n + 1)
                    wait_past(pe, copied[u], n)
                    product_T(nc, W, u, hT, ps[u]).then_inc(tile_done[u], 1)

                @rounds(pe, pairs)
                def _(it):
                    for u in range(2):
                        tile(u, it)
                tile(0, pairs)


class Rotary:

    def __init__(self, core, scope):
        s = core.sb(scope)
        self.core, self.cos, self.sin = core, s("r_cos", [P, SEQ]), s("r_sin", [P, SEQ])
        self.inputs, self.angle_ready, self.sin_ready, self.chain = (
            core.sem(f"r_{n}") for n in ("inputs", "angle", "sin", "chain"))

    def scratch(self, scope):
        s = self.core.sb(scope)
        self.work, self.turns = s("r_work", [P, SEQ]), s("r_turns", [P, SEQ])
        self.pos, self.freq = s("r_pos", [P, SEQ], I32), s("r_freq", [P, 1])

    def load(self, sp, positions, freq):
        sp.dma_start(self.pos[:], positions.rearrange("a t -> (a t)").partition_broadcast(P)).then_inc(self.inputs, 16)
        sp.dma_start(self.freq[:], freq).then_inc(self.inputs, 16)

    def angles(self, dve):
        V, work, turns = self.core.nc.vector, self.work, self.turns
        self.steps = steps = Steps(dve, self.chain)
        dve.wait_ge(self.inputs, 32)
        steps(V.tensor_copy(work[:], self.pos[:]))
        steps(V.tensor_scalar(work[:], work[:], self.freq[:, 0:1], None, ALU.mult))
        steps(V.tensor_scalar(turns[:], work[:], 0.15915494309189535, 12582912.0, ALU.mult, ALU.add))
        steps(V.tensor_scalar(turns[:], turns[:], 12582912.0, None, ALU.subtract))
        for part in (6.28125, 1.93500518798828125e-3, 3.0199159819567529e-7):
            steps(V.scalar_tensor_tensor(out=work[:], in0=turns[:], scalar=-part, in1=work[:],
                                         op0=ALU.mult, op1=ALU.add))
        V.tensor_scalar(work[:], work[:], 3.1415925, -3.1415925, ALU.min, ALU.max).then_inc(self.angle_ready, 1)

    def sines(self, act):
        act.wait_ge(self.angle_ready, 1)
        self.core.nc.scalar.activation(self.sin[:], self.work[:], ACT.Sin).then_inc(self.sin_ready, 1)
        self.core.nc.scalar.activation(self.cos[:], self.work[:], ACT.Sin, scale=0.5).then_inc(self.sin_ready, 1)

    def cosines(self, dve):
        V, cos = self.core.nc.vector, self.cos
        dve.wait_ge(self.sin_ready, 2)
        self.steps(V.tensor_tensor(cos[:], cos[:], cos[:], ALU.mult))
        V.tensor_scalar(cos[:], cos[:], -2.0, 1.0, ALU.mult, ALU.add)


def in_projection_N(core, hT, W, rotary, positions, freq):
    nc = core.nc
    with ExitStack() as sc:
        s, p = core.sb(sc), core.ps(sc)
        rotary.scratch(sc)
        block_done = W.used
        stage = [s(f"iN_stage{u}", [P, NB, CW]) for u in range(2)]
        ps = [[p(f"iN_ps{u}{r}", [P, HALF]) for r in range(4)] for u in range(2)]
        copied, stored = core.sems("iN_copied", 2), core.kept_sems("iN_stored", 2)
        pairs = N_IN // CW // 2
        o_v = core.projN.rearrange("(b p) c -> p b c", p=P)
        with nc.Block() as block:
            @block.sync
            def _(sp):
                rotary.load(sp, positions, freq)
                with sp.Fori(1, pairs) as it:
                    for u in range(2):
                        W.load(sp, u, it)

            @block.scalar
            def _(act):
                def evacuate(u, n):
                    wait_past(act, stored[u], 16 * n)
                    for b in range(NB):
                        act.wait_ge(block_done[u], NB * n + b + 1)
                        nc.scalar.activation(stage[u][:, b, :], ps[u][b % 4][:, 0:CW], ACT.Copy)\
                            .then_inc(copied[u], 1)

                @rounds(act, pairs - 1)
                def _(it):
                    for u in range(2):
                        evacuate(u, it)
                        W.hi(act, u, it + 1)
                evacuate(0, pairs - 1)
                rotary.sines(act)
                evacuate(1, pairs - 1)

            @block.vector
            def _(dve):
                rotary.angles(dve)
                with dve.Fori(1, pairs) as it:
                    for u in range(2):
                        W.lo(dve, u, it)
                rotary.cosines(dve)

            @block.gpsimd
            def _(pool):
                @rounds(pool, pairs)
                def _(it):
                    for u in range(2):
                        pool.wait_ge(copied[u], NB * it + NB)
                        pool.dma_start(o_v[:, :, bass.ds((it * 2 + u) * CW, CW)], stage[u][:])\
                            .then_inc(stored[u], 16)
                for u in range(2):
                    pool.wait_ge(stored[u], 16 * pairs)

            @block.tensor
            def _(pe):
                @rounds(pe, pairs)
                def _(it):
                    for u in range(2):
                        pe.wait_ge(W.lo_done[u], it + 1)
                        for b in range(NB):
                            wait_past(pe, copied[u], NB * it + max(b - 3, 0))
                            product_N(nc, W.part[u], hT, b, ps[u][b % 4][:, 0:CW]).then_inc(block_done[u], 1)


def gla_stage(core, cat, opened, scale, w_up, b_up, g_gla, tri, rev):
    nc = core.nc
    with ExitStack() as sc:
        s, p = core.sb(sc), core.ps(sc)
        qT, kT = s("g_qT", [P, GP, SEQ]), s("g_kT", [P, GP, SEQ])
        code, up = s("g_code", [RANK + 1, SEQ]), s("g_up", [RANK + 1, GK])
        v, r, y = s("g_v", [P, NB, GW]), opened, scale
        tri_s, rev_s = s("g_tri", [P, P]), s("g_rev", [P, P])
        mask = s("g_mask", [P, NB, P])
        e, la = s("g_e", [P, NB, GK]), s("g_la", [P, NB, GK])
        grow, shrink = s("g_grow", [P, GP, SEQ]), s("g_shrink", [P, GP, SEQ])
        rev_decay = e
        q_pad, k_pad = s("g_qpad", [P, 2, GP, SEQ]), s("g_kpad", [P, 2, NB, GK])
        attn = [s(f"g_attn{u}", [P, NB, P]) for u in range(2)]
        state = qT[:].rearrange("p i (n v) -> p (i n) v", v=GDV)
        g_b = s("g_gb", [P, GW])
        ss, va, t = (s(f"g_{n}", [P, NB * GH]) for n in ("ss", "va", "t"))
        pA, pB = p("g_pA", [P, NB, GK]), p("g_pB", [P, GP * SEQ])
        logT = pB[:, :].rearrange("p (h t) -> p h t", h=GP)
        kv = pA[:, :, :].rearrange("p b c -> p (b c)").rearrange("p (o n v) -> p o n v", o=2, v=GDV)
        attn_p = pB[:, 0:SEQ].rearrange("p (b c) -> p b c", c=P)
        o_p = pB[:, SEQ:2 * SEQ].rearrange("p (b c) -> p b c", c=P)
        names = ("ones code_in up_in qk_in v_in r_in tri_in mask_in gb_in z_ready e_act e_ready la_ready cum_ready "
                 "rev_ready decay_ready rev_exp kt_ready kd_ready kend_ready kv_ready state_ready attn_ready "
                 "masked zeroed padded o_ready o_copied silu squared var root chain").split()
        m = {n: core.sem(f"g_{n}") for n in names}
        with nc.Block() as block:
            @block.sync
            def _(sp):
                sp.dma_start(up[0:RANK, :], w_up).then_inc(m["up_in"], 16)
                sp.dma_start(up[RANK:RANK + 1, :], b_up.rearrange("(a c) -> a c", a=1)).then_inc(m["up_in"], 16)
                sp.wait_ge(m["ones"], 1)
                sp.dma_start(code[0:RANK, :], core.projT[NT_IN][0:RANK, :]).then_inc(m["code_in"], 16)
                sp.dma_start(tri_s[:], tri).then_inc(m["tri_in"], 16)
                sp.dma_start(rev_s[:], rev).then_inc(m["tri_in"], 16)
                for i in range(GP):
                    sp.dma_start(qT[:, i, :], core.projT[i]).then_inc(m["qk_in"], 16)
                    sp.dma_start(kT[:, i, :], core.projT[GP + i]).then_inc(m["qk_in"], 16)
                rows = core.projN.rearrange("(b p) c -> p b c", p=P)
                for b in range(NB):
                    sp.dma_start(mask[:, b, :], tri).then_inc(m["mask_in"], 16)
                sp.dma_start(v[:], rows[:, :, 0:GW]).then_inc(m["v_in"], 16)
                sp.dma_start(r[:], rows[:, :, GW:2 * GW]).then_inc(m["r_in"], 16)
                sp.dma_start(g_b[:], g_gla.partition_broadcast(P)).then_inc(m["gb_in"], 16)

            @block.gpsimd
            def _(pool):
                nc.gpsimd.memset(code[:], 1.0).then_inc(m["ones"], 1)
                nc.gpsimd.memset(q_pad[:], 0.0).then_inc(m["padded"], 1)
                nc.gpsimd.memset(k_pad[:], 0.0).then_inc(m["padded"], 1)
                for u in range(2):
                    nc.gpsimd.memset(attn[u][:], 0.0).then_inc(m["zeroed"], 1)
                pool.wait_ge(m["kd_ready"], 2)
                nc.gpsimd.memset(state[:, 0, :], 0.0).then_inc(m["zeroed"], 1)

            @block.scalar
            def _(act):
                steps = Steps(act, m["e_act"])
                act.wait_ge(m["z_ready"], 1)
                steps(nc.scalar.activation(e[:], pA[:], ACT.Abs))
                steps(nc.scalar.activation(e[:], e[:], ACT.Exp, scale=-1.0))
                nc.scalar.activation(la[:], e[:], ACT.Ln, bias=1.0).then_inc(m["e_ready"], 1)
                act.wait_ge(m["cum_ready"], 1)
                nc.scalar.activation(grow[:], logT, ACT.Exp).then_inc(m["decay_ready"], 1)
                nc.scalar.activation(shrink[:], logT, ACT.Exp, scale=-1.0).then_inc(m["decay_ready"], 1)
                act.wait_ge(m["rev_ready"], 1)
                nc.scalar.activation(rev_decay[:], pA[:], ACT.Exp).then_inc(m["rev_exp"], 1)
                act.wait_ge(m["r_in"], 16)
                nc.scalar.activation(r[:], r[:], ACT.Silu).then_inc(m["silu"], 1)
                for h in range(GH):
                    act.wait_ge(m["o_ready"], h + 1)
                    cols = slice(h * GDV, (h + 1) * GDV)
                    nc.scalar.activation(cat[:, :, cols], o_p, ACT.Copy).then_inc(m["o_copied"], 1)
                    act.wait_ge(m["o_copied"], h + 1)
                    nc.scalar.activation(v[:, :, cols], cat[:, :, cols], ACT.Square).then_inc(m["squared"], 1)
                act.wait_ge(m["var"], 1)
                nc.scalar.activation(y[:], t[:], ACT.Sqrt).then_inc(m["root"], 1)

            @block.vector
            def _(dve):
                steps = Steps(dve, m["chain"])
                dve.wait_ge(m["e_ready"], 1)
                nc.vector.scalar_tensor_tensor(out=la[:], in0=pA[:], scalar=0.0, in1=la[:],
                                               op0=ALU.min, op1=ALU.subtract).then_inc(m["la_ready"], 1)
                dve.wait_ge(m["qk_in"], 32 * GP)
                dve.wait_ge(m["decay_ready"], 2)
                dve.wait_ge(m["padded"], 2)
                for j in range(2):
                    rows = slice(j * GDK, (j + 1) * GDK)
                    nc.vector.scalar_tensor_tensor(out=q_pad[rows, j, :, :], in0=qT[rows], scalar=float(GDK) ** -0.5,
                                                   in1=grow[rows], op0=ALU.mult, op1=ALU.mult)\
                        .then_inc(m["kd_ready"], 1)
                nc.vector.tensor_tensor(shrink[:], kT[:], shrink[:], ALU.mult).then_inc(m["kd_ready"], 1)
                dve.wait_ge(m["kt_ready"], 1)
                dve.wait_ge(m["rev_exp"], 1)
                for odd in range(2):
                    rows = slice(odd * CH, odd * CH + CH)
                    nc.vector.tensor_tensor(k_pad[rows, odd, :, :], pA[rows], rev_decay[rows], ALU.mult)\
                        .then_inc(m["kend_ready"], 1)
                dve.wait_ge(m["silu"], 1)
                dve.wait_ge(m["gb_in"], 16)
                nc.vector.tensor_tensor(r[:], r[:], g_b[:].unsqueeze(1).to_broadcast([P, NB, GW]), ALU.mult)
                dve.wait_ge(m["zeroed"], 3)
                dve.wait_ge(m["mask_in"], 16 * NB)
                for hp in range(GP):
                    if hp:
                        dve.wait_ge(m["o_ready"], 2 * hp)
                    dve.wait_ge(m["kv_ready"], hp + 1)
                    for n in range(NCH - 1):
                        last = nc.vector.scalar_tensor_tensor(
                            out=state[:, n + 1, :], in0=state[:, n, :],
                            scalar=grow[:, hp, n * CH + CH - 1:n * CH + CH],
                            in1=kv[:, n % 2, n // 2, :], op0=ALU.mult, op1=ALU.add)
                        if n < NCH - 2:
                            steps(last)
                    last.then_inc(m["state_ready"], 1)
                    for h in (2 * hp, 2 * hp + 1):
                        dve.wait_ge(m["attn_ready"], h + 1)
                        if h >= 2:
                            dve.wait_ge(m["o_ready"], h - 1)
                        nc.vector.copy_predicated(attn[h % 2][:], mask[:].bitcast(U32), attn_p)\
                            .then_inc(m["masked"], 1)
                for h in range(GH):
                    dve.wait_ge(m["squared"], h + 1)
                    last = nc.vector.tensor_reduce(ss[:].rearrange("p (b h) -> p b h", h=GH)[:, :, h:h + 1],
                                                   v[:, :, h * GDV:(h + 1) * GDV], AX_X, ALU.add)
                steps(last)
                rstd(nc, steps, ss[:], va[:], y[:], t[:], GDV, m["var"], m["root"])

            @block.tensor
            def _(pe):
                pe.wait_ge(m["code_in"], 16)
                pe.wait_ge(m["up_in"], 32)
                for b in range(NB):
                    last = nc.tensor.matmul(pA[:, b, :], code[:, b * P:(b + 1) * P], up[:], start=True, stop=True)
                last.then_inc(m["z_ready"], 1)
                pe.wait_ge(m["la_ready"], 1)
                pe.wait_ge(m["tri_in"], 32)
                for hp in range(GP):
                    for b in range(NB):
                        last = nc.tensor.matmul(logT[:, hp, b * P:(b + 1) * P], la[:, b, hp * P:(hp + 1) * P],
                                                tri_s[:], start=True, stop=True)
                last.then_inc(m["cum_ready"], 1)
                for b in range(NB):
                    last = nc.tensor.matmul(pA[:, b, :], rev_s[:], la[:, b, :], start=True, stop=True)
                last.then_inc(m["rev_ready"], 1)
                pe.wait_ge(m["rev_exp"], 1)
                pe.wait_ge(m["qk_in"], 32 * GP)
                for b in range(NB):
                    for hp in range(GP):
                        last = nc.tensor.transpose(pA[:, b, hp * P:(hp + 1) * P], kT[:, hp, b * P:(b + 1) * P],
                                                   core.ident[:])
                last.then_inc(m["kt_ready"], 1)
                pe.wait_ge(m["kd_ready"], 3)
                pe.wait_ge(m["kend_ready"], 2)
                pe.wait_ge(m["v_in"], 16)
                for hp in range(GP):
                    if hp:
                        pe.wait_ge(m["state_ready"], hp)
                    for j in range(2):
                        h = 2 * hp + j
                        for odd in range(2):
                            for n in range(odd, NCH, 2):
                                last = nc.tensor.matmul(kv[j * GDK:(j + 1) * GDK, odd, n // 2, :],
                                                        k_pad[:, odd, n // 2, h * GDK:(h + 1) * GDK],
                                                        v[:, n // 2, h * GDV:(h + 1) * GDV],
                                                        start=True, stop=True, skip_group_check=True)
                    last.then_inc(m["kv_ready"], 1)
                    for j in range(2):
                        h = 2 * hp + j
                        if h:
                            pe.wait_ge(m["masked"], h)
                        for b in range(NB):
                            cols = slice(b * P, (b + 1) * P)
                            last = nc.tensor.matmul(attn_p[:, b, :], shrink[:, hp, cols], q_pad[:, j, hp, cols],
                                                    start=True, stop=True)
                        last.then_inc(m["attn_ready"], 1)
                        pe.wait_ge(m["state_ready"], hp + 1)
                        pe.wait_ge(m["masked"], h + 1)
                        if h:
                            pe.wait_ge(m["o_copied"], h)
                        for b in range(NB):
                            nc.tensor.matmul(o_p[:, b, :], attn[h % 2][:, b, :], v[:, b, h * GDV:(h + 1) * GDV],
                                             start=True, stop=False, skip_group_check=True)
                            for n in (2 * b, 2 * b + 1):
                                half = slice((n % 2) * CH, (n % 2) * CH + CH)
                                last = nc.tensor.matmul(o_p[half, b, :], q_pad[:, j, hp, n * CH:(n + 1) * CH],
                                                        state[:, n, :], start=False, stop=(n % 2 == 1),
                                                        skip_group_check=True)
                        last.then_inc(m["o_ready"], 1)


def attention_stage(core, cat, opened, scale, rotary, rot, logmult):
    nc = core.nc
    with ExitStack() as sc:
        s, p = core.sb(sc), core.ps(sc)
        cos, sin, work = rotary.cos, rotary.sin, s("a_work", [P, 2, SEQ])
        rot_s, bias = s("a_rot", [P, P]), s("a_bias", [P, SEQ])
        raw = s("a_raw", [P, 2, SEQ])
        q_pad, k_s = s("a_qpad", [P, 2, SEQ]), s("a_k", [P, SEQ])
        vb = s("a_v", [P, NB, AH * AD])
        sc_s = [s(f"a_scores{u}", [P, SEQ]) for u in range(2)]
        pr = [s(f"a_probs{u}", [P, SEQ]) for u in range(2)]
        prT = [s(f"a_probsT{u}", [P, NB, P]) for u in range(2)]
        top, low, mark = s("a_top", [P, 2]), s("a_low", [P, 2]), s("a_mark", [P, 1])
        units = 2 * NB
        den, inv = s("a_den", [P, units]), s("a_inv", [P, units])
        s_p = [p(f"a_ps{u}", [P, 2, HALF]) for u in range(2)]
        t_p = p("a_pt", [P, NB, P])
        o_p = [p(f"a_po{u}", [P, HALF]) for u in range(2)]
        m = {n: core.sem(f"a_{n}") for n in ("bias_in rot_in v_in qk_in padded rope_ps rope_read raw_scaled rope_ready "
                                             "last_ready scaled").split()}
        scored, topped, lowered, exped, turned, prT_ready, mixed, o_done = (
            core.sems(f"a_{n}", 2) for n in ("scored", "topped", "lowered", "exped", "turned", "prT", "mixed", "o_done"))
        UH = units // 2
        pairs = AH // 2

        ROPE = 8

        def block_of(n):
            return n % 2, NB - 1 - n // 2 if n % 2 else n // 2

        def two_on(it, n, final):
            if n + 2 < units:
                return [(it, n + 2)]
            return [] if final else [(it + 1, n + 2 - units)]

        with nc.Block() as block:
            @block.sync
            def _(sp):
                sp.dma_start(rot_s[:], rot).then_inc(m["rot_in"], 16)

                @rounds(sp, pairs)
                def _(it):
                    wait_past(sp, m["rope_ready"], 3 * it)
                    sp.dma_start(raw[:, 0, :], core.projT[it + 2 * GP]).then_inc(m["qk_in"], 16)
                    sp.dma_start(raw[:, 1, :], core.projT[it + 2 * GP + pairs]).then_inc(m["qk_in"], 16)
                    if isinstance(it, int) and it == 0:
                        sp.dma_start(bias[:], logmult).then_inc(m["bias_in"], 16)
                        sp.dma_start(vb[:], core.projN.rearrange("(b p) c -> p b c", p=P)[:, :, 2 * GW:N_IN])\
                            .then_inc(m["v_in"], 16)

            @block.vector
            def _(dve):
                TT, TS = nc.vector.tensor_tensor, nc.vector.tensor_scalar

                def rotate(it, i):
                    dve.wait_ge(m["qk_in"], 32 * it + 32)
                    dve.wait_ge(m["rope_ps"], 2 * it + i + 1)
                    TT(work[:, i, :], s_p[i][:].rearrange("p a b -> p (a b)"), sin[:], ALU.mult)\
                        .then_inc(m["rope_read"], 1)
                    TT(raw[:, i, :], raw[:, i, :], cos[:], ALU.mult).then_inc(m["raw_scaled"], 1)

                def rotated(it):
                    dve.wait_ge(m["rope_read"], 2 * it + 2)
                    dve.wait_ge(m["raw_scaled"], 2 * it + 2)
                    for j in range(2):
                        rows = slice(j * AD, (j + 1) * AD)
                        TT(q_pad[rows, j, :], raw[rows, 0, :], work[rows, 0, :], ALU.add).then_inc(m["rope_ready"], 1)
                    TT(k_s[:], raw[:, 1, :], work[:, 1, :], ALU.add).then_inc(m["rope_ready"], 1)

                def maximum(it, n):
                    _, i = block_of(n)
                    u, w = n % 2, (i + 1) * P
                    dve.wait_ge(scored[u], it * UH + n // 2 + 1)
                    wait_past(dve, exped[u], it * UH + n // 2)
                    hold(nc, mark[:])
                    nc.vector.tensor_tensor_reduce(
                        out=sc_s[u][:, 0:w], in0=s_p[u][:].rearrange("p a b -> p (a b)")[:, 0:w],
                        in1=bias[:, SEQ - w:SEQ], scale=1.0, scalar=LOWEST, op0=ALU.add, op1=ALU.max,
                        accum_out=top[:, u:u + 1]).then_inc(topped[u], 1)
                    dve.wait_ge(topped[u], it * UH + n // 2 + 1)
                    TS(low[:, u:u + 1], top[:, u:u + 1], -float(AD) ** -0.5, None, ALU.mult)\
                        .then_inc(lowered[u], 1)

                def turn(it, n):
                    u, w = n % 2, block_of(n)[1] + 1
                    dve.wait_ge(turned[u], it * UH + n // 2 + 1)
                    wait_past(dve, mixed[u], it * UH + n // 2)
                    nc.vector.tensor_copy(prT[u][:, 0:w, :], t_p[:, 0:w, :]).then_inc(prT_ready[u], 1)

                def output(it, n):
                    j, i = block_of(n)
                    u = n % 2
                    dve.wait_ge(mixed[u], it * UH + n // 2 + 1)
                    nc.vector.reciprocal(inv[:, n:n + 1], den[:, n:n + 1]).then_inc(m["last_ready"], 1)
                    dve.wait_ge(m["last_ready"], it * units + n + 1)
                    TS(cat[:, i, bass.ds(it * 2 * AD + (GW + j * AD), AD)], o_p[u][:, 0:AD],
                       inv[:, n:n + 1], None, ALU.mult).then_inc(o_done[u], 1)

                def pair(it, final=False):
                    for n in range(units):
                        if n in (ROPE, ROPE + 1) and not final:
                            rotate(it + 1, n - ROPE)
                        for unit in two_on(it, n, final):
                            maximum(*unit)
                        if n == units - 3 and not final:
                            rotated(it + 1)
                        if n % 2:
                            turn(it, n)
                        if n:
                            output(it, n - 1)
                    output(it, units - 1)

                dve.wait_ge(m["padded"], 1)
                for i in range(2):
                    rotate(0, i)
                rotated(0)
                dve.wait_ge(m["bias_in"], 16)
                for n in range(2):
                    maximum(0, n)
                rounds(dve, pairs - 1)(pair)
                pair(pairs - 1, final=True)

            @block.gpsimd
            def _(pool):
                nc.gpsimd.memset(q_pad[:], 0.0).then_inc(m["padded"], 1)
                for b in range(NB):
                    oa = cat[:, b, 0:GW]
                    nc.gpsimd.tensor_tensor(oa.rearrange("p (h c) -> p h c", h=GH),
                                            oa.rearrange("p (h c) -> p h c", h=GH),
                                            scale[:, b * GH:(b + 1) * GH].unsqueeze(2).to_broadcast([P, GH, GDV]),
                                            ALU.mult).then_inc(m["scaled"], 1)
                    pool.wait_ge(m["scaled"], b + 1)
                    nc.gpsimd.tensor_tensor(oa, oa, opened[:, b, :], ALU.mult)

            @block.scalar
            def _(act):
                def expo(it, n):
                    u, w = n % 2, (block_of(n)[1] + 1) * P
                    act.wait_ge(lowered[u], it * UH + n // 2 + 1)
                    wait_past(act, turned[u], it * UH + n // 2)
                    wait_past(act, o_done[u], (it - 1) * UH + n // 2 + 1)
                    nc.scalar.activation(pr[u][:, 0:w], sc_s[u][:, 0:w], ACT.Exp, bias=low[:, u:u + 1],
                                         scale=float(AD) ** -0.5, accum_out=den[:, n:n + 1])\
                        .then_inc(exped[u], 1)

                def turn(it, n):
                    u, w = n % 2, block_of(n)[1] + 1
                    act.wait_ge(turned[u], it * UH + n // 2 + 1)
                    wait_past(act, mixed[u], it * UH + n // 2)
                    nc.scalar.activation(prT[u][:, 0:w, :], t_p[:, 0:w, :], ACT.Copy).then_inc(prT_ready[u], 1)

                def pair(it, final=False):
                    for n in range(units):
                        if n % 2 == 0:
                            turn(it, n)
                        for unit in two_on(it, n, final):
                            expo(*unit)

                for n in range(2):
                    expo(0, n)
                rounds(act, pairs - 1)(pair)
                pair(pairs - 1, final=True)

            @block.tensor
            def _(pe):
                pe.wait_ge(m["rot_in"], 16)
                def rope(it, i):
                    pe.wait_ge(m["qk_in"], 32 * it + 32)
                    for half in range(2):
                        last = nc.tensor.matmul(s_p[i][:, half, :], rot_s[:],
                                                raw[:, i, half * HALF:(half + 1) * HALF], start=True, stop=True)
                    last.then_inc(m["rope_ps"], 1)

                def score(it, n, next_rope=False):
                    j, i = block_of(n)
                    u = n % 2
                    wait_past(pe, topped[u], it * UH + n // 2)
                    if next_rope:
                        pe.wait_ge(m["rope_read"], 2 * it + 3 + u)
                    w = (i + 1) * P
                    for half in range(0, w, HALF):
                        width = min(HALF, w - half)
                        last = nc.tensor.matmul(s_p[u][:, half // HALF, 0:width], q_pad[:, j, i * P:(i + 1) * P],
                                                k_s[:, half:half + width], start=True, stop=True)
                    last.then_inc(scored[u], 1)

                def turn(it, n):
                    u, w = n % 2, block_of(n)[1] + 1
                    pe.wait_ge(exped[u], it * UH + n // 2 + 1)
                    wait_past(pe, prT_ready[1 - u], it * UH + (n + 1) // 2)
                    for b in range(w):
                        last = nc.tensor.transpose(t_p[:, b, :], pr[u][:, b * P:(b + 1) * P], core.ident[:])
                    last.then_inc(turned[u], 1)

                def mix(it, n):
                    j, i = block_of(n)
                    u = n % 2
                    pe.wait_ge(prT_ready[u], it * UH + n // 2 + 1)
                    wait_past(pe, o_done[u], it * UH + n // 2)
                    for b in range(i + 1):
                        last = nc.tensor.matmul(o_p[u][:, 0:AD], prT[u][:, b, :],
                                                vb[:, b, bass.ds(it * 2 * AD + j * AD, AD)],
                                                start=(b == 0), stop=(b == i))
                    last.then_inc(mixed[u], 1)

                def pair(it, final=False):
                    for n in range(units):
                        if n in (ROPE, ROPE + 1) and not final:
                            pe.wait_ge(topped[n % 2], it * UH + n // 2 + 1)
                            rope(it + 1, n - ROPE)
                            turn(it, n)
                            score(it, n + 2, next_rope=True)
                        else:
                            if n == units - 2 and not final:
                                pe.wait_ge(m["rope_ready"], 3 * it + 6)
                            for unit in two_on(it, n, final):
                                score(*unit)
                            turn(it, n)
                        if n:
                            mix(it, n - 1)
                    mix(it, units - 1)

                for i in range(2):
                    rope(0, i)
                pe.wait_ge(m["rope_ready"], 3)
                for n in range(2):
                    score(0, n)
                pe.wait_ge(m["v_in"], 16)
                rounds(pe, pairs - 1)(pair)
                pair(pairs - 1, final=True)


def out_projection(core, cat, w_out):
    nc = core.nc
    with ExitStack() as sc:
        p = core.ps(sc)
        catT = core.hT_pair(sc, "catT")
        w_v = w_out.rearrange("(k p) c -> p k c", p=P)
        W = Weights(core, sc, "o", CW, lambda n: w_v[:, :, bass.ds(n * CW, CW)], NB)
        block_done = W.used
        square = Squares(core, "o", [cat[:, b, :] for b in range(NB)])
        turned, hi_done, lo_done, added = core.sem("o_turned"), core.sem("o_hi"), core.sem("o_lo"), core.sems("o_added", 2)
        pairs = D // CW // 2
        with ExitStack() as inner:
            tp = [core.ps(inner)(f"o_tp{u}", [P, KD, P]) for u in range(2)]
            with nc.Block() as block:
                @block.sync
                def _(sp):
                    for u in range(2):
                        W.load(sp, u, 0)

                @block.gpsimd
                def _(pool):
                    for u in range(2):
                        W.lo(pool, u, 0)

                @block.tensor
                def _(pe):
                    for b in range(NB):
                        if b >= 2:
                            pe.wait_ge(lo_done, b - 1)
                        for k in range(KD):
                            last = nc.tensor.transpose(tp[b % 2][:, k, :], cat[:, b, k * P:(k + 1) * P], core.ident[:])
                        last.then_inc(turned, 1)

                @block.scalar
                def _(act):
                    for b in range(NB):
                        act.wait_ge(turned, b + 1)
                        nc.scalar.activation(catT[0][:, :, b * P:(b + 1) * P], tp[b % 2][:], ACT.Copy)\
                            .then_inc(hi_done, 1)
                        if b == 4:
                            for u in range(2):
                                W.hi(act, u, 0)

                @block.vector
                def _(dve):
                    for b in range(NB):
                        dve.wait_ge(hi_done, b + 1)
                        cols = slice(b * P, (b + 1) * P)
                        nc.vector.tensor_tensor(catT[1][:, :, cols], tp[b % 2][:],
                                                catT[0][:, :, cols].bitcast(F32), ALU.subtract).then_inc(lo_done, 1)
        ps = [[p(f"o_ps{u}{r}", [P, HALF]) for r in range(4)] for u in range(2)]
        with nc.Block() as block:
            @block.sync
            def _(sp):
                for it in range(1, pairs):
                    for u in range(2):
                        W.load(sp, u, it)

            @block.scalar
            def _(act):
                for it in range(1, pairs):
                    for u in range(2):
                        W.hi(act, u, it)
                for b in range(NB):
                    act.wait_ge(added[1], NB * (pairs - 1) + b + 1)
                    square(act, b)

            @block.vector
            def _(dve):
                def add(u, n):
                    for b in range(NB):
                        dve.wait_ge(block_done[u], NB * n + b + 1)
                        cols = core.xres[:, b, bass.ds((n * 2 + u) * CW, CW)]
                        nc.vector.tensor_tensor(cols, ps[u][b % 4][:, 0:CW], cols, ALU.add).then_inc(added[u], 1)

                @rounds(dve, pairs - 1)
                def _(it):
                    for u in range(2):
                        add(u, it)
                        W.lo(dve, u, it + 1)
                for u in range(2):
                    add(u, pairs - 1)

            @block.tensor
            def _(pe):
                @rounds(pe, pairs)
                def _(it):
                    for u in range(2):
                        pe.wait_ge(W.lo_done[u], it + 1)
                        for b in range(NB):
                            wait_past(pe, added[u], NB * it + max(b - 3, 0))
                            product_N(nc, W.part[u], catT, b, ps[u][b % 4][:, 0:CW]).then_inc(block_done[u], 1)


class EarlyTiles:
    TILES = KEYS * GROUP // BODY // NB
    PER_SLOT = TILES // 2
    STEPS = 2 * KD
    AHEAD = 2

    def __init__(self, core, scope, hT, uT):
        s, p = core.sb(scope), core.ps(scope)
        self.nc, self.hT, self.uT = core.nc, hT, uT
        self.raw = [s(f"y_raw{i}", [P, KD, P]) for i in range(2)]
        self.part = [[s(f"y_{n}{i}", [P, KD, P], F32R) for n in ("hi", "lo")] for i in range(2)]
        self.act_s = [s(f"y_act{i}", [P, SEQ]) for i in range(2)]
        self.stored = core.kept_sems("y_stored", 2)
        self.banks = [p(f"y_banks{i}", [P, 2, HALF]) for i in range(2)]
        self.landed, self.hi_done, self.lo_done, self.h_done, self.gelu_done = (
            core.sems(f"y_{n}", 2) for n in ("landed", "hi_done", "lo_done", "h_done", "gelu"))

    def load(self, sp, b, t):
        wait_past(sp, self.lo_done[t % 2], b * self.PER_SLOT + t // 2)
        tile = b * (self.TILES * BODY // GROUP) + t // GROUP * BODY + t % GROUP
        sp.dma_start(self.raw[t % 2][:], self.uT[tile]).then_inc(self.landed[t % 2], 16)

    def hi(self, act, b, t):
        act.wait_ge(self.landed[t % 2], 16 * (b * self.PER_SLOT + t // 2 + 1))
        wait_past(act, self.h_done[t % 2], b * self.PER_SLOT + t // 2)
        self.nc.scalar.activation(self.part[t % 2][0][:], self.raw[t % 2][:], ACT.Copy)\
            .then_inc(self.hi_done[t % 2], 1)

    def lo(self, pool, b, t):
        pool.wait_ge(self.hi_done[t % 2], b * self.PER_SLOT + t // 2 + 1)
        self.nc.gpsimd.tensor_tensor(self.part[t % 2][1][:], self.raw[t % 2][:],
                                     self.part[t % 2][0][:].bitcast(F32), ALU.subtract)\
            .then_inc(self.lo_done[t % 2], 1)

    def gelu(self, act, b, t):
        act.wait_ge(self.h_done[t % 2], b * self.PER_SLOT + t // 2 + 1)
        wait_past(act, self.stored[t % 2], 16 * (b * self.PER_SLOT + t // 2))
        self.nc.scalar.activation(self.act_s[t % 2][:], self.banks[t % 2][:], ACT.Gelu)\
            .then_inc(self.gelu_done[t % 2], 1)

    def products(self, pe, b, begin, end):
        for step in range(begin, end):
            t, at = step // self.STEPS, step % self.STEPS
            half, kd = at // KD, at % KD
            if at == 0:
                pe.wait_ge(self.lo_done[t % 2], b * self.PER_SLOT + t // 2 + 1)
                wait_past(pe, self.gelu_done[t % 2], b * self.PER_SLOT + t // 2)
            for a, c in PASSES:
                last = self.nc.tensor.matmul(self.banks[t % 2][:, half, :], self.part[t % 2][a][:, kd, :],
                                             self.hT[c][:, kd, half * HALF:(half + 1) * HALF],
                                             start=(kd == 0 and (a, c) == PASSES[0]),
                                             stop=(kd == KD - 1 and (a, c) == PASSES[-1]))
            if at == self.STEPS - 1:
                last.then_inc(self.h_done[t % 2], 1)


def query_stage(core, hT, W, keysT, top_v, top_i, early):
    nc = core.nc
    with ExitStack() as sc:
        s, p = core.sb(sc), core.ps(sc)
        tile_done = W.used
        keys = s("q_keys", [P, SIDES, KEYS])
        qr = [s(f"q_qr{u}", [P, SEQ]) for u in range(2)]
        scores = [s(f"q_sc{u}", [P, NB, KEYS]) for u in range(2)]
        rest = s("q_rest", [P, NB, KEYS])
        mark = s("q_mark", [P, 1])
        best, best_i = s("q_best", [P, NB, TOPK]), s("q_best_i", [P, NB, TOPK], U32)
        ps = early.banks
        sc_p = [p(f"q_scp{u}", [P, NB, KEYS]) for u in range(2)]
        keys_in, chain = core.sem("q_keys_in"), core.sem("q_chain")
        copied, scored, sc_copied, picked = (core.sems(f"q_{n}", 2) for n in ("copied", "scored", "sc_copied", "picked"))
        pairs = SIDES // 2
        with nc.Block() as block:
            @block.sync
            def _(sp):
                sp.dma_start(keys[:], keysT).then_inc(keys_in, 16)
                with sp.Fori(1, pairs) as it:
                    for u in range(2):
                        W.load(sp, u, it)
                for t in range(2 * early.AHEAD):
                    early.load(sp, 0, t)

            @block.gpsimd
            def _(pool):
                for t in range(2 * early.AHEAD):
                    early.lo(pool, 0, t)

            @block.scalar
            def _(act):
                def evacuate(u, n):
                    act.wait_ge(tile_done[u], n + 1)
                    wait_past(act, scored[u], n)
                    nc.scalar.activation(qr[u][:], ps[u][:], ACT.Copy).then_inc(copied[u], 1)

                def copy_scores(u, n):
                    act.wait_ge(scored[u], n + 1)
                    wait_past(act, picked[u], n)
                    nc.scalar.activation(scores[u][:], sc_p[u][:], ACT.Copy).then_inc(sc_copied[u], 1)

                @rounds(act, pairs - 1)
                def _(it):
                    for u in range(2):
                        evacuate(u, it)
                        W.hi(act, u, it + 1)
                        copy_scores(u, it)
                for t in range(early.AHEAD):
                    early.hi(act, 0, t)
                for u in range(2):
                    evacuate(u, pairs - 1)
                    copy_scores(u, pairs - 1)
                for t in range(early.AHEAD, 2 * early.AHEAD):
                    early.hi(act, 0, t)
                    if t == early.AHEAD:
                        early.gelu(act, 0, 0)

            @block.vector
            def _(dve):
                steps = Steps(dve, chain)
                PER = 10

                def pick(u, n):
                    dve.wait_ge(sc_copied[u], n + 1)
                    V, src = nc.vector, scores[u]
                    hold(nc, mark[:])
                    for b in range(NB):
                        last = V.max(best[:, b, 0:8], src[:, b, :])
                    steps(last)
                    hold(nc, mark[:])
                    for b in range(NB):
                        last = V.max_index(best_i[:, b, 0:8], best[:, b, 0:8], src[:, b, :])
                    for b in range(NB):
                        last = V.match_replace(rest[:, b, :], best[:, b, 0:8], src[:, b, :], LOWEST)
                    steps(last)
                    hold(nc, mark[:])
                    for b in range(NB):
                        last = V.max(best[:, b, 8:16], rest[:, b, :])
                    steps(last)
                    hold(nc, mark[:])
                    for b in range(NB):
                        last = V.max_index(best_i[:, b, 8:16], best[:, b, 8:16], rest[:, b, :])
                    steps(last)
                    side = bass.ds(n * 2 + u, 1)
                    steps(V.tensor_scalar(top_v[:, :, side, :].rearrange("p b a k -> p (b a) k"), best[:], 1.0, None,
                                          ALU.mult))
                    V.tensor_scalar(top_i[:, :, side, :].rearrange("p b a k -> p (b a) k"), best_i[:], 1.0, None,
                                    ALU.mult).then_inc(picked[u], 1)
                    dve.wait_ge(picked[u], n + 1)

                @rounds(dve, pairs - 1)
                def _(it):
                    steps.base, steps.n = it * PER, 0
                    for u in range(2):
                        W.lo(dve, u, it + 1)
                        pick(u, it)
                    assert steps.n == PER
                steps.base = (pairs - 1) * PER
                steps.n = 0
                for u in range(2):
                    pick(u, pairs - 1)

            @block.tensor
            def _(pe):
                def tile(u, n):
                    pe.wait_ge(W.lo_done[u], n + 1)
                    wait_past(pe, copied[u], n)
                    product_T(nc, W, u, hT, ps[u]).then_inc(tile_done[u], 1)

                def score(u, n):
                    pe.wait_ge(copied[u], n + 1)
                    wait_past(pe, sc_copied[u], n)
                    for b in range(NB):
                        last = nc.tensor.matmul(sc_p[u][:, b, :], qr[u][:, b * P:(b + 1) * P],
                                                keys[:, bass.ds(n * 2 + u, 1), :].rearrange("p a k -> p (a k)"),
                                                start=True, stop=True)
                    last.then_inc(scored[u], 1)

                tile(0, 0)
                pe.wait_ge(keys_in, 16)
                @rounds(pe, pairs - 1)
                def _(it):
                    tile(1, it)
                    score(0, it)
                    tile(0, it + 1)
                    score(1, it)
                tile(1, pairs - 1)
                score(0, pairs - 1)
                score(1, pairs - 1)
                for u in range(2):
                    pe.wait_ge(copied[u], pairs)
                early.products(pe, 0, 0, early.AHEAD * early.STEPS)


def gate_stage(core, top_v, top_i, early):
    nc = core.nc
    with ExitStack() as sc:
        s, p = core.sb(sc), core.ps(sc)
        CN = TOPK * TOPK
        cand, rest = s("t_cand", [P, PH, CN]), s("t_rest", [P, PH, CN])
        best, pos = s("t_best", [P, PH, TOPK]), s("t_pos", [P, PH, TOPK], U32)
        part_u = s("t_part_u", [P, PH, TOPK], U32)
        part = s("t_part", [P, PH, TOPK])
        packed = s("t_packed", [P, 3, SLOTS])
        packedT = s("t_packedT", [P, 3, P])
        total, mark = s("t_total", [P, PH]), s("t_mark", [P, 1])
        iota = s("t_iota", [P, KEYS])
        iota_i = s("t_iota_i", [P, KEYS], I32)
        RQ, TQ = 2, 4
        first, second = s("t_first", [P, RQ, TQ, KEYS]), s("t_second", [P, RQ, TQ, KEYS])
        dense = [core.xres[:].rearrange("p b (j t) -> p (b j) t", t=TB), s("t_dense", [P, KEYS, TB])[:]]
        tr_p = p("t_trp", [P, HALF])
        g_p = [p(f"t_gp{r}", [P, TQ, KEYS]) for r in range(RQ)]
        m = {n: core.sem(f"t_{n}")
             for n in "iota_i iota chain best_ready exped packed turned unpacked x_resting".split()}
        hot, produced, copied = (core.sems(f"t_{n}", RQ) for n in ("hot", "produced", "copied"))
        stored = core.sems("t_stored", 2)
        ET, ES, TS = early.TILES, early.PER_SLOT, early.STEPS
        groups = P // TQ
        G4 = groups // RQ
        HG = groups // 2
        LAG, TAIL = 6, 22

        def done(b, t):
            return isinstance(b, int) and b == 0 and t < 2 * early.AHEAD

        def first_steps(b):
            return 3 * TS + (early.AHEAD * TS if isinstance(b, int) and b == 0 else 0)

        def steps_before(b, q):
            begin = first_steps(b) + LAG
            rest = ET * TS - begin - (TAIL if isinstance(b, int) and b == NB - 1 else 0)
            return begin + rest * q // groups

        def tiles_before(b, q):
            return range(steps_before(b, q - 1) // TS if q else 0, steps_before(b, q) // TS)

        with nc.Block() as block:
            @block.gpsimd
            def _(pool):
                def store(b, t):
                    pool.wait_ge(early.gelu_done[t % 2], b * ES + t // 2 + 1)
                    pool.dma_start(core.acts[b * ET + t], early.act_s[t % 2][:])\
                        .then_inc(early.stored[t % 2], 16)

                def token_block(b, final=False):
                    def after(t):
                        if t + 2 >= ET:
                            if not final:
                                early.lo(pool, b + 1, t + 2 - ET)
                        elif not done(b, t + 2):
                            early.lo(pool, b, t + 2)
                        store(b, t)

                    for t in range(ET):
                        after(t)

                nc.gpsimd.iota(iota_i[:], pattern=[[1, KEYS]], base=0, channel_multiplier=0).then_inc(m["iota_i"], 1)
                pool.wait_ge(m["iota_i"], 1)
                nc.gpsimd.tensor_copy(iota[:], iota_i[:]).then_inc(m["iota"], 1)
                rounds(pool, NB - 1)(token_block)
                token_block(NB - 1, final=True)
                for u in range(2):
                    pool.wait_ge(early.stored[u], 16 * ES * NB)

            @block.vector
            def _(dve):
                V = nc.vector
                steps = Steps(dve, m["chain"])
                dve.wait_ge(m["iota"], 1)
                PER = 17

                @rounds(dve, NB)
                def _(b):
                    steps.base, steps.n = b * PER, 0
                    tv = [top_v[:, bass.ds(b, 1), c::2, :].rearrange("p a h k -> p (a h) k") for c in range(2)]
                    ti = [top_i[:, bass.ds(b, 1), c::2, :].rearrange("p a h k -> p (a h) k") for c in range(2)]
                    wide = [P, PH, TOPK, TOPK]
                    steps(V.tensor_tensor(cand[:].rearrange("p h (i j) -> p h i j", i=TOPK),
                                          tv[0].unsqueeze(3).to_broadcast(wide), tv[1].unsqueeze(2).to_broadcast(wide),
                                          ALU.add))
                    hold(nc, mark[:])
                    for h in range(PH):
                        last = V.max(best[:, h, 0:8], cand[:, h, :])
                    steps(last)
                    hold(nc, mark[:])
                    for h in range(PH):
                        last = V.max_index(pos[:, h, 0:8], best[:, h, 0:8], cand[:, h, :])
                    for h in range(PH):
                        last = V.match_replace(rest[:, h, :], best[:, h, 0:8], cand[:, h, :], LOWEST)
                    steps(last)
                    hold(nc, mark[:])
                    for h in range(PH):
                        last = V.max(best[:, h, 8:16], rest[:, h, :])
                    steps(last)
                    hold(nc, mark[:])
                    for h in range(PH):
                        last = V.max_index(pos[:, h, 8:16], best[:, h, 8:16], rest[:, h, :])
                    steps(last)
                    wait_past(dve, m["turned"], 3 * b)
                    gate = packed[:, 0, :].rearrange("p (h k) -> p h k", h=PH)
                    V.tensor_tensor(gate, best[:], best[:, :, 0:1].to_broadcast([P, PH, TOPK]), ALU.subtract)\
                        .then_inc(m["best_ready"], 1)
                    hot4 = rest[:].rearrange("p h (i j) -> p h i j", i=TOPK)
                    for c in range(2):
                        if c == 0:
                            steps(V.tensor_scalar(part_u[:], pos[:], 4, None, ALU.logical_shift_right))
                        else:
                            steps(V.tensor_scalar(part_u[:], pos[:], TOPK - 1, None, ALU.bitwise_and))
                        steps(V.tensor_copy(part[:], part_u[:]))
                        steps(V.tensor_tensor(hot4, part[:].unsqueeze(3).to_broadcast(wide),
                                              iota[:, 0:TOPK].unsqueeze(1).unsqueeze(1).to_broadcast(wide),
                                              ALU.is_equal))
                        steps(V.tensor_tensor(hot4, hot4, ti[c].unsqueeze(2).to_broadcast(wide), ALU.mult))
                        steps(V.tensor_reduce(packed[:, 1 + c, :], rest[:].rearrange("p h (i j) -> p (h i) j", i=TOPK),
                                              AX_X, ALU.add))
                    dve.wait_ge(m["exped"], b + 1)
                    steps(V.tensor_reduce(total[:], gate, AX_X, ALU.add))
                    steps(V.reciprocal(total[:], total[:]))
                    V.tensor_tensor(gate, gate, total[:].unsqueeze(2).to_broadcast([P, PH, TOPK]), ALU.mult)\
                        .then_inc(m["packed"], 1)
                    dve.wait_ge(m["turned"], 3 * b + 3)
                    V.tensor_copy(packedT[:], tr_p[:, 0:3 * P].rearrange("p (a t) -> p a t", a=3))\
                        .then_inc(m["unpacked"], 1)
                    dve.wait_ge(m["unpacked"], b + 1)
                    for q in range(groups):
                        r = q % RQ
                        wait_past(dve, produced[r], b * G4 + q // RQ)
                        keys = packedT[:, 1, q * TQ:(q + 1) * TQ].unsqueeze(2)
                        V.tensor_tensor(first[:, r, :, :], iota[:].unsqueeze(1).to_broadcast([P, TQ, KEYS]),
                                        keys.to_broadcast([P, TQ, KEYS]), ALU.is_equal)
                        for i in range(TQ):
                            tok = q * TQ + i
                            last = V.tensor_scalar(second[:, r, i, :], iota[:], packedT[:, 2, tok:tok + 1],
                                                   packedT[:, 0, tok:tok + 1], ALU.is_equal, ALU.mult)
                        last.then_inc(hot[r], 1)
                    assert steps.n == PER, steps.n

            @block.scalar
            def _(act):
                def copy(b, q):
                    r, u = q % RQ, q // HG
                    if q % HG == 0:
                        wait_past(act, stored[u], 16 * b)
                    if q == 0 and isinstance(b, int) and b == 0:
                        act.wait_ge(m["x_resting"], 16)
                    act.wait_ge(produced[r], b * G4 + q // RQ + 1)
                    at = (q % HG) * TQ
                    nc.scalar.activation(dense[u][:, :, at:at + TQ], g_p[r][:].rearrange("p t j -> p j t"),
                                         ACT.Copy).then_inc(copied[r], 1)

                def token_block(b, final=False):
                    def after(t):
                        if not (done(b, t) and t == 0):
                            early.gelu(act, b, t)
                        if t + 2 >= ET:
                            if not final:
                                early.hi(act, b + 1, t + 2 - ET)
                        elif not done(b, t + 2):
                            early.hi(act, b, t + 2)
                        if t == first_steps(b) // TS - 2:
                            act.wait_ge(m["best_ready"], b + 1)
                            nc.scalar.activation(packed[:, 0, :], packed[:, 0, :], ACT.Exp).then_inc(m["exped"], 1)

                    for q in range(groups):
                        for t in tiles_before(b, q):
                            after(t)
                        copy(b, q)
                    for t in range(steps_before(b, groups - 1) // TS, ET):
                        after(t)

                rounds(act, NB - 1)(token_block)
                token_block(NB - 1, final=True)

            @block.sync
            def _(sp):
                def store(b, u):
                    for r in range(RQ):
                        sp.wait_ge(copied[r], b * G4 + (u + 1) * HG // RQ)
                    sp.dma_start(core.gates[b * 2 + u], dense[u]).then_inc(stored[u], 16)

                def token_block(b, final=False):
                    for t in range(2, ET):
                        if not done(b, t):
                            early.load(sp, b, t)
                        if t == 3 and not (isinstance(b, int) and b == 0):
                            store(b - 1, 1)
                    if not final:
                        for t in range(2):
                            early.load(sp, b + 1, t)
                    store(b, 0)

                sp.dma_start(core.resting, core.xres[:]).then_inc(m["x_resting"], 16)
                rounds(sp, NB - 1)(token_block)
                token_block(NB - 1, final=True)
                store(NB - 1, 1)
                for u in range(2):
                    sp.wait_ge(stored[u], 16 * NB)

            @block.tensor
            def _(pe):
                def token_block(b):
                    begin = first_steps(b)
                    early.products(pe, b, early.AHEAD * TS if isinstance(b, int) and b == 0 else 0, begin)
                    pe.wait_ge(m["packed"], b + 1)
                    for i in range(3):
                        nc.tensor.transpose(tr_p[:, i * P:(i + 1) * P], packed[:, i, :], core.ident[:])\
                            .then_inc(m["turned"], 1)
                    early.products(pe, b, begin, begin + LAG)
                    for q in range(groups):
                        r = q % RQ
                        if q:
                            early.products(pe, b, steps_before(b, q - 1), steps_before(b, q))
                        pe.wait_ge(hot[r], b * G4 + q // RQ + 1)
                        wait_past(pe, copied[r], b * G4 + q // RQ)
                        for i in range(TQ):
                            last = nc.tensor.matmul(g_p[r][:, i, :], first[:, r, i, :], second[:, r, i, :],
                                                    start=True, stop=True)
                        last.then_inc(produced[r], 1)
                    early.products(pe, b, steps_before(b, groups - 1), ET * TS)

                rounds(pe, NB - 1)(token_block)
                token_block(NB - 1)


def expert_stage(core, hT, uT, v_tab):
    nc = core.nc
    bodies = KEYS // BODY
    late = range(GROUP, BODY)
    with ExitStack() as sc:
        s, p = core.sb(sc), core.ps(sc)
        u_raw, v_raw = s("e_uraw", [P, KD, P]), [s(f"e_vraw{i}", [P, D]) for i in range(GROUP)]
        u_part = {k: [s(f"e_u{n}{k}", [P, KD, P], F32R) for n in ("hi", "lo")] for k in late}
        v_part = [[s(f"e_v{n}{k}", [P, D], F32R) for n in ("hi", "lo")] for k in range(BODY)]
        w_part = [[s(f"e_w{n}{k}", [P, SEQ], F32R) for n in ("hi", "lo")] for k in range(BODY)]
        gates = s("e_gates", [P, NTB, GROUP, TB])
        act_s = [s(f"e_act{i}", [P, SEQ]) for i in range(GROUP)]
        a_p = {k: p(f"e_ap{k}", [P, 2, HALF]) for k in late}
        o_p = [p(f"e_op{i}", [P, 2, HALF]) for i in range(2)]
        x_back = core.sem("e_x_back")
        square = Squares(core, "e", [a[:] for a in act_s])
        g_in, out_done, added = (core.sems(f"e_{n}", 2) for n in ("g_in", "out_done", "added"))
        u_in, act_in, u_hi, u_lo, v_in, v_hi, v_lo, h_done, gelu_done, weighed, w_hi, w_lo = (
            core.sems(f"e_{n}", BODY) for n in ("u_in", "act_in", "u_hi", "u_lo", "v_in", "v_hi", "v_lo", "h_done",
                                                "gelu", "weighed", "w_hi", "w_lo"))
        gates_v = core.gates.rearrange("t i j c -> i t j c")
        v_v = v_tab.rearrange("(i j) d -> j i d", j=KEYS)
        with nc.Block() as block:
            @block.sync
            def _(sp):
                def load_u(it, k):
                    if k == GROUP:
                        wait_past(sp, u_lo[BODY - 1], it)
                    else:
                        sp.wait_ge(u_lo[k - 1], it + 1)
                    sp.dma_start(u_raw[:], uT[it * BODY + k]).then_inc(u_in[k], 16)

                def load_v(it, k):
                    if k < GROUP:
                        wait_past(sp, v_lo[k + GROUP], it)
                    else:
                        sp.wait_ge(v_lo[k - GROUP], it + 1)
                    sp.dma_start(v_raw[k % GROUP][:], v_v[it * BODY + k]).then_inc(v_in[k], 16)

                def load_act(it, k):
                    wait_past(sp, w_lo[k + GROUP], it)
                    sp.dma_start(act_s[k][:], core.acts[it * GROUP + k]).then_inc(act_in[k], 16)

                def load_gates(it, g):
                    for k in range(GROUP):
                        if g:
                            sp.wait_ge(weighed[k], it + 1)
                        else:
                            wait_past(sp, weighed[k + GROUP], it)
                    sp.dma_start(gates[:], gates_v[:, :, bass.ds(it * BODY + g * GROUP, GROUP), :])\
                        .then_inc(g_in[g], 16)

                @rounds(sp, bodies)
                def _(it):
                    for k in late:
                        load_u(it, k)
                    for k in range(GROUP):
                        load_act(it, k)
                    load_gates(it, 0)
                    for k in range(BODY):
                        load_v(it, k)
                    load_gates(it, 1)
                    if isinstance(it, int) and it == 0:
                        sp.dma_start(core.xres[:], core.resting).then_inc(x_back, 16)

            @block.scalar
            def _(act):
                def split_u(it, k):
                    act.wait_ge(u_in[k], 16 * (it + 1))
                    wait_past(act, h_done[k], it)
                    nc.scalar.activation(u_part[k][0][:], u_raw[:], ACT.Copy).then_inc(u_hi[k], 1)

                def split_v(it, k):
                    act.wait_ge(v_in[k], 16 * (it + 1))
                    wait_past(act, out_done[k // GROUP], NB * it)
                    nc.scalar.activation(v_part[k][0][:], v_raw[k % GROUP][:], ACT.Copy).then_inc(v_hi[k], 1)

                def gelu(it, k):
                    act.wait_ge(h_done[k], it + 1)
                    act.wait_ge(w_lo[k - GROUP], it + 1)
                    nc.scalar.activation(act_s[k % GROUP][:], a_p[k][:], ACT.Gelu).then_inc(gelu_done[k], 1)

                def split_w(it, k):
                    act.wait_ge(weighed[k], it + 1)
                    wait_past(act, out_done[k // GROUP], NB * it)
                    nc.scalar.activation(w_part[k][0][:], act_s[k % GROUP][:], ACT.Copy).then_inc(w_hi[k], 1)

                @rounds(act, bodies)
                def _(it):
                    for k in late:
                        split_u(it, k)
                    for k in range(GROUP):
                        split_v(it, k)
                    for k in range(GROUP):
                        split_w(it, k)
                    for k in late:
                        split_v(it, k)
                    for k in late:
                        gelu(it, k)
                        split_w(it, k)

                for k in late:
                    act.wait_ge(w_lo[k], bodies)
                for b in range(NB):
                    act.wait_ge(added[1], NB * (bodies - 1) + b + 1)
                    square(act, b)

            @block.gpsimd
            def _(pool):
                def lo(raw, part, hi_done, lo_done, it, k):
                    pool.wait_ge(hi_done[k], it + 1)
                    nc.gpsimd.tensor_tensor(part[k][1][:], raw[:], part[k][0][:].bitcast(F32),
                                            ALU.subtract).then_inc(lo_done[k], 1)

                @rounds(pool, bodies)
                def _(it):
                    for k in late:
                        lo(u_raw, u_part, u_hi, u_lo, it, k)
                    for k in range(BODY):
                        lo(v_raw[k % GROUP], v_part, v_hi, v_lo, it, k)

            @block.vector
            def _(dve):
                def weigh(it, k):
                    dve.wait_ge(g_in[k // GROUP], 16 * (it + 1))
                    if k < GROUP:
                        dve.wait_ge(act_in[k], 16 * (it + 1))
                    else:
                        dve.wait_ge(gelu_done[k], it + 1)
                    w = act_s[k % GROUP][:].rearrange("p (t c) -> p t c", c=TB)
                    nc.vector.tensor_tensor(w, w, gates[:, :, k % GROUP, :], ALU.mult)\
                        .then_inc(weighed[k], 1)

                def lo(it, k):
                    dve.wait_ge(w_hi[k], it + 1)
                    nc.vector.tensor_tensor(w_part[k][1][:], act_s[k % GROUP][:], w_part[k][0][:].bitcast(F32),
                                            ALU.subtract).then_inc(w_lo[k], 1)

                def add(it, g, b):
                    dve.wait_ge(out_done[g], NB * it + b + 1)
                    nc.vector.tensor_tensor(core.xres[:, b, :], o_p[b % 2][:].rearrange("p a c -> p (a c)"),
                                            core.xres[:, b, :], ALU.add).then_inc(added[g], 1)

                @rounds(dve, bodies)
                def _(it):
                    for k in range(GROUP):
                        weigh(it, k)
                    for k in range(GROUP):
                        lo(it, k)
                    weigh(it, GROUP)
                    lo(it, GROUP)
                    weigh(it, GROUP + 1)
                    if isinstance(it, int) and it == 0:
                        dve.wait_ge(x_back, 16)
                    add(it, 0, 0)
                    lo(it, GROUP + 1)
                    for b in range(1, NB):
                        add(it, 0, b)
                    for b in range(NB):
                        add(it, 1, b)

            @block.tensor
            def _(pe):
                def with_u(it, k):
                    pe.wait_ge(u_lo[k], it + 1)
                    wait_past(pe, gelu_done[k], it)
                    for half in range(2):
                        for kd in range(KD):
                            for a, c in PASSES:
                                last = nc.tensor.matmul(a_p[k][:, half, :], u_part[k][a][:, kd, :],
                                                        hT[c][:, kd, half * HALF:(half + 1) * HALF],
                                                        start=(kd == 0 and (a, c) == PASSES[0]),
                                                        stop=(kd == KD - 1 and (a, c) == PASSES[-1]))
                    last.then_inc(h_done[k], 1)

                def with_v(it, g):
                    tiles = range(g * GROUP, (g + 1) * GROUP)
                    for k in tiles:
                        pe.wait_ge(w_lo[k], it + 1)
                        pe.wait_ge(v_lo[k], it + 1)
                    for b in range(NB):
                        if b >= 2:
                            pe.wait_ge(added[g], NB * it + b - 1)
                        elif g:
                            pe.wait_ge(added[0], NB * it + NB - 1 + b)
                        elif not (isinstance(it, int) and it == 0):
                            pe.wait_ge(added[1], NB * (it - 1) + NB - 1 + b)
                        for k in tiles:
                            for a in range(2):
                                for c in range(2 - a):
                                    for half in range(2):
                                        last = nc.tensor.matmul(
                                            o_p[b % 2][:, half, :], w_part[k][a][:, b * P:(b + 1) * P],
                                            v_part[k][c][:, half * HALF:(half + 1) * HALF],
                                            start=(k == tiles[0] and a == 0 and c == 0),
                                            stop=(k == tiles[-1] and a == 1))
                        last.then_inc(out_done[g], 1)

                @rounds(pe, bodies)
                def _(it):
                    for k in late:
                        with_u(it, k)
                    with_v(it, 0)
                    with_v(it, 1)


def embedding_stage(core, hT, W, pT, w_proj, g_row, out):
    PARTS = ((0, 4), (4, 7), (7, 8))
    nc = core.nc
    with ExitStack() as sc:
        s, p = core.sb(sc), core.ps(sc)
        gate_done = W.used
        p_raw, w_raw = s("l_praw", [P, KP, SEQ]), s("l_wraw", [P, KP, D])
        p_part = [s(f"l_p{n}", [P, KP, SEQ], F32R) for n in ("hi", "lo")]
        w_part = [s(f"l_wp{n}", [P, KP, D], F32R) for n in ("hi", "lo")]
        gate = [s(f"l_gate{i}", [P, CW]) for i in range(2)]
        g_b, xn = s("l_g", [P, D]), s("l_xn", [P, 2, D])
        v, y, t = (s(f"l_{n}", [P, NB]) for n in ("v", "y", "t"))
        gate_p = [p(f"l_gp{r}", [P, HALF]) for r in range(4)]
        proj_p = [p(f"l_pp{r}", [P, HALF]) for r in range(4)]
        small_in, small_hi, small_lo, chain = (core.sem(f"l_{n}") for n in ("small_in", "small_hi", "small_lo", "chain"))
        g_in, var_ready, root_ready, xn_ready = (core.sem(f"l_{n}") for n in ("g_in", "var", "root", "xn_ready"))
        proj_done, opened, added, stored = (
            core.sems(f"l_{n}", 2) for n in ("proj_done", "opened", "added", "stored"))
        pairs = D // CW // 2
        square = Squares(core, "l", [p_raw[:, u, :] for u in range(KP)])
        with nc.Block() as block:
            @block.sync
            def _(sp):
                sp.dma_start(p_raw[:], pT).then_inc(small_in, 16)
                sp.dma_start(w_raw[:], w_proj).then_inc(small_in, 16)
                sp.dma_start(g_b[:], g_row.partition_broadcast(P)).then_inc(g_in, 16)
                for it in range(1, pairs):
                    for u in range(2):
                        W.load(sp, u, it)
                for b in range(NB):
                    sp.wait_ge(xn_ready, b + 1)
                    sp.dma_start(out[b * P:(b + 1) * P, :], xn[:, b % 2, :]).then_inc(stored[b % 2], 16)
                for u in range(2):
                    sp.wait_ge(stored[u], 16 * (NB // 2))

            @block.scalar
            def _(act):
                act.wait_ge(small_in, 32)
                nc.scalar.activation(p_part[0][:], p_raw[:], ACT.Copy).then_inc(small_hi, 1)
                nc.scalar.activation(w_part[0][:], w_raw[:], ACT.Copy).then_inc(small_hi, 1)

                def open_gate(u, n, b):
                    act.wait_ge(gate_done[u], NB * n + b + 1)
                    if b >= 2:
                        act.wait_ge(added[u], NB * n + b - 1)
                    elif u:
                        act.wait_ge(added[0], NB * n + NB - 1 + b)
                    elif n:
                        act.wait_ge(added[1], NB * (n - 1) + NB - 1 + b)
                    nc.scalar.activation(gate[b % 2][:], gate_p[b % 4][:, 0:CW], ACT.Sigmoid).then_inc(opened[u], 1)

                def open_gates(u, n):
                    for b in range(NB):
                        open_gate(u, n, b)

                for it in range(pairs):
                    for u in range(2):
                        if (it, u) == (pairs - 1, 1):
                            break
                        open_gates(u, it)
                        if it + 1 < pairs:
                            W.hi(act, u, it + 1)
                act.wait_ge(small_lo, 1)
                roots = 0
                for b in range(NB + 1):
                    if b < NB:
                        open_gate(1, pairs - 1, b)
                    if b:
                        act.wait_ge(added[1], NB * (pairs - 1) + b)
                        square(act, b - 1)
                    if b in (5, NB):
                        for begin, end in PARTS[roots:1 if b == 5 else len(PARTS)]:
                            roots += 1
                            act.wait_ge(var_ready, roots)
                            nc.scalar.activation(y[:, begin:end], t[:, begin:end], ACT.Sqrt).then_inc(root_ready, 1)

            @block.vector
            def _(dve):
                dve.wait_ge(small_hi, 2)
                for part, raw in ((p_part, p_raw), (w_part, w_raw)):
                    nc.vector.tensor_tensor(part[1][:], raw[:], part[0][:].bitcast(F32), ALU.subtract)\
                        .then_inc(small_lo, 1)
                steps = Steps(dve, chain)

                def add(u, n, b):
                    dve.wait_ge(opened[u], NB * n + b + 1)
                    dve.wait_ge(proj_done[u], NB * n + b + 1)
                    steps(nc.vector.tensor_tensor(gate[b % 2][:], proj_p[b % 4][:, 0:CW], gate[b % 2][:], ALU.mult))
                    cols = core.xres[:, b, (n * 2 + u) * CW:(n * 2 + u + 1) * CW]
                    nc.vector.tensor_tensor(cols, cols, gate[b % 2][:], ALU.add).then_inc(added[u], 1)

                def norm(part):
                    begin, end = PARTS[part]
                    cols = slice(begin, end)
                    dve.wait_ge(square.squared, end)
                    rstd(nc, steps, core.ss[:, cols], v[:, cols], y[:, cols], t[:, cols], D, var_ready, root_ready,
                         part + 1)
                    for b in range(begin, end):
                        if b >= 2:
                            dve.wait_ge(stored[b % 2], 16 * (b // 2))
                        nc.vector.scalar_tensor_tensor(out=xn[:, b % 2, :], in0=core.xres[:, b, :],
                                                       scalar=y[:, b:b + 1], in1=g_b[:],
                                                       op0=ALU.mult, op1=ALU.mult).then_inc(xn_ready, 1)

                for it in range(pairs):
                    for u in range(2):
                        if (it, u) == (pairs - 1, 1):
                            break
                        for b in range(NB):
                            add(u, it, b)
                        if it + 1 < pairs:
                            W.lo(dve, u, it + 1)
                dve.wait_ge(g_in, 16)
                for b in range(NB):
                    add(1, pairs - 1, b)
                    if b == 4:
                        norm(0)
                norm(1)
                norm(2)

            @block.tensor
            def _(pe):
                def project(it, u, b):
                    at = (it * 2 + u) * CW
                    part = [w[:, :, at:at + CW] for w in w_part]
                    product_N(nc, part, p_part, b, proj_p[b % 4][:, 0:CW], KP).then_inc(proj_done[u], 1)

                for it in range(pairs):
                    for u in range(2):
                        if it:
                            pe.wait_ge(W.lo_done[u], it + 1)
                        for begin in range(0, NB, 4):
                            for b in range(begin, begin + 4):
                                if b >= 4:
                                    pe.wait_ge(added[u], NB * it + b - 3)
                                elif u:
                                    pe.wait_ge(added[0], NB * it + NB - 3 + b)
                                elif it:
                                    pe.wait_ge(added[1], NB * (it - 1) + NB - 3 + b)
                                product_N(nc, W.part[u], hT, b, gate_p[b % 4][:, 0:CW]).then_inc(gate_done[u], 1)
                                if (it, u, begin) != (0, 0, 0):
                                    project(it, u, b)
                            if (it, u, begin) == (0, 0, 0):
                                pe.wait_ge(small_lo, 2)
                                for b in range(4):
                                    project(it, u, b)


def layer(nc, x, pT, positions, w_t, w_n, w_up, b_up, g_mix, g_peer, g_ple, g_final, g_gla, w_out,
          w_q, keysT, uT, v_tab, w_gate, w_proj, ident, tri, rev, rot, freq, logmult, out):
    def columns(w):
        by_tile = w.rearrange("(k p) c -> p k c", p=P)
        return lambda n: by_tile[:, :, bass.ds(n * CW, CW)]

    with ExitStack() as top:
        core = Core(nc, top)
        with ExitStack() as mix:
            rotary = Rotary(core, mix)
            with ExitStack() as sc:
                hT = core.hT_pair(sc, "h1T")
                W_t = Weights(core, sc, "iT", P, lambda n: w_t[n])
                norm_stage(core, "n1", g_mix, hT, W_t, x, ident)
                W_n = Weights(core, sc, "iN", CW, columns(w_n), NB)
                in_projection_T(core, hT, W_t, W_n)
                in_projection_N(core, hT, W_n, rotary, positions, freq)
            sb = core.sb(mix)
            cat = sb("cat", [P, NB, D])
            with ExitStack() as sc:
                opened, scale = core.sb(sc)("opened", [P, NB, GW]), core.sb(sc)("scale", [P, NB * GH])
                gla_stage(core, cat, opened, scale, w_up, b_up, g_gla, tri, rev)
                attention_stage(core, cat, opened, scale, rotary, rot, logmult)
            out_projection(core, cat, w_out)
        core.recycle()
        with ExitStack() as sc:
            hT = core.hT_pair(sc, "h2T")
            with ExitStack() as inner:
                sb = core.sb(inner)
                top_v, top_i = sb("top_v", [P, NB, SIDES, TOPK]), sb("top_i", [P, NB, SIDES, TOPK])
                early = EarlyTiles(core, inner, hT, uT)
                with ExitStack() as query:
                    W_q = Weights(core, query, "q", P, lambda n: w_q[n])
                    norm_stage(core, "n2", g_peer, hT, W_q)
                    query_stage(core, hT, W_q, keysT, top_v, top_i, early)
                gate_stage(core, top_v, top_i, early)
            core.recycle()
            expert_stage(core, hT, uT, v_tab)
            W_l = Weights(core, sc, "l", CW, columns(w_gate), NB)
            norm_stage(core, "n3", g_ple, hT, W_l)
            embedding_stage(core, hT, W_l, pT, w_proj, g_final, out)


def constants():
    import numpy as np

    s, c = np.arange(P)[:, None], np.arange(P)[None, :]
    same = s // CH == c // CH
    tri = np.where(same & (s <= c), 1 / 16, 0).astype(np.float32)
    rev = np.where(same & (s > c), 1 / 16, 0).astype(np.float32)
    rot, freq = np.zeros((P, P), np.float32), np.zeros((P, 1), np.float32)
    rotated = AD // 4
    inv = np.float32(500000.0) ** (-np.arange(0, rotated, 2, dtype=np.float32) / np.float32(rotated))
    for head in range(0, P, AD):
        for i in range(rotated // 2):
            rot[head + rotated // 2 + i, head + i] = -1.0
            rot[head + i, head + rotated // 2 + i] = 1.0
            freq[head + i] = freq[head + rotated // 2 + i] = inv[i]
    back = s + (SEQ - P) - np.arange(SEQ)[None, :]
    count = sum(((back >= 0) & (back <= w) & (back % d == 0)).astype(np.float64)
                for w, d in ((128, 1), (512, 4), (2048, 16)))
    logmult = np.where(count > 0, AD ** 0.5 * np.log(np.maximum(count, 1)), -1e30).astype(np.float32)
    return {"c_ident": np.eye(P, dtype=np.float32), "c_tri": tri, "c_rev": rev, "c_rot": rot, "c_freq": freq,
            "c_logmult": logmult}


def laid_out(inputs):
    import numpy as np

    a = {k: np.asarray(v) for k, v in inputs.items()}

    def tiles(w):
        return np.ascontiguousarray(w.reshape(KD, P, -1, P).transpose(2, 1, 0, 3))

    w = a["w_in"][0]
    cut = np.cumsum([GK, GK, GW, GW, RANK, HALF, HALF, HALF])
    q, k, v, r, _, qb, kb, vb = (w[:, i:j] for i, j in zip([0, *cut], cut))
    code = w[:, cut[3]:cut[3] + P]
    return {
        "x": a["x"][0],
        "pT": np.ascontiguousarray(a["p"][0, 0].reshape(SEQ, KP, P).transpose(2, 1, 0)),
        "positions": a["positions"],
        "w_t": tiles(np.concatenate([q, k, qb, kb, code], axis=1)),
        "w_n": np.ascontiguousarray(np.concatenate([v, r, vb], axis=1)),
        "w_up": a["w_gla_gate_up"][0],
        "b_up": a["b_gla_gate"][0],
        "g_mix": a["g_mix"][0], "g_peer": a["g_peer"][0], "g_ple": a["g_ple"][0], "g_final": a["g_final"],
        "g_gla": a["g_gla_out"][0].reshape(GW),
        "w_out": a["w_out"][0],
        "w_q": tiles(a["w_peer_q"][0]),
        "keysT": np.ascontiguousarray(a["peer_sub_keys"][0].reshape(SIDES, KEYS, P).transpose(2, 0, 1)),
        "uT": np.ascontiguousarray(a["peer_u"][0].reshape(P, KEYS, KD, P).transpose(1, 3, 2, 0)),
        "v_tab": a["peer_v"][0],
        "w_gate": a["w_ple_gate"][0],
        "w_proj": np.ascontiguousarray(a["w_ple_proj"][0].reshape(KP, P, D).transpose(1, 0, 2)),
    }


def kernel(**inputs):
    import numpy as np
    import concourse.bacc as bacc
    from concourse.bass_utils import run_bass_kernel_spmd

    nc = bacc.Bacc("TRN2", target_bir_lowering=False, num_devices=1)
    arrays = {f"in_{k}": np.ascontiguousarray(v) for k, v in {**laid_out(inputs), **constants()}.items()}
    args = [nc.dram_tensor(k, v.shape, mybir.dt.from_np(v.dtype), kind="ExternalInput").ap()
            for k, v in arrays.items()]
    out = nc.dram_tensor("out", (SEQ, D), F32, kind="ExternalOutput").ap()
    layer(nc, *args, out)
    r = run_bass_kernel_spmd(nc, [arrays], core_ids=[0])
    return r.results[0]["out"].reshape(1, SEQ, D)
```
